# Optimizing a Trainium2 kernel written in Bass

```python
import jax, jax.numpy as jnp
from jax import lax
import numpy as np

D_MODEL = 2048
BATCH = 1
SEQ = 256
DEPTH = 1

MIX_WIDTH = D_MODEL
ATTN_WIDTH = MIX_WIDTH // 2
LRU_WIDTH = MIX_WIDTH - ATTN_WIDTH
HEAD_DIM = 64
N_Q_HEADS = ATTN_WIDTH // HEAD_DIM
N_KV_HEADS = 4
Q_PER_KV = N_Q_HEADS // N_KV_HEADS
WINDOW = 128
BLOCK = 128
ROPE_THETA = 10000.0
LRU_BLOCK = 64
N_LRU_BLOCKS = LRU_WIDTH // LRU_BLOCK
CONV_WIDTH = 4
CONV_PAD_LEFT = 2
CONV_PAD_RIGHT = CONV_WIDTH - 1 - CONV_PAD_LEFT
LRU_C = 8.0
PEER_HEADS = 8
PEER_QDIM = 256
PEER_HALF = PEER_QDIM // 2
N_KEYS = 128
N_EXPERTS = N_KEYS * N_KEYS
PEER_TOPK = 16
PEER_CHUNK = 128
EPS = 1e-6
NEG = -1e30

Q_COLS = N_Q_HEADS * HEAD_DIM
KV_COLS = N_KV_HEADS * HEAD_DIM
IN_COLS = Q_COLS + 2 * KV_COLS + 2 * LRU_WIDTH


def rms_norm(x, g):
    xf = x.astype(jnp.float32)
    y = xf * lax.rsqrt(jnp.mean(xf * xf, axis=-1, keepdims=True) + EPS)
    return (y * g.astype(jnp.float32)).astype(x.dtype)

def rope(x, pos):
    half = HEAD_DIM // 2
    inv = ROPE_THETA ** (-jnp.arange(half, dtype=jnp.float32) / half)
    ang = pos.astype(jnp.float32)[:, None] * inv[None, :]
    cos = jnp.cos(ang)[None, :, None, :]
    sin = jnp.sin(ang)[None, :, None, :]
    xf = x.astype(jnp.float32)
    x1, x2 = xf[..., :half], xf[..., half:]
    return jnp.concatenate([x1 * cos - x2 * sin, x2 * cos + x1 * sin], axis=-1).astype(x.dtype)

def windowed_gqa_sink(q, k, v, sink):
    B, S = q.shape[0], q.shape[1]
    nb = S // BLOCK
    qb = q.reshape(B, nb, BLOCK, N_KV_HEADS, Q_PER_KV, HEAD_DIM)

    def band(t):
        tp = jnp.pad(t, ((0, 0), (BLOCK, BLOCK), (0, 0), (0, 0)))
        tp = tp.reshape(B, nb + 2, BLOCK, N_KV_HEADS, HEAD_DIM)
        return jnp.concatenate([tp[:, :-2], tp[:, 1:-1], tp[:, 2:]], axis=2)

    kb, vb = band(k), band(v)
    s = jnp.einsum('bnqgrd,bnkgd->bngrqk', qb, kb,
                   preferred_element_type=jnp.float32) * (HEAD_DIM ** -0.5)
    qpos = jnp.arange(nb)[:, None] * BLOCK + jnp.arange(BLOCK)[None, :]
    kpos = (jnp.arange(nb)[:, None] - 1) * BLOCK + jnp.arange(3 * BLOCK)[None, :]
    rel = kpos[:, None, :] - qpos[:, :, None]
    valid = (jnp.abs(rel) <= WINDOW) & (kpos[:, None, :] >= 0) & (kpos[:, None, :] < S)
    s = jnp.where(valid[None, :, None, None], s, NEG)
    sk = sink.astype(jnp.float32).reshape(1, 1, N_KV_HEADS, Q_PER_KV, 1, 1)
    m = jnp.maximum(jnp.max(s, axis=-1, keepdims=True), sk)
    p = jnp.exp(s - m)
    p = p / (jnp.sum(p, axis=-1, keepdims=True) + jnp.exp(sk - m))
    o = jnp.einsum('bngrqk,bnkgd->bnqgrd', p.astype(v.dtype), vb)
    return o.reshape(B, S, Q_COLS)

def centred_depthwise_conv(x, w, b):
    C = x.shape[-1]
    y = lax.conv_general_dilated(x, w.reshape(CONV_WIDTH, 1, C), window_strides=(1,),
                                 padding=[(CONV_PAD_LEFT, CONV_PAD_RIGHT)],
                                 dimension_numbers=('NWC', 'WIO', 'NWC'),
                                 feature_group_count=C)
    return y + b

def rg_lru(x, w_a, b_a, w_x, b_x, lam, reverse):
    B, S, _ = x.shape
    xb = x.reshape(B, S, N_LRU_BLOCKS, LRU_BLOCK)
    r = jax.nn.sigmoid(jnp.einsum('bshi,hij->bshj', xb, w_a).reshape(B, S, LRU_WIDTH) + b_a)
    i = jax.nn.sigmoid(jnp.einsum('bshi,hij->bshj', xb, w_x).reshape(B, S, LRU_WIDTH) + b_x)
    log_a = (-LRU_C * r.astype(jnp.float32)) * jax.nn.softplus(-lam.astype(jnp.float32))
    a = jnp.exp(log_a)
    u = jnp.sqrt(-jnp.expm1(2.0 * log_a)) * (i * x).astype(jnp.float32)

    def combine(left, right):
        a1, b1 = left
        a2, b2 = right
        return a1 * a2, a2 * b1 + b2

    _, h = lax.associative_scan(combine, (a, u), axis=1, reverse=reverse)
    return h.astype(x.dtype)

def peer(x, w_pq, sub_k1, sub_k2, u_emb, v_emb):
    B, S, D = x.shape
    T = B * S
    xt = x.reshape(T, D)
    q = (xt @ w_pq).reshape(T, PEER_HEADS, 2, PEER_HALF)
    s1 = jnp.einsum('thd,hkd->thk', q[:, :, 0], sub_k1, preferred_element_type=jnp.float32)
    s2 = jnp.einsum('thd,hkd->thk', q[:, :, 1], sub_k2, preferred_element_type=jnp.float32)
    v1, i1 = lax.top_k(s1, PEER_TOPK)
    v2, i2 = lax.top_k(s2, PEER_TOPK)
    cand = (v1[..., :, None] + v2[..., None, :]).reshape(T, PEER_HEADS, PEER_TOPK * PEER_TOPK)
    cidx = (i1[..., :, None] * N_KEYS + i2[..., None, :]).reshape(T, PEER_HEADS, PEER_TOPK * PEER_TOPK)
    sc, sel = lax.top_k(cand, PEER_TOPK)
    eidx = jnp.take_along_axis(cidx, sel, axis=-1)
    gates = jax.nn.softmax(sc, axis=-1)
    nc = T // PEER_CHUNK
    E = PEER_HEADS * PEER_TOPK

    def expert_chunk(args):
        xc, ic, gc = args
        uc = u_emb[ic]
        act = jax.nn.gelu(jnp.einsum('cd,ced->ce', xc, uc))
        vc = v_emb[ic]
        return jnp.einsum('ce,ced->cd', (gc * act).astype(vc.dtype), vc)

    out = lax.map(expert_chunk, (xt.reshape(nc, PEER_CHUNK, D),
                                 eidx.reshape(nc, PEER_CHUNK, E),
                                 gates.reshape(nc, PEER_CHUNK, E)))
    return out.reshape(B, S, D).astype(x.dtype)

def first_inputs(seed: int = 0) -> dict:
    key = jax.random.key(seed)
    ks = jax.random.split(key, 32)
    f32 = jnp.float32
    L = DEPTH

    def nrm(k, shape, scale):
        return jax.random.normal(k, shape, f32) * scale

    def gain(k, n):
        return 1.0 + 0.02 * jax.random.normal(k, (L, n), f32)

    def lam_init(k):
        a_c = jax.random.uniform(k, (L, LRU_WIDTH), f32, 0.9, 0.999)
        a = a_c ** (1.0 / LRU_C)
        return jnp.log(a) - jnp.log1p(-a)

    gs = LRU_BLOCK ** -0.5
    return {
        "x": jax.random.normal(ks[0], (BATCH, SEQ, D_MODEL), f32),
        "g_mix": gain(ks[1], D_MODEL),
        "w_in": nrm(ks[2], (L, D_MODEL, IN_COLS), D_MODEL ** -0.5),
        "sink": nrm(ks[3], (L, N_Q_HEADS), 0.5),
        "conv_w": nrm(ks[4], (L, CONV_WIDTH, LRU_WIDTH), CONV_WIDTH ** -0.5),
        "conv_b": nrm(ks[5], (L, LRU_WIDTH), 0.01),
        "fwd_wa": nrm(ks[6], (L, N_LRU_BLOCKS, LRU_BLOCK, LRU_BLOCK), gs),
        "fwd_ba": nrm(ks[7], (L, LRU_WIDTH), 0.01),
        "fwd_wx": nrm(ks[8], (L, N_LRU_BLOCKS, LRU_BLOCK, LRU_BLOCK), gs),
        "fwd_bx": nrm(ks[9], (L, LRU_WIDTH), 0.01),
        "fwd_lam": lam_init(ks[10]),
        "bwd_wa": nrm(ks[11], (L, N_LRU_BLOCKS, LRU_BLOCK, LRU_BLOCK), gs),
        "bwd_ba": nrm(ks[12], (L, LRU_WIDTH), 0.01),
        "bwd_wx": nrm(ks[13], (L, N_LRU_BLOCKS, LRU_BLOCK, LRU_BLOCK), gs),
        "bwd_bx": nrm(ks[14], (L, LRU_WIDTH), 0.01),
        "bwd_lam": lam_init(ks[15]),
        "g_attn_out": gain(ks[16], ATTN_WIDTH),
        "g_lru_out": gain(ks[17], LRU_WIDTH),
        "w_out": nrm(ks[18], (L, MIX_WIDTH, D_MODEL), MIX_WIDTH ** -0.5),
        "g_ffn": gain(ks[19], D_MODEL),
        "w_pq": nrm(ks[20], (L, D_MODEL, PEER_HEADS * PEER_QDIM), D_MODEL ** -0.5),
        "sub_k1": nrm(ks[21], (L, PEER_HEADS, N_KEYS, PEER_HALF), PEER_HALF ** -0.5),
        "sub_k2": nrm(ks[22], (L, PEER_HEADS, N_KEYS, PEER_HALF), PEER_HALF ** -0.5),
        "u_emb": nrm(ks[23], (L, N_EXPERTS, D_MODEL), D_MODEL ** -0.5),
        "v_emb": nrm(ks[24], (L, N_EXPERTS, D_MODEL), (PEER_HEADS * PEER_TOPK) ** -0.5),
        "g_final": 1.0 + 0.02 * jax.random.normal(ks[25], (D_MODEL,), f32),
    }

def first_block(x, g_mix, w_in, sink, conv_w, conv_b,
              fwd_wa, fwd_ba, fwd_wx, fwd_bx, fwd_lam,
              bwd_wa, bwd_ba, bwd_wx, bwd_bx, bwd_lam,
              g_attn_out, g_lru_out, w_out, g_ffn,
              w_pq, sub_k1, sub_k2, u_emb, v_emb, g_final):
    B, S, D = x.shape
    pos = jnp.arange(S)
    splits = [Q_COLS, Q_COLS + KV_COLS, Q_COLS + 2 * KV_COLS, Q_COLS + 2 * KV_COLS + LRU_WIDTH]
    for l in range(DEPTH):
        h = rms_norm(x, g_mix[l])
        proj = h @ w_in[l]
        q, k, v, x_gate, x_rec = jnp.split(proj, splits, axis=-1)
        q = rope(q.reshape(B, S, N_Q_HEADS, HEAD_DIM), pos)
        k = rope(k.reshape(B, S, N_KV_HEADS, HEAD_DIM), pos)
        v = v.reshape(B, S, N_KV_HEADS, HEAD_DIM)
        y_attn = windowed_gqa_sink(q, k, v, sink[l])

        c = centred_depthwise_conv(x_rec, conv_w[l], conv_b[l])
        h_rec = (rg_lru(c, fwd_wa[l], fwd_ba[l], fwd_wx[l], fwd_bx[l], fwd_lam[l], False)
                 + rg_lru(c, bwd_wa[l], bwd_ba[l], bwd_wx[l], bwd_bx[l], bwd_lam[l], True))
        y_lru = jax.nn.gelu(x_gate) * h_rec

        y = jnp.concatenate([rms_norm(y_attn, g_attn_out[l]), rms_norm(y_lru, g_lru_out[l])], axis=-1)
        x = x + y @ w_out[l]
        x = x + peer(rms_norm(x, g_ffn[l]), w_pq[l], sub_k1[l], sub_k2[l], u_emb[l], v_emb[l])
    return rms_norm(x, g_final)


DEPTH_2 = 2

N_A_LAYERS = DEPTH_2 // 2
N_B_LAYERS = DEPTH_2 - N_A_LAYERS

SSD_EXPAND = 2
SSD_D_INNER = SSD_EXPAND * D_MODEL
SSD_HEAD_DIM = 64
SSD_N_HEADS = SSD_D_INNER // SSD_HEAD_DIM
SSD_N_GROUPS = 8
SSD_HEADS_PER_GROUP = SSD_N_HEADS // SSD_N_GROUPS
SSD_D_STATE = 128
SSD_CONV_W = 4
SSD_CHUNK = 256
SSD_BC_DIM = SSD_N_GROUPS * SSD_D_STATE
SSD_CONV_DIM = SSD_D_INNER + 2 * SSD_BC_DIM
SSD_IN_DIM = SSD_D_INNER + SSD_CONV_DIM + SSD_N_HEADS

DIL_PATTERNS = ((128, 1), (512, 4), (2048, 16))
DIL_N_GROUPS = len(DIL_PATTERNS)
DIL_HEADS = 8
DIL_HEAD_DIM = 128
DIL_Q_WIDTH = DIL_N_GROUPS * DIL_HEADS * DIL_HEAD_DIM
DIL_OUT_WIDTH = DIL_HEADS * DIL_HEAD_DIM
DIL_IN_DIM = DIL_Q_WIDTH + DIL_OUT_WIDTH
DIL_KV_DIM = 2 * DIL_Q_WIDTH
DIL_BLOCK = 128

DEEPNORM_ALPHA = (2 * DEPTH_2) ** 0.25
DEEPNORM_BETA = (8 * DEPTH_2) ** -0.25
LN_EPS = 1e-5
RMS_EPS = 1e-5


def _layer_norm(x, g, b):
    xf = x.astype(jnp.float32)
    mu = jnp.mean(xf, -1, keepdims=True)
    var = jnp.mean(jnp.square(xf - mu), -1, keepdims=True)
    return ((xf - mu) * lax.rsqrt(var + LN_EPS)).astype(x.dtype) * g + b

def _adaln(c, w, b):
    mod = jax.nn.silu(c) @ w + b
    shift, scale, gate = jnp.split(mod, 3, axis=-1)
    return shift[:, None, :], scale[:, None, :], gate[:, None, :]

def _causal_depthwise_conv(x, w, b):
    y = lax.conv_general_dilated(
        x, w[:, None, :], window_strides=(1,), padding=[(SSD_CONV_W - 1, 0)],
        dimension_numbers=("NWC", "WIO", "NWC"), feature_group_count=x.shape[-1])
    return y + b

def _ssd_chunked(xdt, dtA, Bm, Cm):
    f32 = jnp.float32
    bsz, L = xdt.shape[:2]
    G, K, P, N = SSD_N_GROUPS, SSD_HEADS_PER_GROUP, SSD_HEAD_DIM, SSD_D_STATE
    Lp = -(-L // SSD_CHUNK) * SSD_CHUNK
    nc = Lp // SSD_CHUNK

    def chunks(a):
        a = jnp.pad(a, [(0, 0), (0, Lp - L)] + [(0, 0)] * (a.ndim - 2))
        a = a.reshape((bsz, nc, SSD_CHUNK) + a.shape[2:])
        return jnp.moveaxis(a, 1, 0)

    xs = chunks(xdt.reshape(bsz, L, G, K, P).astype(f32))
    As = chunks(dtA.reshape(bsz, L, G, K).astype(f32))
    Bs = chunks(Bm.astype(f32))
    Cs = chunks(Cm.astype(f32))
    causal = jnp.tril(jnp.ones((SSD_CHUNK, SSD_CHUNK), bool))[None, :, :, None, None]

    def step(state, inp):
        xc, ac, bc, cc = inp
        acum = jnp.cumsum(ac, axis=1)
        seg = acum[:, :, None] - acum[:, None, :]
        decay = jnp.exp(jnp.where(causal, seg, -jnp.inf))
        cb = jnp.einsum("blgn,bsgn->blsg", cc, bc)
        y_diag = jnp.einsum("blsgk,bsgkp->blgkp", cb[..., None] * decay, xc)
        y_off = jnp.einsum("blgn,bgkpn->blgkp", cc, state) * jnp.exp(acum)[..., None]
        tail = jnp.exp(acum[:, -1:] - acum)
        new_state = (state * jnp.exp(acum[:, -1])[..., None, None]
                     + jnp.einsum("bsgn,bsgkp->bgkpn", bc, xc * tail[..., None]))
        return new_state, y_diag + y_off

    state0 = jnp.zeros((bsz, G, K, P, N), f32)
    _, ys = lax.scan(step, state0, (xs, As, Bs, Cs))
    ys = jnp.moveaxis(ys, 0, 1).reshape(bsz, Lp, SSD_N_HEADS * P)
    return ys[:, :L]

def _ssd_mixer(h, in_w, conv_w, conv_b, dt_bias, A_log, D_skip, norm_g, out_w):
    bsz, L, _ = h.shape
    proj = h @ in_w
    z, xBC, dt = jnp.split(proj, [SSD_D_INNER, SSD_D_INNER + SSD_CONV_DIM], axis=-1)
    xBC = jax.nn.silu(_causal_depthwise_conv(xBC, conv_w, conv_b))
    xs, Bm, Cm = jnp.split(xBC, [SSD_D_INNER, SSD_D_INNER + SSD_BC_DIM], axis=-1)
    xs = xs.reshape(bsz, L, SSD_N_HEADS, SSD_HEAD_DIM)
    Bm = Bm.reshape(bsz, L, SSD_N_GROUPS, SSD_D_STATE)
    Cm = Cm.reshape(bsz, L, SSD_N_GROUPS, SSD_D_STATE)
    dt = jax.nn.softplus((dt + dt_bias).astype(jnp.float32))
    A = -jnp.exp(A_log.astype(jnp.float32))
    y = _ssd_chunked(xs * dt[..., None], dt * A, Bm, Cm)
    y = y + (xs * D_skip[:, None]).reshape(bsz, L, SSD_D_INNER)
    y = y * jax.nn.silu(z.astype(jnp.float32))
    yg = y.reshape(bsz, L, SSD_N_GROUPS, -1)
    yg = yg * lax.rsqrt(jnp.mean(jnp.square(yg), -1, keepdims=True) + RMS_EPS)
    y = yg.reshape(bsz, L, SSD_D_INNER).astype(h.dtype) * norm_g
    return y @ out_w

def _alibi_slopes():
    n = DIL_N_GROUPS * DIL_HEADS
    s = 2.0 ** (-8.0 * np.arange(1, n + 1) / n)
    return jnp.asarray(s.reshape(DIL_N_GROUPS, DIL_HEADS), dtype=jnp.float32)

def _dilated_window_attention(q, k, v, window, dilation, slopes):
    f32 = jnp.float32
    bsz, L, H, E = q.shape
    span = window // dilation
    M = -(-L // (dilation * DIL_BLOCK)) * DIL_BLOCK
    nb = M // DIL_BLOCK
    pad = M * dilation - L

    def to_blocks(a):
        a = jnp.pad(a, [(0, 0), (0, pad), (0, 0), (0, 0)])
        a = a.reshape(bsz, M, dilation, H, E).transpose(0, 2, 1, 3, 4)
        return a.reshape(bsz, dilation, nb, DIL_BLOCK, H, E)

    def with_prev(a):
        prev = jnp.pad(a[:, :, :-1], [(0, 0), (0, 0), (1, 0), (0, 0), (0, 0), (0, 0)])
        return jnp.concatenate([prev, a], axis=3)

    qb = to_blocks(q)
    kb = with_prev(to_blocks(k))
    vb = with_prev(to_blocks(v))
    s = jnp.einsum("brnqhe,brnkhe->brnhqk", qb, kb,
                   preferred_element_type=f32) * (E ** -0.5)
    qi = jnp.arange(DIL_BLOCK)[:, None]
    kj = jnp.arange(2 * DIL_BLOCK)[None, :]
    delta = qi + DIL_BLOCK - kj
    valid = (delta >= 0) & (delta <= span)
    first = (jnp.arange(nb) == 0)[:, None, None]
    valid = valid[None] & ~(first & (kj < DIL_BLOCK)[None])
    alibi = -slopes[:, None, None] * (delta * dilation).astype(f32)[None]
    s = jnp.where(valid[None, None, :, None], s + alibi[None, None, None], -jnp.inf)
    m = jnp.max(s, -1, keepdims=True)
    p = jnp.exp(s - m)
    den = jnp.sum(p, -1)
    o = jnp.einsum("brnhqk,brnkhe->brnqhe", p, vb.astype(f32))
    o = o / jnp.moveaxis(den, 3, 4)[..., None]
    lse = jnp.moveaxis(m[..., 0] + jnp.log(den), 3, 4)

    def from_blocks(a):
        a = a.reshape((bsz, dilation, M) + a.shape[4:])
        a = jnp.moveaxis(a, 1, 2).reshape((bsz, M * dilation) + a.shape[3:])
        return a[:, :L]

    return from_blocks(o), from_blocks(lse)

def _shared_kv(x, kv_w):
    bsz, L, _ = x.shape
    k, v = jnp.split(x @ kv_w, 2, axis=-1)
    shp = (bsz, L, DIL_N_GROUPS, DIL_HEADS, DIL_HEAD_DIM)
    return k.reshape(shp), v.reshape(shp)

def _dilated_mixer(h, k_sh, v_sh, in_w, out_w):
    bsz, L, _ = h.shape
    q, z = jnp.split(h @ in_w, [DIL_Q_WIDTH], axis=-1)
    q = q.reshape(bsz, L, DIL_N_GROUPS, DIL_HEADS, DIL_HEAD_DIM)
    slopes = _alibi_slopes()
    outs, lses = [], []
    for g, (window, dilation) in enumerate(DIL_PATTERNS):
        o, lse = _dilated_window_attention(q[:, :, g], k_sh[:, :, g], v_sh[:, :, g],
                                           window, dilation, slopes[g])
        outs.append(o)
        lses.append(lse)
    o = jnp.stack(outs, 2)
    wts = jax.nn.softmax(jnp.stack(lses, 2), axis=2)
    o = jnp.einsum("blghe,blgh->blhe", o, wts).reshape(bsz, L, DIL_OUT_WIDTH)
    o = o.astype(h.dtype) * jax.nn.silu(z)
    return o @ out_w

def second_inputs(seed: int = 0) -> dict:
    key = jax.random.key(seed)
    ks = jax.random.split(key, 20)
    f32 = jnp.float32
    nA, nB, D = N_A_LAYERS, N_B_LAYERS, D_MODEL
    nrm = lambda k, shp, sc: jax.random.normal(k, shp, f32) * sc
    dt0 = jnp.exp(jax.random.uniform(ks[8], (nA, SSD_N_HEADS), f32,
                                     np.log(1e-3), np.log(1e-1)))
    return {
        "x": nrm(ks[0], (BATCH, SEQ, D), 1.0),
        "c": nrm(ks[1], (BATCH, D), 1.0),
        "ada_w": nrm(ks[2], (DEPTH_2, D, 3 * D), 0.1 * D ** -0.5),
        "ada_b": nrm(ks[3], (DEPTH_2, 3 * D), 0.01),
        "ln_g": 1.0 + nrm(ks[4], (DEPTH_2, D), 0.01),
        "ln_b": nrm(ks[5], (DEPTH_2, D), 0.01),
        "a_in_w": nrm(ks[6], (nA, D, SSD_IN_DIM), D ** -0.5),
        "a_conv_w": nrm(ks[7], (nA, SSD_CONV_W, SSD_CONV_DIM), SSD_CONV_W ** -0.5),
        "a_conv_b": nrm(ks[9], (nA, SSD_CONV_DIM), 0.01),
        "a_dt_bias": dt0 + jnp.log(-jnp.expm1(-dt0)),
        "a_A_log": jnp.log(jax.random.uniform(ks[10], (nA, SSD_N_HEADS), f32, 1.0, 16.0)),
        "a_D": 1.0 + nrm(ks[11], (nA, SSD_N_HEADS), 0.01),
        "a_norm_g": 1.0 + nrm(ks[12], (nA, SSD_D_INNER), 0.01),
        "a_out_w": nrm(ks[13], (nA, SSD_D_INNER, D), DEEPNORM_BETA * SSD_D_INNER ** -0.5),
        "kv_w": nrm(ks[14], (D, DIL_KV_DIM), D ** -0.5),
        "b_in_w": nrm(ks[15], (nB, D, DIL_IN_DIM), D ** -0.5),
        "b_out_w": nrm(ks[16], (nB, DIL_OUT_WIDTH, D), DEEPNORM_BETA * DIL_OUT_WIDTH ** -0.5),
    }

def second_block(x, c, ada_w, ada_b, ln_g, ln_b, a_in_w, a_conv_w, a_conv_b, a_dt_bias,
              a_A_log, a_D, a_norm_g, a_out_w, kv_w, b_in_w, b_out_w):
    k_sh, v_sh = None, None
    for layer in range(DEPTH_2):
        shift, scale, gate = _adaln(c, ada_w[layer], ada_b[layer])
        h = x * (1.0 + scale) + shift
        if layer < N_A_LAYERS:
            i = layer
            y = _ssd_mixer(h, a_in_w[i], a_conv_w[i], a_conv_b[i], a_dt_bias[i],
                           a_A_log[i], a_D[i], a_norm_g[i], a_out_w[i])
        else:
            i = layer - N_A_LAYERS
            y = _dilated_mixer(h, k_sh, v_sh, b_in_w[i], b_out_w[i])
        x = _layer_norm(DEEPNORM_ALPHA * x + (1.0 + gate) * y, ln_g[layer], ln_b[layer])
        if layer == N_A_LAYERS - 1:
            k_sh, v_sh = _shared_kv(x, kv_w)
    return x


def setup_inputs(seed=0):
    out = dict(first_inputs(seed))
    for name, value in second_inputs(seed + 1).items():
        if name != "x":
            out[name + "_2"] = value
    return out


def reference(
    x, g_mix, w_in, sink, conv_w, conv_b, fwd_wa, fwd_ba, fwd_wx, fwd_bx, fwd_lam, bwd_wa,
    bwd_ba, bwd_wx, bwd_bx, bwd_lam, g_attn_out, g_lru_out, w_out, g_ffn, w_pq, sub_k1, sub_k2,
    u_emb, v_emb, g_final, c_2, ada_w_2, ada_b_2, ln_g_2, ln_b_2, a_in_w_2, a_conv_w_2,
    a_conv_b_2, a_dt_bias_2, a_A_log_2, a_D_2, a_norm_g_2, a_out_w_2, kv_w_2, b_in_w_2,
    b_out_w_2,
):
    x = first_block(
        x, g_mix, w_in, sink, conv_w, conv_b, fwd_wa, fwd_ba, fwd_wx, fwd_bx, fwd_lam, bwd_wa,
        bwd_ba, bwd_wx, bwd_bx, bwd_lam, g_attn_out, g_lru_out, w_out, g_ffn, w_pq, sub_k1,
        sub_k2, u_emb, v_emb, g_final,
    )
    return second_block(
        x, c_2, ada_w_2, ada_b_2, ln_g_2, ln_b_2, a_in_w_2, a_conv_w_2, a_conv_b_2, a_dt_bias_2,
        a_A_log_2, a_D_2, a_norm_g_2, a_out_w_2, kv_w_2, b_in_w_2, b_out_w_2,
    )


_drawn_inputs = setup_inputs


def setup_inputs(seed=0):
    import zlib

    import numpy as np

    out = dict(_drawn_inputs(seed))
    spreads = {}
    factors = {'sink': 8.0,
     'fwd_ba': 8.0,
     'fwd_bx': 8.0,
     'bwd_ba': 8.0,
     'bwd_bx': 8.0,
     'g_attn_out': 4.927,
     'g_lru_out': 5.356,
     'g_ffn': 8.0,
     'ada_b_2': 6.647,
     'ln_g_2': 3.938,
     'ln_b_2': 4.016,
     'a_conv_b_2': 8.0,
     'a_D_2': 8.0,
     'a_norm_g_2': 8.0}
    for name, (base, spread) in spreads.items():
        noise = np.random.default_rng([zlib.crc32(name.encode()), seed]).standard_normal(out[name].shape)
        drawn = base * np.exp(spread * noise) if base else spread * noise
        out[name] = __import__('jax').numpy.asarray(drawn.astype(out[name].dtype))
    for name, factor in factors.items():
        out[name] = (out[name] * factor).astype(out[name].dtype)
    return out
```

```python
from contextlib import ExitStack

import numpy as np

import concourse.bass as bass
from concourse import mybir

ALU = mybir.AluOpType
ACT = mybir.ActivationFunctionType
AX = mybir.AxisListType
F32 = mybir.dt.float32
F32R = mybir.dt.float32r
BF16 = mybir.dt.bfloat16
U32 = mybir.dt.uint32
ds = bass.ds

P = 128
S = 256
TT = S // P
D = 2048
KC = D // P
TILE = 1024
EPS = 1e-6
LN_EPS = 1e-5
ALPHA = 4.0 ** 0.25

NQ, HD, NKV = 16, 64, 4
QC = NQ * HD
KVC = 2 * NKV * HD
LRU = 1024
LC = LRU // P
PH = 8
NK = 128
TOPK = 16
HALVES = 2
EB = NK // HALVES
DI = 4096
SG, SN, SHEADS = 8, 128, 64
XC = DI // P
BC = XC + 2 * SG
DG, DH = 3, 8

NEG = -1e30


class Columns:

    def __init__(self):
        self.at, self.n = {}, 0

    def add(self, name, width):
        self.at[name] = self.n
        self.n += width

    def __getitem__(self, name):
        return self.at[name]


PC = Columns()
for _name, _w in [
    ("g_mix", KC), ("g_ffn", KC), ("g_attn", LC), ("g_lru", LC),
    ("conv_w", 4 * LC), ("conv_b", LC), ("gate_b", 4 * LC), ("lam", 2 * LC),
    ("ada_b", 96), ("cond", KC), ("a_conv_w", 4 * BC), ("a_conv_b", BC),
    ("norm_g", XC), ("skip", XC), ("dt_bias", 1), ("a_log", 1),
    ("eps", 1), ("ln_eps", 1), ("tiny", 1),
]:
    PC.add(_name, _w)
CC = Columns()
for _name, _w in [("ident", P), ("ones", P), ("iota", P), ("iota16", TOPK)]:
    CC.add(_name, _w)
CW = Columns()
for _name, _w in [("cos", TT * 32), ("sin", TT * 32), ("window", TT * S)]:
    CW.add(_name, _w)
CD = Columns()
for _name, _w in [("d0", DG * P), ("d1", DG * S), ("slopes", DG * DH)]:
    CD.add(_name, _w)

STREAM = [
    ("q", 4), ("kv", 2), ("gate", 4), ("rec", 4), ("w_out", 8), ("w_pq", 8),
    ("u0", 32), ("v0", 32), ("u1", 32), ("v1", 32),
    ("xbc", 24), ("z", 16), ("a_out", 16), ("k2", 12), ("v2", 12), ("q2", 12), ("z2", 4), ("b_out", 4),
]
FIRST_BODY = {}
BODIES = 0
for _name, _n in STREAM:
    FIRST_BODY[_name] = BODIES
    BODIES += _n
NB = dict(STREAM)


class Chain:

    def __init__(self, eng, sem):
        self.eng, self.sem, self.n = eng, sem, 0
        self.offset = None

    def __call__(self, instruction):
        self.post(instruction)
        self.wait()

    def post(self, instruction):
        instruction.then_inc(self.sem, 1)
        self.n += 1

    def wait(self, back=0):
        n = self.n - back
        self.eng.wait_ge(self.sem, n if self.offset is None else self.offset + n)

    def loop(self, j, per):
        self.start, self.per = self.n, per
        self.offset = j * per

    def end(self, trips):
        assert self.n - self.start == self.per, (self.n - self.start, self.per)
        self.n = self.start + self.per * trips
        self.offset = None


def build(nc, a, out):
    ctx = ExitStack()
    with ctx:
        def psum(name, shape, dt=F32):
            return ctx.enter_context(nc.psum_tensor(name, shape, dt))

        def sb(name, shape, dt=F32, group=None):
            return (group or ctx).enter_context(nc.sbuf_tensor(name, shape, dt))

        names = {}

        def sem(name):
            if name not in names:
                names[name] = ctx.enter_context(nc.semaphore(name))
            return names[name]

        PS = psum("PS", [P, 8, 512])

        X = sb("X", [P, TT, D])
        xt_hi = sb("xt_hi", [P, KC, S], F32R)
        xt_lo = sb("xt_lo", [P, KC, S], F32R)
        raw = sb("raw", [P, 4, TILE])
        w_hi = sb("w_hi", [P, 4, TILE], F32R)
        w_lo = sb("w_lo", [P, 4, TILE], F32R)
        st_hi = sb("st_hi", [P, 2, S], F32R)
        st_lo = sb("st_lo", [P, 2, S], F32R)
        cc = sb("cc", [P, CC.n])
        pc = sb("pc", [P, PC.n])
        diag = sb("diag", [P, TT, P])
        xtmp = sb("xtmp", [P, 2, S])
        stat = sb("stat", [P, 16])
        mod = sb("mod", [P, 96])
        ident = cc[:, CC["ident"]:CC["ident"] + P]
        ones = cc[:, CC["ones"]:CC["ones"] + P]

        mixer = ExitStack()
        yT = sb("yT", [P, KC, S], F32, mixer)
        gateT = sb("gateT", [P, LC, S], F32, mixer)
        convT = sb("convT", [P, LC, S], F32, mixer)
        attn = ExitStack()
        cw = sb("cw", [P, CW.n], F32, attn)
        qn = sb("qn", [P, TT, QC], F32, attn)
        kvn = sb("kvn", [P, TT, KVC], F32, attn)
        kdup = sb("kdup", [P, TT, NKV, 2, HD], F32, attn)
        qT = sb("qT", [P, QC // P, S], F32, attn)
        kT = sb("kT", [P, NKV, S], F32, attn)
        sc = sb("sc", [P, 2, 4, S], F32, attn)
        pr = sb("pr", [P, 4, S], F32, attn)
        pT = sb("pT", [P, 8, P], F32, attn)
        yn = sb("yn", [P, TT, QC], F32, attn)
        rtmp = sc
        sinkb = sb("sinkb", [P, NQ], F32, attn)
        sm = sb("sm", [P, 8, 2, 4], F32, attn)
        attn.close()
        lru = ExitStack()
        wbd = sb("wbd", [P, 4, LC, P], F32, lru)
        rr = sb("rr", [P, LC, S], F32, lru)
        ii = sb("ii", [P, LC, S], F32, lru)
        aa = sb("aa", [P, LC, S], F32, lru)
        hh = sb("hh", [P, 2, LC, S], F32, lru)
        spl = sb("spl", [P, 8, 2 * LC], F32, lru)
        rstdb = sb("rstdb", [P, 2, S], F32, lru)
        lru.close()
        mixer.close()

        peer = ExitStack()
        slotsT = sb("slotsT", [P, 3, S], F32, peer)
        silu_c = sb("silu_c", [P, KC], F32, peer)
        route = ExitStack()
        skT = sb("skT", [P, 2 * PH, NK], F32, route)
        pqT = sb("pqT", [P, 2 * PH, S], F32, route)
        score = sb("score", [P, TT * 2 * PH, NK], F32, route)
        topv = sb("topv", [P, TT * 2 * PH, TOPK], F32, route)
        topi = sb("topi", [P, TT * 2 * PH, TOPK], U32, route)
        topf = sb("topf", [P, TT * 2 * PH, TOPK], F32, route)
        cand = sb("cand", [P, TT * PH, TOPK, TOPK], F32, route)
        pick = sb("pick", [P, TT * PH, TOPK], F32, route)
        seli = sb("seli", [P, TT * PH, TOPK], U32, route)
        selh = sb("selh", [P, 2, TT * PH, TOPK], U32, route)
        self_ = sb("self_", [P, 2, TT * PH, TOPK], F32, route)
        slots = sb("slots", [P, 3, TT * PH, TOPK], F32, route)
        rsum = sb("rsum", [P, TT * PH], F32, route)
        route.close()
        experts = ExitStack()
        hid = sb("hid", [P, EB, S], F32, experts)
        hot1 = sb("hot1", [P, 2, 4, NK], F32, experts)
        hot2 = sb("hot2", [P, 2, 4, EB], F32, experts)
        ada = sb("ada", [P, 3, TILE], F32, experts)
        ada_acc = sb("ada_acc", [P, 3, TILE], F32, experts)
        experts.close()
        final = ExitStack()
        row = sb("row", [P, D], F32, final)
        final.close()
        peer.close()

        ssd = ExitStack()
        xbc = sb("xbc", [P, BC, S], F32, ssd)
        cbuf = sb("cbuf", [P, 2, S], F32, ssd)
        w_dt = sb("w_dt", [P, KC, SHEADS], F32, ssd)
        causal = sb("causal", [P, P], F32, ssd)
        causal_b = sb("causal_b", [P, P], BF16, ssd)
        ident_b = sb("ident_b", [P, P], BF16, ssd)
        dts = sb("dts", [SHEADS, 8, S], F32, ssd)
        dtn = sb("dtn", [P, TT, SHEADS], F32, ssd)
        nacn = sb("nacn", [P, TT, SHEADS], F32, ssd)
        xs_st = sb("xs_st", [P, 4, S], F32, ssd)
        b_st = sb("b_st", [P, S], F32, ssd)
        pick_h = sb("pick_h", [SHEADS, 8, P], F32, ssd)
        xd = sb("xd", [P, TT, 512], F32, ssd)
        cbm = sb("cbm", [P, 384], F32, ssd)
        ex = sb("ex", [P, 2, 384], F32, ssd)
        mm_ = sb("mm_", [P, 2, 384], F32, ssd)
        zt = sb("zt", [P, 2, S], F32, ssd)
        sq = sb("sq", [P, 4, S], F32, ssd)
        rg = sb("rg", [P, 2, S], F32, ssd)
        ssd.close()
        norms = ExitStack()
        Y = sb("Y", [P, TT, D], F32, norms)
        rows = sb("rows", [P, 3, D], F32, norms)
        dcol = sb("dcol", [P, 2, P], F32, norms)
        norms.close()
        dil = ExitStack()
        k2T = sb("k2T", [P, DG * DH, S], F32, dil)
        v2n = sb("v2n", [P, TT, DG * DH * P], F32, dil)
        q2T = sb("q2T", [P, DG * DH, S], F32, dil)
        zn = sb("zn", [P, TT, DH * P], F32, dil)
        cd = sb("cd", [P, CD.n], F32, dil)
        q_st = sb("q_st", [P, DG, S], F32, dil)
        sc2 = sb("sc2", [P, 9 * P], F32, dil)
        pT2 = sb("pT2", [P, 9, P], F32, dil)
        sm2 = sb("sm2", [P, 8], F32, dil)
        dil.close()
        oT = k2T

        raw_loaded = [sem(f"raw_loaded{u}") for u in range(4)]
        hi_done, lo_done, tile_used = sem("hi_done"), sem("lo_done"), sem("tile_used")
        stage_hi_done, stage_lo_done = sem("stage_hi_done"), sem("stage_lo_done")
        consts_loaded, x_loaded, params_loaded = sem("consts_loaded"), sem("x_loaded"), sem("params_loaded")
        xt_turned, xt_hi_done, xt_lo_done = sem("xt_turned"), sem("xt_hi_done"), sem("xt_lo_done")
        act_free, dve_free = sem("act_free"), sem("dve_free")
        ACT_BLOCKS = {"gate": 0, "w_pq": 8, "u0": 24, "u1": 88, "z": 152, "k2": 184, "q2": 208}
        DVE_BLOCKS = {"rec": 0, "xbc": 8}
        CHUNKS = {"w_out": 0, "v0": 16, "v1": 80, "a_out": 144, "b_out": 176}
        dve_link, act_link = sem("dve_link"), sem("act_link")

        block = ctx.enter_context(nc.Block())

        def one(tensor, i):
            return tensor[:, ds(i, 1), :].rearrange("p a s -> p (a s)")

        def tile_source(name, j, u):
            if name in ("w_out", "a_out", "b_out"):
                return a[name][2 * j + u // 2][:, (u % 2) * TILE:(u % 2 + 1) * TILE]
            if name in ("u0", "u1", "v0", "v1"):
                return a[name[0] + "_emb"][4 * j + (128 * int(name[1]) + u)]
            return a[name][4 * j + u]

        @block.sync
        def _(sp):
            sp.dma_start(X[:, :, :], a["x"]).then_inc(x_loaded, 16)
            sp.dma_start(cc[:, :], a["cc"]).then_inc(consts_loaded, 16)
            sp.dma_start(pc[:, :], a["pc"]).then_inc(params_loaded, 16)

            def weight(name, j, u):
                first = name == STREAM[0][0] and type(j) is int
                if not first:
                    sp.wait_ge(lo_done, 4 * (j + FIRST_BODY[name]) + u - 3)
                sp.dma_start(raw[:, u, :], tile_source(name, j, u)).then_inc(raw_loaded[u], 16)

            for name, n in STREAM:
                start = 0
                if name == STREAM[0][0]:
                    for u in range(4):
                        weight(name, 0, u)
                    start = 1
                with sp.Fori(start, n) as j:
                    for u in range(4):
                        weight(name, j, u)
            sp.wait_ge(sem("out_ready"), 1)
            sp.dma_start(out, X[:, :, :]).then_inc(sem("stored"), 16)
            sp.wait_ge(sem("stored"), 16)

        @block.gpsimd
        def _(pool):
            pool.dma_start(cw[:, :], a["cw"]).then_inc(sem("window_loaded"), 16)
            pool.dma_start(sinkb[:, :], a["sink"].partition_broadcast(P)).then_inc(sem("window_loaded"), 16)
            pool.wait_ge(sem("y_attn_done"), 1)
            pool.memset(wbd[:, :, :, :], 0.0).then_inc(sem("bd_zero"), 1)
            pool.wait_ge(sem("bd_zero"), 1)
            for kind in range(4):
                for half in range(2):
                    pool.dma_start(wbd[64 * half:64 * half + 64, kind, :, 64 * half:64 * half + 64],
                                   a["gate_w"][kind, half]).then_inc(sem("bd_loaded"), 16)
            pool.wait_ge(sem("x1_done"), 1)
            pool.dma_start(skT[:, :, :], a["skT"]).then_inc(sem("keys_loaded"), 16)
            pool.wait_ge(sem("route_over"), 1)
            with pool.Fori(0, 64) as k:
                for q in range(3):
                    pool.wait_ge(sem("ada_used"), 3 * k + q + 1)
                    pool.dma_start(ada[:, q, :], a["ada_w"][3 * k + q]).then_inc(sem(f"ada_loaded{q}"), 16)
            pool.wait_ge(sem("x2_done"), HALVES)
            pool.dma_start(row[:, :], a["rows"][0].partition_broadcast(P)).then_inc(sem("row_loaded"), 16)
            pool.wait_ge(sem("x3_done"), 1)
            pool.dma_start(w_dt[:, :, :], a["w_dt"]).then_inc(sem("w_dt_loaded"), 16)
            pool.dma_start(causal[:, :], a["causal"]).then_inc(sem("w_dt_loaded"), 16)
            pool.wait_ge(sem("ssd_ready"), 1)
            with pool.Fori(0, SG) as g:
                pool.wait_ge(sem("group_done"), g + 1)
                pool.tensor_copy(xs_st[:, :, :], xbc[:, ds(4 * g, 4), :]).then_inc(sem("group_staged"), 1)
                pool.tensor_copy(b_st[:, :], one(xbc, g + XC)).then_inc(sem("group_staged"), 1)
                pool.tensor_copy(pick_h[:, :, :], cc[0:SHEADS, ds(8 * g + CC["ident"], 8)].unsqueeze(2)
                                 .to_broadcast([SHEADS, 8, P])).then_inc(sem("group_staged"), 1)
            pool.wait_ge(sem("y_copied"), 1)
            for r in range(2):
                pool.dma_start(rows[:, 1 + r, :], a["rows"][1 + r].partition_broadcast(P))\
                    .then_inc(sem("ln_rows_loaded"), 16)
            pool.wait_ge(sem("x4_done"), 1)
            pool.dma_start(cd[:, :], a["cd"]).then_inc(sem("distances_loaded"), 16)
            pool.wait_ge(act_free, 2 + ACT_BLOCKS["q2"] + 24)
            with pool.Fori(0, DH) as h:
                pool.wait_ge(sem("head_scored"), h + 1)
                pool.tensor_copy(q_st[:, :, :],
                                 q2T[:, :, :].rearrange("p (g h) s -> p g h s", g=DG)[:, :, ds(h, 1), :]
                                 .rearrange("p g o s -> p g (o s)")).then_inc(sem("q_staged"), 1)
            pool.wait_ge(sem("y_copied"), 2)
            for r in range(2):
                pool.dma_start(rows[:, 1 + r, :], a["rows"][3 + r].partition_broadcast(P))\
                    .then_inc(sem("ln_rows_loaded"), 16)

        @block.tensor
        def _(pe):
            def three(o, w_h, w_l, x_h, x_l, start, stop):
                pe.matmul(o, w_h, x_h, start=start, stop=False, skip_group_check=True)
                pe.matmul(o, w_h, x_l, start=False, stop=False, skip_group_check=True)
                return pe.matmul(o, w_l, x_h, start=False, stop=stop, skip_group_check=True)

            def channel_blocks(name, free, before):
                with pe.Fori(0, NB[name]) as j:
                    for b in range(2):
                        pe.wait_ge(free, 2 * j + before + b + 1)
                        for h in range(2):
                            u = 2 * b + h
                            pe.wait_ge(lo_done, 4 * (j + FIRST_BODY[name]) + u + 1)
                            for k in range(8):
                                w = slice(k * P, k * P + P)
                                last = three(PS[:, b, 0:S], w_hi[:, u, w], w_lo[:, u, w],
                                             xt_hi[:, 8 * h + k, :], xt_lo[:, 8 * h + k, :],
                                             h == 0 and k == 0, h == 1 and k == 7)
                            last.then_inc(tile_used, 1)

            def token_columns(tiles, body0, bank0, kpt):
                n = 16 // kpt
                for i in range(n):
                    pe.wait_ge(lo_done, tiles + (body0 * 4 + i + 1))
                    for kk in range(kpt):
                        k = i * kpt + kk
                        for tt in range(TT):
                            for g in range(2 // kpt):
                                c = (kk if kpt == 2 else g) * 512
                                o = PS[:, bank0 + tt * (2 // kpt) + g, :]
                                t = slice(tt * P, tt * P + P)
                                u = i % 4
                                pe.matmul(o, xt_hi[:, k, t], w_hi[:, u, c:c + 512], start=k == 0, stop=False)
                                pe.matmul(o, xt_lo[:, k, t], w_hi[:, u, c:c + 512], start=False, stop=False)
                                last = pe.matmul(o, xt_hi[:, k, t], w_lo[:, u, c:c + 512],
                                                 start=False, stop=k == KC - 1)
                    last.then_inc(tile_used, 1)

            def rows_body(name, j, first, stop):
                for u in range(4):
                    pe.wait_ge(lo_done, 4 * (j + FIRST_BODY[name]) + u + 1)
                    s = u // 2
                    if u % 2 == 0:
                        pe.wait_ge(stage_lo_done, 2 * j + CHUNKS[name] + s + 1)
                    for tt in range(TT):
                        for g in range(2):
                            o = PS[:, tt * 4 + (u % 2) * 2 + g, :]
                            t, c = slice(tt * P, tt * P + P), slice(g * 512, g * 512 + 512)
                            pe.matmul(o, st_hi[:, s, t], w_hi[:, u, c], start=first and s == 0, stop=False,
                                      skip_group_check=True)
                            pe.matmul(o, st_lo[:, s, t], w_hi[:, u, c], start=False, stop=False,
                                      skip_group_check=True)
                            last = pe.matmul(o, st_hi[:, s, t], w_lo[:, u, c], start=False, stop=stop and s == 1,
                                             skip_group_check=True)
                    last.then_inc(tile_used, 1)

            def all_rows(name):
                rows_body(name, 0, True, False)
                if NB[name] > 2:
                    with pe.Fori(1, NB[name] - 1) as j:
                        rows_body(name, j, False, False)
                rows_body(name, NB[name] - 1, False, True)

            def turn(n, by):
                for c in range(KC):
                    if c >= 8:
                        pe.wait_ge(xt_lo_done, KC * n + c - 7)
                    for tt in range(TT):
                        last = pe.matmul(PS[:, c % 8, tt * P:tt * P + P], X[:, tt, c * P:c * P + P], by(tt),
                                         start=True, stop=True)
                    last.then_inc(xt_turned, 1)

            pe.wait_ge(consts_loaded, 16)
            pe.wait_ge(x_loaded, 16)
            pe.wait_ge(sem("diag_done"), 1)
            turn(0, lambda tt: diag[:, tt, :])
            pe.wait_ge(xt_lo_done, KC)
            token_columns(0, FIRST_BODY["q"], 0, 1)
            token_columns(0, FIRST_BODY["kv"], 4, 2)
            pe.wait_ge(sem("qkv_out"), 2)
            channel_blocks("gate", act_free, ACT_BLOCKS["gate"])
            pe.wait_ge(act_free, 2 + ACT_BLOCKS["gate"] + 8)
            channel_blocks("rec", dve_free, DVE_BLOCKS["rec"])

            pe.wait_ge(dve_free, 2 + DVE_BLOCKS["rec"] + 8)
            pe.wait_ge(sem("rope_done"), 1)
            for tt in range(TT):
                for c in range(QC // P):
                    pe.transpose(PS[:, c // 2, (c % 2) * S + tt * P:(c % 2) * S + tt * P + P],
                                 qn[:, tt, c * P:c * P + P], ident)
                for g in range(NKV):
                    last = pe.transpose(PS[:, 4 + g // 2, (g % 2) * S + tt * P:(g % 2) * S + tt * P + P],
                                        kdup[:, tt, g, :, :].rearrange("p a d -> p (a d)"), ident)
            last.then_inc(sem("qk_turned"), 1)

            steps = [(tt, g) for tt in range(TT) for g in range(NKV)]

            def scores(n):
                tt, g = steps[n]
                if n >= 2:
                    pe.wait_ge(sem("scores_read"), n - 1)
                for i in range(2):
                    for par in range(2):
                        h = slice(64 * par, 64 * par + 64)
                        last = pe.matmul(PS[:, 2 * (n % 2) + par, i * S:i * S + S],
                                         qT[h, 2 * g + i, tt * P:tt * P + P], kT[h, g, :], start=True, stop=True)
                last.then_inc(sem("scores_done"), 1)

            pe.wait_ge(sem("qkT_done"), 2)
            scores(0)
            for n, (tt, g) in enumerate(steps):
                if n + 1 < len(steps):
                    scores(n + 1)
                pe.wait_ge(sem("probs_done"), n + 1)
                if n:
                    pe.wait_ge(sem("pT_done"), n)
                for i in range(4):
                    for kc in range(2):
                        last = pe.transpose(PS[:, 4 + i // 2, ((i % 2) * 2 + kc) * P:((i % 2) * 2 + kc + 1) * P],
                                            pr[:, i, kc * P:kc * P + P], ident)
                last.then_inc(sem("p_turned"), 1)
                pe.wait_ge(sem("pT_done"), n + 1)
                if n:
                    pe.wait_ge(sem("attn_out"), n)
                for i in range(4):
                    for kc in range(2):
                        last = pe.matmul(PS[:, 6, i * HD:i * HD + HD], pT[:, 2 * i + kc, :],
                                         kvn[:, kc, NKV * HD + g * HD:NKV * HD + g * HD + HD],
                                         start=kc == 0, stop=kc == 1, skip_group_check=True)
                last.then_inc(sem("pv_done"), 1)
            pe.wait_ge(sem("diag_done"), 2)
            for c in range(LC):
                for tt in range(TT):
                    last = pe.matmul(PS[:, c // 2, (c % 2) * S + tt * P:(c % 2) * S + tt * P + P],
                                     yn[:, tt, c * P:c * P + P], diag[:, tt, :], start=True, stop=True)
            last.then_inc(sem("y_turned"), 1)

            pe.wait_ge(sem("bd_loaded"), 128)
            pe.wait_ge(sem("y_attn_done"), 1)
            for kind in range(4):
                if kind >= 2:
                    pe.wait_ge(sem("gates_read"), kind - 1)
                for c in range(LC):
                    last = pe.matmul(PS[:, 4 * (kind % 2) + c // 2, (c % 2) * S:(c % 2) * S + S],
                                     wbd[:, kind, c, :], convT[:, c, :], start=True, stop=True)
                last.then_inc(sem("gates_done"), 1)
            pe.wait_ge(sem("lru_squared"), 1)
            for c in range(LC):
                last = pe.matmul(PS[:, 0, 0:S], ones, rr[:, c, :], start=c == 0, stop=c == LC - 1)
            last.then_inc(sem("lru_summed"), 1)
            pe.wait_ge(sem("y_lru_done"), 1)
            all_rows("w_out")

            pe.wait_ge(sem("x1_done"), 1)
            pe.wait_ge(sem("diag_done"), 3)
            turn(1, lambda tt: diag[:, tt, :])
            pe.wait_ge(xt_lo_done, 2 * KC)
            channel_blocks("w_pq", act_free, ACT_BLOCKS["w_pq"])
            pe.wait_ge(sem("keys_loaded"), 16)
            pe.wait_ge(act_free, 2 + ACT_BLOCKS["w_pq"] + 16)
            for tt in range(TT):
                for i in range(2 * PH):
                    last = pe.matmul(PS[:, 4 * tt + i // 4, (i % 4) * NK:(i % 4 + 1) * NK],
                                     pqT[:, i, tt * P:tt * P + P], skT[:, i, :], start=True, stop=True)
            last.then_inc(sem("keys_scored"), 1)
            pe.wait_ge(sem("slots_done"), 1)
            for what in range(3):
                for tt in range(TT):
                    last = pe.transpose(PS[:, what, tt * P:tt * P + P],
                                        slots[:, what, tt * PH:(tt + 1) * PH, :].rearrange("p h k -> p (h k)"), ident)
            last.then_inc(sem("slots_turned"), 1)
            pe.wait_ge(sem("route_over"), 1)

            for half in range(HALVES):
                u, v = f"u{half}", f"v{half}"
                for part in range(2):
                    with pe.Fori(0, 16) as j:
                        jj = j + 16 * part
                        for b in range(2):
                            pe.wait_ge(act_free, 2 * jj + ACT_BLOCKS[u] + b + 1)
                            for h in range(2):
                                i = 2 * b + h
                                pe.wait_ge(lo_done, 4 * (jj + FIRST_BODY[u]) + i + 1)
                                for k in range(8):
                                    w = slice(k * P, k * P + P)
                                    last = three(PS[:, b, 0:S], w_hi[:, i, w], w_lo[:, i, w],
                                                 xt_hi[:, 8 * h + k, :], xt_lo[:, 8 * h + k, :],
                                                 h == 0 and k == 0, h == 1 and k == 7)
                                last.then_inc(tile_used, 1)
                    seg = 2 * half + part
                    pe.wait_ge(sem("ada_used"), 48 * (seg + 1) + 3)
                    for q in range(3):
                        for c in range(8):
                            last = pe.matmul(PS[:, 7, q * 8 + c:q * 8 + c + 1], ada_acc[:, q, c * P:c * P + P],
                                             ones[:, 0:1], start=True, stop=True, skip_group_check=True)
                    last.then_inc(sem("ada_summed"), 1)
                if half == 0:
                    pe.sem_inc(sem("gates_spread"), 2)
                with pe.Fori(0, 32) as j:
                    for r in range(2):
                        pe.wait_ge(sem("hot_done"), 2 * j + (64 * half + r + 1))
                        pe.wait_ge(sem("gates_applied"), 2 * j + (64 * half + r + 1))
                        for t in range(4):
                            last = pe.matmul(PS[:, 4 + r, t * EB:t * EB + EB], hot1[:, r, t, :], hot2[:, r, t, :],
                                             start=True, stop=True, skip_group_check=True)
                        last.then_inc(sem("gates_spread"), 1)
                pe.wait_ge(sem("gates_applied"), 64 * (half + 1) + 2)
                pe.wait_ge(sem("mod_done"), 2 * (half + 1))
                pe.wait_ge(act_free, 2 + ACT_BLOCKS[u] + EB)
                all_rows(v)
                pe.wait_ge(sem("x2_done"), half + 1)

            pe.wait_ge(sem("x3_done"), 1)
            turn(2, lambda tt: ident)
            pe.wait_ge(sem("w_dt_loaded"), 32)
            pe.wait_ge(xt_lo_done, 3 * KC)
            for k in range(KC):
                pe.matmul(PS[0:SHEADS, 2, 0:S], w_dt[:, k, :], xt_hi[:, k, :].bitcast(F32), start=k == 0, stop=False)
                last = pe.matmul(PS[0:SHEADS, 2, 0:S], w_dt[:, k, :], xt_lo[:, k, :].bitcast(F32),
                                 start=False, stop=k == KC - 1)
            last.then_inc(sem("dt_product"), 1)
            channel_blocks("xbc", dve_free, DVE_BLOCKS["xbc"])
            pe.wait_ge(sem("decay_done"), 1)
            for tt in range(TT):
                t = slice(tt * P, tt * P + P)
                pe.transpose(PS[:, 3, tt * 64:tt * 64 + 64], dts[:, 0, t], ident[0:SHEADS, 0:SHEADS])
                last = pe.transpose(PS[:, 3, P + tt * 64:P + tt * 64 + 64], dts[:, 1, t], ident[0:SHEADS, 0:SHEADS])
            last.then_inc(sem("dt_turned"), 1)
            pe.wait_ge(sem("ssd_ready"), 1)
            pe.wait_ge(sem("dtn_done"), 1)
            pe.wait_ge(dve_free, 2 + DVE_BLOCKS["xbc"] + BC)
            pe.sem_inc(sem("group_done"), 1)
            pe.sem_inc(sem("y_product"), 2)
            with pe.Fori(0, SG) as g:
                pe.wait_ge(sem("group_staged"), 3 * g + 3)
                pe.wait_ge(sem("xd_done"), 2 * g + 1)
                for tt in range(TT):
                    for c in range(4):
                        last = pe.transpose(PS[:, tt, c * P:c * P + P], xs_st[:, c, tt * P:tt * P + P], ident)
                last.then_inc(sem("xs_turned"), 1)
                pe.wait_ge(sem("cb_done"), g + 1)
                pe.matmul(PS[:, 2, 0:S], b_st[:, 0:P], one(xbc, g + XC + SG),
                          start=True, stop=True, skip_group_check=True)
                pe.matmul(PS[:, 2, S:S + P], b_st[:, P:S],
                          xbc[:, ds(g + XC + SG, 1), P:S].rearrange("p a s -> p (a s)"),
                          start=True, stop=True, skip_group_check=True).then_inc(sem("cb_product"), 1)

                def spread(k):
                    pe.wait_ge(sem("decays_read"), 8 * g + k + 1)
                    o = 3 + k % 2
                    pe.matmul(PS[:, o, 0:S], pick_h[:, k, :], dts[:, 2, :], start=True, stop=False,
                              skip_group_check=True)
                    pe.matmul(PS[:, o, S:S + P], pick_h[:, k, :], dts[:, 2, P:S], start=False, stop=False,
                              skip_group_check=True)
                    masked = pe.matmul(PS[:, o, 0:P], ident_b[:, :], causal_b[:, :], start=False, stop=False,
                                       skip_group_check=True)
                    if k == 7:
                        masked.then_inc(sem("group_done"), 1)
                    pe.matmul(PS[:, o, S:S + P], ident_b[:, :], causal_b[:, :], start=False, stop=True,
                              skip_group_check=True).then_inc(sem("decays_spread"), 1)

                spread(0)
                for k in range(8):
                    if k < 7:
                        spread(k + 1)
                    if k == 0:
                        pe.wait_ge(sem("xd_done"), 2 * g + 3)
                    pe.wait_ge(sem("mixed"), 8 * g + k + 3)
                    if k % 2 == 0:
                        pe.wait_ge(sem("y_added"), 4 * g + k // 2 + 1)
                    h = slice(64 * (k % 2), 64 * (k % 2) + 64)
                    o = 5 + (k // 2) % 2
                    pe.matmul(PS[h, o, 0:S], xd[:, 0, k * 64:k * 64 + 64], mm_[:, k % 2, 0:S], start=True, stop=False,
                              skip_group_check=True)
                    pe.matmul(PS[h, o, P:S], xd[:, 1, k * 64:k * 64 + 64], mm_[:, k % 2, S:S + P],
                              start=False, stop=True, skip_group_check=True).then_inc(sem("y_product"), 1)
            pe.wait_ge(sem("y_added"), 32 + 2)
            channel_blocks("z", act_free, ACT_BLOCKS["z"])
            with pe.Fori(0, SG) as g:
                pe.wait_ge(sem("group_squared"), g + 1)
                pe.wait_ge(sem("group_root"), g + 1)
                for c in range(4):
                    last = pe.matmul(PS[:, 2, 0:S], ones, sq[:, c, :], start=c == 0, stop=c == 3)
                last.then_inc(sem("group_summed"), 1)
            pe.wait_ge(sem("ssd_normed"), SG + 1)
            all_rows("a_out")

            def gate_rows(layer):
                for c in range(KC):
                    pe.wait_ge(sem("dcol_done"), KC * layer + c + 1)
                    pe.matmul(PS[:, c // 4, (c % 4) * P:(c % 4 + 1) * P], ones, dcol[:, c % 2, :],
                              start=True, stop=True, skip_group_check=True).then_inc(sem("gate_spread"), 1)

            pe.wait_ge(sem("y_copied"), 1)
            gate_rows(0)

            pe.wait_ge(sem("x4_done"), 1)
            turn(3, lambda tt: ident)
            pe.wait_ge(xt_lo_done, 4 * KC)
            channel_blocks("k2", act_free, ACT_BLOCKS["k2"])
            pe.wait_ge(act_free, 2 + ACT_BLOCKS["k2"] + 24)
            with pe.Fori(0, DG) as g:
                pe.wait_ge(sem("v2_out"), g + 1)
                token_columns(16 * g, FIRST_BODY["v2"], 0, 1)
            pe.wait_ge(sem("v2_out"), DG + 1)
            turn(4, lambda tt: ident)
            pe.wait_ge(xt_lo_done, 5 * KC)
            channel_blocks("q2", act_free, ACT_BLOCKS["q2"])
            token_columns(0, FIRST_BODY["z2"], 4, 1)
            pe.wait_ge(sem("z2_out"), 1)
            pe.sem_inc(sem("head_scored"), 1)
            with pe.Fori(0, DH) as h:
                pe.wait_ge(sem("q_staged"), h + 1)
                pe.wait_ge(sem("dist_added"), h + 1)
                for g in range(DG):
                    pe.matmul(PS[:, 0, g * P:g * P + P], q_st[:, g, 0:P],
                              k2T[:, ds(h + g * DH, 1), 0:P].rearrange("p a s -> p (a s)"),
                              start=True, stop=True, skip_group_check=True)
                    last = pe.matmul(PS[:, 1 + g // 2, (g % 2) * S:(g % 2) * S + S], q_st[:, g, P:S],
                                     one(k2T, h + g * DH),
                                     start=True, stop=True, skip_group_check=True)
                last.then_inc(sem("head_scored"), 1)
                pe.wait_ge(sem("head_exp"), h + 1)
                for i in range(9):
                    last = pe.transpose(PS[:, 3 + i // 4, (i % 4) * P:(i % 4 + 1) * P], sc2[:, i * P:i * P + P], ident)
                last.then_inc(sem("head_turned"), 1)
                pe.wait_ge(sem("pT2_done"), h + 1)
                pe.wait_ge(sem("head_out"), h + 1)
                for g in range(DG):
                    pe.matmul(PS[:, 6, 0:P], pT2[:, g, :], v2n[:, 0, ds(h * P + g * 1024, P)],
                              start=g == 0, stop=g == DG - 1, skip_group_check=True)
                for g in range(DG):
                    for kt in range(2):
                        last = pe.matmul(PS[:, 7, 0:P], pT2[:, 3 + 2 * g + kt, :],
                                         v2n[:, kt, ds(h * P + g * 1024, P)],
                                         start=g == 0 and kt == 0, stop=g == DG - 1 and kt == 1,
                                         skip_group_check=True)
                last.then_inc(sem("head_product"), 1)
            pe.wait_ge(sem("head_out"), DH + 1)
            for c in range(DH):
                for tt in range(TT):
                    last = pe.transpose(PS[:, c // 2, (c % 2) * S + tt * P:(c % 2) * S + tt * P + P],
                                        zn[:, tt, c * P:c * P + P], ident)
            last.then_inc(sem("o_turned"), 1)
            pe.wait_ge(sem("oT_done"), 1)
            all_rows("b_out")
            pe.wait_ge(sem("y_copied"), 2)
            gate_rows(1)

        @block.scalar
        def _(act):
            def high(body, u, first=False):
                act.wait_ge(raw_loaded[u], 16 * (body + 1))
                if not first:
                    act.wait_ge(tile_used, 4 * body + u - 3)
                act.activation(w_hi[:, u, :], raw[:, u, :], ACT.Copy).then_inc(hi_done, 1)

            def bodies(name, evac=None, start=0, n=None, last=False):
                n = NB[name] if n is None else n
                with act.Fori(start, start + n) as j:
                    for u in range(4):
                        if not last:
                            high(j + FIRST_BODY[name] + 1, u)
                        if evac and u % 2 == 1:
                            act.wait_ge(tile_used, 4 * (j + FIRST_BODY[name]) + u + 1)
                            evac(2 * j + u // 2, u // 2)

            def stage(name, source, k, s, body):
                act.wait_ge(tile_used, 4 * body + 2 * s + 2)
                act.activation(st_hi[:, s, :], source(k), ACT.Copy).then_inc(stage_hi_done, 1)

            def rows_bodies(name, source):
                f = FIRST_BODY[name]
                n = NB[name]
                act.wait_ge(tile_used, 4 * f)
                for s in range(2):
                    act.activation(st_hi[:, s, :], source(s), ACT.Copy).then_inc(stage_hi_done, 1)
                with act.Fori(0, n - 1) as j:
                    for u in range(4):
                        high(j + f + 1, u)
                        if u % 2 == 1:
                            stage(name, source, 2 * j + 2 + u // 2, u // 2, j + f)
                if name != "b_out":
                    for u in range(4):
                        high(f + n, u)

            def turned(n, scale, bias=None):
                for c in range(KC):
                    act.wait_ge(xt_turned, KC * n + c + 1)
                    act.activation(xt_hi[:, c, :], PS[:, c % 8, 0:S], ACT.Identity, scale=scale(c),
                                   bias=bias(c) if bias else 0.0).then_inc(xt_hi_done, 1)

            def root(o, i, scale, eps):
                return act.activation(o, i, ACT.Sqrt, scale=scale, bias=pc[:, PC[eps]:PC[eps] + 1])

            act.wait_ge(params_loaded, 16)
            act.wait_ge(x_loaded, 16)
            act.sem_inc(act_free, 2)
            for u in range(4):
                high(0, u, first=True)
            for tt in range(TT):
                act.activation(PS[:, 0:4, :].rearrange("p b n -> p (b n)"), X[:, tt, :], ACT.Square,
                               accum_out=stat[:, tt:tt + 1]).then_inc(sem("x_squared"), 1)
                act.wait_ge(sem("x_squared"), tt + 1)
            root(stat[:, 2:4], stat[:, 0:2], 1.0 / D, "eps").then_inc(sem("rms_root"), 1)
            turned(0, lambda c: pc[:, PC["g_mix"] + c:PC["g_mix"] + c + 1])
            with act.Fori(0, NB["q"]) as j:
                for u in range(4):
                    high(j + 1, u)
            act.wait_ge(tile_used, 16)
            for tt in range(TT):
                last = act.activation(qn[:, tt, :], PS[:, 2 * tt:2 * tt + 2, :].rearrange("p b n -> p (b n)"), ACT.Copy)
            last.then_inc(sem("qkv_out"), 1)
            bodies("kv")
            act.wait_ge(tile_used, 24)
            act.activation(kvn[:, :, :], PS[:, 4:6, :], ACT.Copy).then_inc(sem("qkv_out"), 1)
            bodies("gate", lambda i, b: act.activation(
                one(gateT, i), PS[:, b, 0:S],
                ACT.Gelu_apprx_tanh).then_inc(act_free, 1))
            bodies("rec")
            act.wait_ge(sem("qk_turned"), 1)
            act.activation(qT[:, :, :].rearrange("p c s -> p (c s)"), PS[:, 0:4, :].rearrange("p b n -> p (b n)"),
                           ACT.Copy).then_inc(sem("qkT_done"), 1)
            act.activation(kT[:, :, :].rearrange("p c s -> p (c s)"), PS[:, 4:6, :].rearrange("p b n -> p (b n)"),
                           ACT.Copy).then_inc(sem("qkT_done"), 1)
            for n in range(8):
                act.wait_ge(sem("max_done"), n + 1)
                if n:
                    act.wait_ge(sem("p_turned"), n)
                act.activation(sm[:, n, 1, :], sm[:, n, 1, :], ACT.Exp).then_inc(sem("sink_exp"), 1)
                for i in range(4):
                    last = act.activation(pr[:, i, :], sc[:, n % 2, i, :], ACT.Exp, bias=sm[:, n, 0, i:i + 1],
                                          accum_out=stat[:, 4 + 4 * (n % 2) + i:5 + 4 * (n % 2) + i])
                last.then_inc(sem("probs_done"), 1)
                act.wait_ge(sem("p_turned"), n + 1)
                if n:
                    act.wait_ge(sem("pv_done"), n)
                act.activation(pT[:, :, :].rearrange("p c s -> p (c s)"), PS[:, 4:6, :].rearrange("p b n -> p (b n)"),
                               ACT.Copy).then_inc(sem("pT_done"), 1)
            act.wait_ge(sem("attn_out"), 8)
            for tt in range(TT):
                last = act.activation(PS[:, 0:2, :].rearrange("p b n -> p (b n)"), yn[:, tt, :], ACT.Square,
                                      accum_out=stat[:, tt:tt + 1])
                last.then_inc(sem("y_squared"), 1)
                act.wait_ge(sem("y_squared"), tt + 1)
            root(stat[:, 2:4], stat[:, 0:2], 1.0 / QC, "eps").then_inc(sem("rms_root"), 1)
            act.wait_ge(sem("y_turned"), 1)
            for c in range(LC):
                g = pc[:, PC["g_attn"] + c:PC["g_attn"] + c + 1]
                last = act.activation(yT[:, c, :], PS[:, c // 2, (c % 2) * S:(c % 2) * S + S], ACT.Copy, scale=g)
            last.then_inc(sem("y_attn_done"), 1)
            act.wait_ge(sem("lam_ready"), 1)
            act.activation(spl[:, 1, :], spl[:, 1, :], ACT.Exp).then_inc(sem("lam_exp"), 1)
            act.wait_ge(sem("spl_done"), 1)
            for kind in range(4):
                act.wait_ge(sem("gates_done"), kind + 1)
                if kind == 2:
                    act.wait_ge(sem("forward_used"), 1)
                for c in range(LC):
                    b = PC["gate_b"] + kind * LC + c
                    last = act.activation((rr if kind % 2 == 0 else ii)[:, c, :],
                                          PS[:, 4 * (kind % 2) + c // 2, (c % 2) * S:(c % 2) * S + S],
                                          ACT.Sigmoid, bias=pc[:, b:b + 1])
                last.then_inc(sem("gates_read"), 1)
                if kind % 2 == 1:
                    act.wait_ge(sem("gates_read"), kind + 1)
                    dr = kind // 2
                    for c in range(LC):
                        act.activation(aa[:, c, :], rr[:, c, :], ACT.Exp, scale=spl[:, 7, dr * LC + c:dr * LC + c + 1])
                    for c in range(LC):
                        last = act.activation(rr[:, c, :], rr[:, c, :], ACT.Tanh,
                                              scale=spl[:, 6, dr * LC + c:dr * LC + c + 1])
                    last.then_inc(sem("decays_done"), 1)
                    act.wait_ge(sem("one_minus_done"), dr + 1)
                    act.activation(hh[:, dr, :, :], hh[:, dr, :, :], ACT.Sqrt,
                                   bias=pc[:, PC["tiny"]:PC["tiny"] + 1]).then_inc(sem("root_done"), 1)
            act.wait_ge(sem("y_mixed"), 1)
            act.activation(rr[:, :, :], yT[:, LC:2 * LC, :], ACT.Square).then_inc(sem("lru_squared"), 1)
            act.wait_ge(sem("lru_summed"), 1)
            root(rstdb[:, 0, :], PS[:, 0, 0:S], 1.0 / LRU, "eps").then_inc(sem("lru_root"), 1)
            act.wait_ge(sem("y_lru_done"), 1)
            rows_bodies("w_out", lambda k: one(yT, k))
            act.wait_ge(sem("x1_done"), 1)
            for tt in range(TT):
                act.activation(PS[:, 0:4, :].rearrange("p b n -> p (b n)"), X[:, tt, :], ACT.Square,
                               accum_out=stat[:, tt:tt + 1]).then_inc(sem("x_squared"), 1)
                act.wait_ge(sem("x_squared"), 2 + tt + 1)
            root(stat[:, 2:4], stat[:, 0:2], 1.0 / D, "eps").then_inc(sem("rms_root"), 1)
            turned(1, lambda c: pc[:, PC["g_ffn"] + c:PC["g_ffn"] + c + 1])
            bodies("w_pq", lambda i, b: act.activation(
                one(pqT, i), PS[:, b, 0:S], ACT.Copy).then_inc(act_free, 1))
            act.wait_ge(sem("keys_scored"), 1)
            for tt in range(TT):
                last = act.activation(score[:, tt * 16:(tt + 1) * 16, :].rearrange("p c s -> p (c s)"),
                                      PS[:, 4 * tt:4 * tt + 4, :].rearrange("p b n -> p (b n)"), ACT.Copy)
                last.then_inc(sem("scores_out"), 1)
            act.wait_ge(sem("pick_shifted"), 1)
            act.activation(pick[:, :, :], pick[:, :, :], ACT.Exp).then_inc(sem("pick_exp"), 1)
            act.wait_ge(sem("slots_turned"), 1)
            act.activation(slotsT[:, :, :], PS[:, 0:3, 0:S], ACT.Copy).then_inc(sem("route_over"), 1)
            act.activation(silu_c[:, :], pc[:, PC["cond"]:PC["cond"] + KC], ACT.Silu).then_inc(sem("silu_c_done"), 1)
            for half in range(HALVES):
                u, v = f"u{half}", f"v{half}"
                bodies(u, lambda i, b: act.activation(
                    one(hid, i), PS[:, b, 0:S],
                    ACT.Gelu_apprx_tanh).then_inc(act_free, 1))
                act.wait_ge(sem("gates_applied"), 64 * (half + 1) + 2)
                rows_bodies(v, lambda k: one(hid, k))
            act.wait_ge(sem("x2_done"), HALVES)
            for tt in range(TT):
                act.activation(PS[:, 0:4, :].rearrange("p b n -> p (b n)"), X[:, tt, :], ACT.Square,
                               accum_out=stat[:, tt:tt + 1]).then_inc(sem("x_squared"), 1)
                act.wait_ge(sem("x_squared"), 4 + tt + 1)
            root(stat[:, 2:4], stat[:, 0:2], 1.0 / D, "eps").then_inc(sem("rms_root"), 1)
            act.wait_ge(sem("mod_done"), 5)
            turned(2, lambda c: mod[:, 16 + c:17 + c], lambda c: mod[:, c:c + 1])
            act.wait_ge(sem("dt_abs"), 1)
            act.activation(dts[:, 3, :], dts[:, 3, :], ACT.Exp).then_inc(sem("dt_exp"), 1)
            act.activation(stat[0:SHEADS, 12:13], pc[0:SHEADS, PC["a_log"]:PC["a_log"] + 1], ACT.Exp)\
                .then_inc(sem("dt_exp"), 1)
            act.sem_inc(sem("conv_read"), 2)
            with act.Fori(0, NB["xbc"]) as j:
                def silu(b):
                    i = 2 * j + b
                    act.wait_ge(sem("conv_done"), i + 1)
                    act.activation(one(xbc, i), cbuf[:, b, :], ACT.Silu,
                                   bias=pc[:, ds(i + PC["a_conv_b"], 1)]).then_inc(sem("conv_read"), 1)

                for u in range(4):
                    high(j + FIRST_BODY["xbc"] + 1, u)
                    if u >= 2:
                        silu(u - 2)
            act.activation(ident_b[:, :], ident, ACT.Copy)
            act.activation(causal_b[:, :], causal[:, :], ACT.Copy).then_inc(sem("masks_done"), 1)
            act.wait_ge(sem("dt_turned"), 1)
            act.activation(dtn[:, :, :].rearrange("p a s -> p (a s)"), PS[:, 3, 0:P], ACT.Copy)
            act.activation(nacn[:, :, :].rearrange("p a s -> p (a s)"), PS[:, 3, P:2 * P], ACT.Copy, scale=-1.0)\
                .then_inc(sem("dtn_done"), 1)
            act.wait_ge(sem("conv_read"), BC + 2)
            act.wait_ge(sem("masks_done"), 1)
            act.wait_ge(sem("dtn_done"), 1)
            act.sem_inc(sem("ssd_ready"), 1)
            act.sem_inc(sem("cb_done"), 1)
            act.sem_inc(sem("decays_read"), 2)
            with act.Fori(0, SG) as g:
                act.wait_ge(sem("cb_product"), g + 1)
                act.wait_ge(sem("mixed"), 8 * g + 2)
                act.activation(cbm[:, :], PS[:, 2, 0:384], ACT.Copy).then_inc(sem("cb_done"), 1)
                for k in range(8):
                    act.wait_ge(sem("decays_spread"), 8 * g + k + 1)
                    act.wait_ge(sem("mixed"), 8 * g + k + 1)
                    o = 3 + k % 2
                    act.activation(ex[:, k % 2, 0:S], PS[:, o, 0:S], ACT.Exp, bias=nacn[:, 0, ds(8 * g + k, 1)])
                    act.activation(ex[:, k % 2, S:384], PS[:, o, S:384], ACT.Exp, bias=nacn[:, 1, ds(8 * g + k, 1)])\
                        .then_inc(sem("decays_read"), 1)
            def gates(i, b):
                act.wait_ge(sem("y_gated"), i + 1)
                act.activation(zt[:, b, :], PS[:, b, 0:S], ACT.Silu).then_inc(act_free, 1)

            bodies("z", gates)
            act.wait_ge(sem("y_gated"), XC + 2)
            act.sem_inc(sem("group_root"), 1)
            with act.Fori(0, SG) as g:
                act.activation(sq[:, :, :], xbc[:, ds(4 * g, 4), :], ACT.Square).then_inc(sem("group_squared"), 1)
                act.wait_ge(sem("group_summed"), g + 1)
                act.wait_ge(sem("ssd_normed"), g + 1)
                root(rg[:, 0, :], PS[:, 2, 0:S], 1.0 / 512, "ln_eps").then_inc(sem("group_root"), 1)
            act.wait_ge(sem("ssd_normed"), SG + 1)
            rows_bodies("a_out", lambda k: one(xbc, k))

            def layer_norm(n):
                act.wait_ge(sem("y_copied"), n + 1)
                act.wait_ge(sem("gate_spread"), KC * (n + 1))
                act.activation(rows[:, 0, :], PS[:, 0:4, :].rearrange("p b n -> p (b n)"), ACT.Copy)\
                    .then_inc(sem("gate_rows_done"), 1)
                for tt in range(TT):
                    act.wait_ge(sem("ln_in"), TT * n + tt + 1)
                    act.activation(PS[:, 0:4, :].rearrange("p b n -> p (b n)"), X[:, tt, :], ACT.Copy,
                                   accum_out=stat[:, tt:tt + 1]).then_inc(sem("ln_sum"), 1)
                    act.wait_ge(sem("ln_sum"), TT * n + tt + 1)
                for tt in range(TT):
                    act.wait_ge(sem("ln_centred"), TT * n + tt + 1)
                    act.activation(PS[:, 0:4, :].rearrange("p b n -> p (b n)"), X[:, tt, :], ACT.Square,
                                   accum_out=stat[:, 4 + tt:5 + tt]).then_inc(sem("ln_squared"), 1)
                    act.wait_ge(sem("ln_squared"), TT * n + tt + 1)
                root(stat[:, 6:8], stat[:, 4:6], 1.0 / D, "ln_eps").then_inc(sem("ln_root"), 1)

            layer_norm(0)
            turned(3, lambda c: 1.0)
            bodies("k2", lambda i, b: act.activation(
                one(k2T, i), PS[:, b, 0:S], ACT.Copy).then_inc(act_free, 1))
            act.sem_inc(sem("v2_out"), 1)
            with act.Fori(0, DG) as g:
                for i in range(4):
                    for u in range(4):
                        high(4 * g + (FIRST_BODY["v2"] + i + 1), u)
                act.wait_ge(tile_used, 16 * g + 4 * FIRST_BODY["v2"] + 16)
                for tt in range(TT):
                    last = act.activation(v2n[:, tt, ds(g * 1024, 1024)],
                                          PS[:, 2 * tt:2 * tt + 2, :].rearrange("p b n -> p (b n)"), ACT.Copy)
                last.then_inc(sem("v2_out"), 1)
            turned(4, lambda c: mod[:, 64 + c:65 + c], lambda c: mod[:, 48 + c:49 + c])

            def queries(i, b):
                act.activation(one(q2T, i), PS[:, b, 0:S], ACT.Copy,
                               scale=float(P) ** -0.5).then_inc(act_free, 1)

            bodies("q2", queries)
            bodies("z2")
            act.wait_ge(tile_used, 4 * FIRST_BODY["b_out"])
            for tt in range(TT):
                last = act.activation(zn[:, tt, :], PS[:, 4 + 2 * tt:6 + 2 * tt, :].rearrange("p b n -> p (b n)"), ACT.Silu)
            last.then_inc(sem("z2_out"), 1)
            with act.Fori(0, DH) as h:
                act.wait_ge(sem("head_max"), h + 1)
                act.activation(sc2[:, 0:384], sc2[:, 0:384], ACT.Exp, bias=sm2[:, 2:3], accum_out=sm2[:, 4:5])
                act.activation(sc2[:, 384:1152], sc2[:, 384:1152], ACT.Exp, bias=sm2[:, 3:4], accum_out=sm2[:, 5:6])\
                    .then_inc(sem("head_exp"), 1)
                act.wait_ge(sem("head_turned"), h + 1)
                act.activation(pT2[:, 0:8, :].rearrange("p c s -> p (c s)"),
                               PS[:, 3:5, :].rearrange("p b n -> p (b n)"), ACT.Copy)
                act.activation(pT2[:, 8, :], PS[:, 5, 0:P], ACT.Copy).then_inc(sem("pT2_done"), 1)
            act.wait_ge(sem("o_turned"), 1)
            act.activation(oT[:, 0:DH, :].rearrange("p c s -> p (c s)"), PS[:, 0:4, :].rearrange("p b n -> p (b n)"),
                           ACT.Copy).then_inc(sem("oT_done"), 1)
            act.wait_ge(sem("oT_done"), 1)
            rows_bodies("b_out", lambda k: one(oT, k))
            layer_norm(1)

        @block.vector
        def _(dve):
            link = Chain(dve, dve_link)

            def low(body, u):
                dve.wait_ge(hi_done, 4 * body + u + 1)
                dve.tensor_tensor(w_lo[:, u, :], raw[:, u, :], w_hi[:, u, :].bitcast(F32), ALU.subtract)\
                    .then_inc(lo_done, 1)

            def bodies(name, evac=None):
                with dve.Fori(0, NB[name]) as j:
                    if evac:
                        link.loop(j, evac.links * 2)
                    for u in range(4):
                        low(j + FIRST_BODY[name] + 1, u)
                        if evac and u % 2 == 1:
                            dve.wait_ge(tile_used, 4 * j + (4 * FIRST_BODY[name] + u + 1))
                            evac(2 * j + u // 2, u // 2)
                if evac:
                    link.end(NB[name])

            def stage(source, k, s, name):
                dve.wait_ge(stage_hi_done, k + (CHUNKS[name] + 1))
                dve.tensor_tensor(st_lo[:, s, :], source(k), st_hi[:, s, :].bitcast(F32), ALU.subtract)\
                    .then_inc(stage_lo_done, 1)

            def rows_bodies(name, source):
                for s in range(2):
                    stage(source, s, s, name)
                with dve.Fori(0, NB[name] - 1) as j:
                    for u in range(4):
                        low(j + (FIRST_BODY[name] + 1), u)
                        if u % 2 == 1:
                            stage(source, 2 * j + (2 + u // 2), u // 2, name)
                if name != "b_out":
                    for u in range(4):
                        low(FIRST_BODY[name] + NB[name], u)
                dve.wait_ge(tile_used, 4 * (FIRST_BODY[name] + NB[name]))

            def banks(first, n):
                return PS[:, first:first + n, :].rearrange("p b n -> p (b n)")

            def turned(n, scale, bias=None):
                for c in range(KC):
                    src = PS[:, c % 8, 0:S]
                    hi = xt_hi[:, c, :].bitcast(F32)
                    dve.wait_ge(xt_hi_done, KC * n + c + 1)
                    if bias:
                        link(dve.tensor_scalar(xtmp[:, c % 2, :], src, scale(c), bias(c), ALU.mult, ALU.add))
                        o = dve.tensor_tensor(xt_lo[:, c, :], xtmp[:, c % 2, :], hi, ALU.subtract)
                    else:
                        o = dve.scalar_tensor_tensor(xt_lo[:, c, :], src, scale(c), hi, ALU.mult, ALU.subtract)
                    o.then_inc(xt_lo_done, 1)

            def row_norms(n):
                dve.wait_ge(sem("rms_root"), n)
                link(dve.reciprocal(stat[:, 12:14], stat[:, 2:4]))
                for tt in range(TT):
                    last = dve.tensor_scalar(diag[:, tt, :], ident, stat[:, 12 + tt:13 + tt], None, ALU.mult)
                last.then_inc(sem("diag_done"), 1)

            def softplus(o, x, e, t1, t2, t3):
                link(dve.tensor_scalar(t1, e, 2.0, None, ALU.add))
                link(dve.reciprocal(t1, t1))
                link(dve.tensor_tensor(t1, t1, e, ALU.mult))
                link(dve.tensor_tensor(t2, t1, t1, ALU.mult))
                link(dve.tensor_scalar(t3, t2, 1.0 / 17, None, ALU.mult))
                for n in range(15, 1, -2):
                    link(dve.scalar_tensor_tensor(t3, t3, 1.0 / n, t2, ALU.add, ALU.mult))
                link(dve.scalar_tensor_tensor(t3, t3, 1.0, t1, ALU.add, ALU.mult))
                link(dve.tensor_scalar(t1, x, 0.0, None, ALU.max))
                link(dve.scalar_tensor_tensor(o, t3, 2.0, t1, ALU.mult, ALU.add))

            def convolve(o, src, weight, centre):
                link(dve.tensor_scalar(o, src, weight(centre), None, ALU.mult))
                for t in range(4):
                    d = t - centre
                    if d < 0:
                        link(dve.scalar_tensor_tensor(o[:, -d:S], src[:, 0:S + d], weight(t), o[:, -d:S], ALU.mult, ALU.add))
                    if d > 0:
                        link(dve.scalar_tensor_tensor(o[:, 0:S - d], src[:, d:S], weight(t), o[:, 0:S - d], ALU.mult, ALU.add))

            dve.sem_inc(dve_free, 2)
            for u in range(4):
                low(0, u)
            dve.wait_ge(consts_loaded, 16)
            dve.wait_ge(params_loaded, 16)
            row_norms(1)
            turned(0, lambda c: pc[:, PC["g_mix"] + c:PC["g_mix"] + c + 1])
            for name in ("q", "kv", "gate"):
                bodies(name)

            def recurrent(i, b):
                convolve(one(convT, i), PS[:, b, 0:S], lambda t: pc[:, ds(4 * i + (PC["conv_w"] + t), 1)], 2)
                link(dve.tensor_scalar(one(convT, i), one(convT, i), pc[:, ds(i + PC["conv_b"], 1)], None, ALU.add))
                dve.sem_inc(dve_free, 1)

            recurrent.links = 5
            bodies("rec", recurrent)

            dve.wait_ge(sem("window_loaded"), 32)
            dve.wait_ge(sem("qkv_out"), 2)
            flat = rtmp[:, :, :, :].rearrange("p a b s -> p (a b s)")
            for tt in range(TT):
                def angles(name, shape):
                    return cw[:, CW[name] + tt * 32:CW[name] + tt * 32 + 32].unsqueeze(1).to_broadcast(shape)

                for src, heads, outs in (
                    (qn[:, tt, :], NQ, [qn[:, tt, :].rearrange("p (h d) -> p h d", d=HD)]),
                    (kvn[:, tt, 0:NKV * HD], NKV, [kdup[:, tt, :, r, :] for r in range(2)]),
                ):
                    x = src.rearrange("p (h d) -> p h d", d=HD)
                    n = heads * 32
                    tmp = [flat[:, i * n:(i + 1) * n].rearrange("p (h d) -> p h d", d=32) for i in range(4)]
                    cos, sin = angles("cos", [P, heads, 32]), angles("sin", [P, heads, 32])
                    link.post(dve.tensor_tensor(tmp[0], x[:, :, 0:32], cos, ALU.mult))
                    link.post(dve.tensor_tensor(tmp[1], x[:, :, 32:64], sin, ALU.mult))
                    link.post(dve.tensor_tensor(tmp[2], x[:, :, 32:64], cos, ALU.mult))
                    link(dve.tensor_tensor(tmp[3], x[:, :, 0:32], sin, ALU.mult))
                    for o in outs:
                        link.post(dve.tensor_tensor(o[:, :, 0:32], tmp[0], tmp[1], ALU.subtract))
                        link(dve.tensor_tensor(o[:, :, 32:64], tmp[2], tmp[3], ALU.add))
            dve.sem_inc(sem("rope_done"), 1)

            steps = [(tt, g) for tt in range(TT) for g in range(NKV)]

            def maxima(n):
                tt, g = steps[n]
                dve.wait_ge(sem("scores_done"), n + 1)
                if n >= 2:
                    dve.wait_ge(sem("probs_done"), n - 1)
                window = cw[:, CW["window"] + tt * S:CW["window"] + (tt + 1) * S].unsqueeze(1).to_broadcast([P, 4, S])
                dve.scalar_tensor_tensor(sc[:, n % 2, :, :], banks(2 * (n % 2), 2).rearrange("p (h s) -> p h s", s=S),
                                         HD ** -0.5, window, ALU.mult, ALU.add).then_inc(sem("scores_read"), 1)
                dve.wait_ge(sem("scores_read"), n + 1)
                link(dve.tensor_reduce(sm[:, n, 0, :], sc[:, n % 2, :, :], AX.X, ALU.max))
                link(dve.tensor_tensor(sm[:, n, 0, :], sm[:, n, 0, :], sinkb[:, 4 * g:4 * g + 4], ALU.max))
                link(dve.tensor_tensor(sm[:, n, 1, :], sinkb[:, 4 * g:4 * g + 4], sm[:, n, 0, :], ALU.subtract))
                dve.tensor_scalar(sm[:, n, 0, :], sm[:, n, 0, :], -1.0, None, ALU.mult).then_inc(sem("max_done"), 1)

            maxima(0)
            for n, (tt, g) in enumerate(steps):
                if n + 1 < len(steps):
                    maxima(n + 1)
                dve.wait_ge(sem("probs_done"), n + 1)
                link(dve.tensor_tensor(sm[:, n, 1, :], sm[:, n, 1, :], stat[:, 4 + 4 * (n % 2):8 + 4 * (n % 2)], ALU.add))
                link(dve.reciprocal(sm[:, n, 1, :], sm[:, n, 1, :]))
                dve.wait_ge(sem("pv_done"), n + 1)
                o = yn[:, tt, g * S:(g + 1) * S].rearrange("p (i r d) -> p r i d", i=2, r=2)
                dve.tensor_tensor(o, PS[:, 6, 0:S].rearrange("p (r i d) -> p r i d", r=2, i=2),
                                  sm[:, n, 1, :].rearrange("p (r i) -> p r i", r=2).unsqueeze(3)
                                  .to_broadcast([P, 2, 2, HD]), ALU.mult).then_inc(sem("attn_out"), 1)
            row_norms(2)

            dve.wait_ge(sem("y_attn_done"), 1)
            lam = pc[:, PC["lam"]:PC["lam"] + 2 * LC]
            link(dve.tensor_scalar(spl[:, 0, :], lam, -1.0, None, ALU.mult))
            dve.scalar_tensor_tensor(spl[:, 1, :], lam, -1.0, lam, ALU.mult, ALU.min).then_inc(sem("lam_ready"), 1)
            dve.wait_ge(sem("lam_exp"), 1)
            softplus(spl[:, 5, :], spl[:, 0, :], spl[:, 1, :], spl[:, 2, :], spl[:, 3, :], spl[:, 4, :])
            link(dve.tensor_scalar(spl[:, 6, :], spl[:, 5, :], 8.0, None, ALU.mult))
            dve.tensor_scalar(spl[:, 7, :], spl[:, 5, :], -8.0, None, ALU.mult).then_inc(sem("spl_done"), 1)
            for dr in range(2):
                wide = lambda t: t.rearrange("p c s -> p (c s)")
                dve.wait_ge(sem("decays_done"), dr + 1)
                h = hh[:, dr, :, :]
                link(dve.tensor_tensor(h, aa[:, :, :], aa[:, :, :], ALU.mult))
                dve.scalar_tensor_tensor(wide(h), wide(h), 1.0, wide(rr[:, :, :]), ALU.add, ALU.mult)\
                    .then_inc(sem("one_minus_done"), 1)
                link(dve.tensor_tensor(ii[:, :, :], ii[:, :, :], convT[:, :, :], ALU.mult))
                edge = 0 if dr == 0 else S - 1
                link(dve.memset(aa[:, :, edge:edge + 1], 0.0))
                dve.wait_ge(sem("root_done"), dr + 1)
                link(dve.tensor_tensor(ii[:, :, :], ii[:, :, :], h, ALU.mult))
                a0, u0, o0 = wide(aa[:, :, :]), wide(ii[:, :, :]), wide(h)
                if dr:
                    a0, u0, o0 = a0[:, ::-1], u0[:, ::-1], o0[:, ::-1]
                dve.tensor_tensor_scan(o0, a0, u0, 0.0, ALU.mult, ALU.add).then_inc(sem("forward_used"), 1)
                dve.wait_ge(sem("forward_used"), dr + 1)
            link(dve.tensor_tensor(hh[:, 0, :, :], hh[:, 0, :, :], hh[:, 1, :, :], ALU.add))
            dve.tensor_tensor(yT[:, LC:2 * LC, :], hh[:, 0, :, :], gateT[:, :, :], ALU.mult).then_inc(sem("y_mixed"), 1)
            dve.wait_ge(sem("lru_root"), 1)
            link(dve.reciprocal(rstdb[:, 1, :], rstdb[:, 0, :]))
            for c in range(LC):
                last = dve.scalar_tensor_tensor(yT[:, LC + c, :], yT[:, LC + c, :], pc[:, PC["g_lru"] + c:PC["g_lru"] + c + 1],
                                                rstdb[:, 1, :], ALU.mult, ALU.mult)
            last.then_inc(sem("y_lru_done"), 1)
            dve.wait_ge(sem("y_lru_done"), 1)

            def add_product(signal):
                for tt in range(TT):
                    last = dve.tensor_tensor(X[:, tt, :], X[:, tt, :], banks(4 * tt, 4), ALU.add)
                    if tt == 0:
                        link.post(last)
                last.then_inc(signal, 1)

            rows_bodies("w_out", lambda k: one(yT, k))
            add_product(sem("x1_done"))
            dve.wait_ge(sem("x1_done"), 1)
            row_norms(3)
            turned(1, lambda c: pc[:, PC["g_ffn"] + c:PC["g_ffn"] + c + 1])
            bodies("w_pq")

            def best(values, left, o_values, o_indices, n):
                for i in range(n):
                    link.post(dve.max(o_values(i)[:, 0:8], values(i)))
                link.wait()
                for i in range(n):
                    link.post(dve.max_index(o_indices(i)[:, 0:8], o_values(i)[:, 0:8], values(i)))
                    link.post(dve.match_replace(left(i), o_values(i)[:, 0:8], values(i), -3.0e38))
                link.wait()
                for i in range(n):
                    link.post(dve.max(o_values(i)[:, 8:16], left(i)))
                link.wait()
                for i in range(n):
                    link.post(dve.max_index(o_indices(i)[:, 8:16], o_values(i)[:, 8:16], left(i)))
                link.wait()

            dve.wait_ge(sem("scores_out"), 2)
            workk = pqT[:, :, :].rearrange("p c s -> p (c s)").rearrange("p (i n) -> p i n", n=NK)
            best(lambda i: score[:, i, :], lambda i: workk[:, i, :], lambda i: topv[:, i, :], lambda i: topi[:, i, :],
                 TT * 2 * PH)
            v = topv[:, :, :].rearrange("p (g h) k -> p g h k", h=2)
            G = TT * PH
            for tt in range(TT):
                g = slice(tt * PH, (tt + 1) * PH)
                link.post(dve.tensor_tensor(cand[:, g, :, :],
                                            v[:, g, 0, :].unsqueeze(3).to_broadcast([P, PH, TOPK, TOPK]),
                                            v[:, g, 1, :].unsqueeze(2).to_broadcast([P, PH, TOPK, TOPK]), ALU.add))
            link(dve.tensor_copy(topf[:, :, :], topi[:, :, :]))
            left = score[:, :, :].rearrange("p c s -> p (c s)").rearrange("p (i n) -> p i n", n=TOPK * TOPK)
            best(lambda i: cand[:, i, :, :].rearrange("p x y -> p (x y)"), lambda i: left[:, i, :],
                 lambda i: pick[:, i, :], lambda i: seli[:, i, :], G)
            link.post(dve.tensor_scalar(selh[:, 0, :, :], seli[:, :, :], 4, None, ALU.logical_shift_right))
            link(dve.tensor_scalar(selh[:, 1, :, :], seli[:, :, :], 15, None, ALU.bitwise_and))
            link(dve.tensor_copy(self_[:, :, :, :], selh[:, :, :, :]))
            link(dve.tensor_tensor(selh[:, 0, :, :].bitcast(F32), pick[:, :, :],
                                   pick[:, :, 0:1].to_broadcast([P, G, TOPK]), ALU.subtract))
            dve.tensor_copy(pick[:, :, :], selh[:, 0, :, :].bitcast(F32)).then_inc(sem("pick_shifted"), 1)
            f = topf[:, :, :].rearrange("p (g h) k -> p g h k", h=2)
            match = pqT[:, :, :].rearrange("p c s -> p (c s)").rearrange("p (i x y) -> p i x y", x=TOPK, y=TOPK)
            sixteen = cc[:, CC["iota16"]:CC["iota16"] + TOPK]
            for h in range(2):
                link(dve.tensor_tensor(match, sixteen.unsqueeze(1).unsqueeze(1).to_broadcast([P, G, TOPK, TOPK]),
                                       self_[:, h, :, :].unsqueeze(3).to_broadcast([P, G, TOPK, TOPK]), ALU.is_equal))
                link(dve.tensor_tensor(match, match, f[:, :, h, :].unsqueeze(2).to_broadcast([P, G, TOPK, TOPK]), ALU.mult))
                link(dve.tensor_reduce(slots[:, h, :, :], match, AX.X, ALU.add))
            dve.wait_ge(sem("pick_exp"), 1)
            link(dve.tensor_reduce(rsum[:, :], pick[:, :, :], AX.X, ALU.add))
            link(dve.reciprocal(rsum[:, :], rsum[:, :]))
            dve.tensor_tensor(slots[:, 2, :, :], pick[:, :, :], rsum[:, :].unsqueeze(2).to_broadcast([P, G, TOPK]),
                              ALU.mult).then_inc(sem("slots_done"), 1)
            dve.wait_ge(sem("silu_c_done"), 1)
            dve.sem_inc(sem("ada_used"), 3)
            dve.sem_inc(sem("gates_applied"), 2)

            for half in range(HALVES):
                u, vv = f"u{half}", f"v{half}"
                for part in range(2):
                    seg = 2 * half + part
                    if seg:
                        dve.wait_ge(sem("ada_summed"), seg)
                    link(dve.memset(ada_acc[:, :, :], 0.0))
                    with dve.Fori(0, 16) as k:
                        for t in range(4):
                            low(k + (16 * part + FIRST_BODY[u] + 1), t)
                            if t:
                                q = t - 1
                                dve.wait_ge(sem(f"ada_loaded{q}"), 16 * k + 16 * (16 * seg + 1))
                                dve.wait_ge(sem("ada_used"), 3 * k + (48 * seg + q + 1))
                                dve.scalar_tensor_tensor(ada_acc[:, q, :], ada[:, q, :], silu_c[:, ds(k, 1)],
                                                         ada_acc[:, q, :], ALU.mult, ALU.add)\
                                    .then_inc(sem("ada_used"), 1)
                    dve.wait_ge(sem("ada_summed"), seg + 1)
                    b = PC["ada_b"] + 24 * seg
                    dve.tensor_tensor(mod[:, 24 * seg:24 * seg + 24], PS[:, 7, 0:24], pc[:, b:b + 24], ALU.add)\
                        .then_inc(sem("mod_done"), 1)
                dve.wait_ge(act_free, 2 + ACT_BLOCKS[u] + EB)
                with dve.Fori(0, 32) as j:
                    for r in range(2):
                        dve.wait_ge(sem("gates_spread"), 2 * j + (64 * half + r + 1))
                        for t in range(4):
                            tok = 8 * j + (4 * r + t)
                            dve.tensor_scalar(hot1[:, r, t, :], cc[:, CC["iota"]:CC["iota"] + NK],
                                              slotsT[:, 0, ds(tok, 1)], slotsT[:, 2, ds(tok, 1)],
                                              ALU.is_equal, ALU.mult)
                            i0 = CC["iota"] + half * EB
                            last = dve.tensor_scalar(hot2[:, r, t, :], cc[:, i0:i0 + EB],
                                                     slotsT[:, 1, ds(tok, 1)], None, ALU.is_equal)
                        last.then_inc(sem("hot_done"), 1)
                    for r in range(2):
                        dve.wait_ge(sem("gates_spread"), 2 * j + (64 * half + r + 3))
                        x = hid[:, :, ds(8 * j + 4 * r, 4)]
                        dve.tensor_tensor(x, x, PS[:, 4 + r, 0:4 * EB].rearrange("p (t b) -> p b t", t=4), ALU.mult)\
                            .then_inc(sem("gates_applied"), 1)
                dve.wait_ge(sem("gates_applied"), 64 * (half + 1) + 2)
                rows_bodies(vv, lambda k: one(hid, k))
                add_product(sem("x2_done"))
                dve.wait_ge(sem("x2_done"), half + 1)
            for lo in (16, 64):
                last = dve.tensor_scalar(mod[:, lo:lo + 32], mod[:, lo:lo + 32], 1.0, None, ALU.add)
            last.then_inc(sem("mod_done"), 1)
            dve.wait_ge(sem("rms_root"), 4)
            link(dve.reciprocal(stat[:, 12:14], stat[:, 2:4]))
            dve.wait_ge(sem("row_loaded"), 16)
            for tt in range(TT):
                last = dve.scalar_tensor_tensor(X[:, tt, :], X[:, tt, :], stat[:, 12 + tt:13 + tt], row[:, :],
                                                ALU.mult, ALU.mult)
            last.then_inc(sem("x3_done"), 1)
            dve.wait_ge(sem("mod_done"), 5)
            turned(2, lambda c: mod[:, 16 + c:17 + c], lambda c: mod[:, c:c + 1])

            dve.wait_ge(sem("dt_product"), 1)
            hp = slice(0, SHEADS)
            link(dve.tensor_scalar(dts[:, 4, :], PS[hp, 2, 0:S], pc[hp, PC["dt_bias"]:PC["dt_bias"] + 1], None, ALU.add))
            dve.scalar_tensor_tensor(dts[:, 3, :], dts[:, 4, :], -1.0, dts[:, 4, :], ALU.mult, ALU.min).then_inc(sem("dt_abs"), 1)
            dve.wait_ge(sem("dt_exp"), 2)
            softplus(dts[:, 0, :], dts[:, 4, :], dts[:, 3, :], dts[:, 5, :], dts[:, 6, :], dts[:, 7, :])
            link(dve.tensor_scalar(stat[hp, 13:14], stat[hp, 12:13], -1.0, None, ALU.mult))
            link(dve.tensor_scalar(dts[:, 5, :], dts[:, 0, :], stat[hp, 13:14], None, ALU.mult))
            link(dve.memset(dts[:, 6, :], 1.0))
            link(dve.tensor_tensor_scan(dts[:, 2, :], dts[:, 6, :], dts[:, 5, :], 0.0, ALU.mult, ALU.add))
            dve.tensor_copy(dts[:, 1, :], dts[:, 2, :]).then_inc(sem("decay_done"), 1)

            with dve.Fori(0, NB["xbc"]) as j:
                link.loop(j, 8)
                for u in range(4):
                    low(j + (FIRST_BODY["xbc"] + 1), u)
                    if u % 2 == 1:
                        b = u // 2
                        i = 2 * j + b
                        dve.wait_ge(tile_used, 4 * j + (4 * FIRST_BODY["xbc"] + u + 1))
                        dve.wait_ge(sem("conv_read"), i + 1)
                        convolve(cbuf[:, b, :], PS[:, b, 0:S], lambda t: pc[:, ds(4 * i + (PC["a_conv_w"] + t), 1)], 3)
                        dve.sem_inc(dve_free, 1)
                        dve.sem_inc(sem("conv_done"), 1)
            link.end(NB["xbc"])

            dve.wait_ge(sem("ssd_ready"), 1)
            dve.sem_inc(sem("xd_done"), 1)
            dve.sem_inc(sem("mixed"), 2)
            dve.sem_inc(sem("y_added"), 2)
            with dve.Fori(0, SG) as g:
                dve.wait_ge(sem("xs_turned"), g + 1)
                dve.wait_ge(sem("y_product"), 8 * g + 2)
                for tt in range(TT):
                    dve.tensor_tensor(xd[:, tt, :].rearrange("p (h d) -> p h d", d=64),
                                      PS[:, tt, :].rearrange("p (h d) -> p h d", d=64),
                                      dtn[:, tt, ds(8 * g, 8)].unsqueeze(2).to_broadcast([P, 8, 64]), ALU.mult)\
                        .then_inc(sem("xd_done"), 1)
                dve.wait_ge(sem("cb_done"), g + 2)

                def add(k):
                    c = 4 * g + k // 2
                    dve.wait_ge(sem("y_product"), 8 * g + (k + 4))
                    dve.scalar_tensor_tensor(one(xbc, c), one(xbc, c), pc[:, ds(c + PC["skip"], 1)],
                                             PS[:, 5 + (k // 2) % 2, 0:S], ALU.mult, ALU.add)\
                        .then_inc(sem("y_added"), 1)

                for k in range(8):
                    dve.wait_ge(sem("decays_read"), 8 * g + (k + 3))
                    dve.wait_ge(sem("y_product"), 8 * g + (k + 1))
                    dve.tensor_tensor(mm_[:, k % 2, :], ex[:, k % 2, :], cbm[:, :], ALU.mult).then_inc(sem("mixed"), 1)
                    if k in (3, 5, 7):
                        add(k - 3)
                add(6)
            dve.wait_ge(sem("y_added"), XC + 2)
            dve.sem_inc(sem("y_gated"), 2)
            with dve.Fori(0, NB["z"]) as j:
                for u in range(4):
                    low(j + (FIRST_BODY["z"] + 1), u)
                    if u % 2 == 1:
                        i = 2 * j + u // 2
                        dve.wait_ge(act_free, i + (2 + ACT_BLOCKS["z"] + 1))
                        dve.tensor_tensor(one(xbc, i), one(xbc, i), zt[:, u // 2, :], ALU.mult).then_inc(sem("y_gated"), 1)
            dve.sem_inc(sem("ssd_normed"), 1)
            with dve.Fori(0, SG) as g:
                link.loop(g, 1)
                dve.wait_ge(sem("group_root"), g + 2)
                link(dve.reciprocal(rg[:, 1, :], rg[:, 0, :]))
                for c in range(4):
                    i = 4 * g + c
                    last = dve.scalar_tensor_tensor(one(xbc, i), one(xbc, i), pc[:, ds(i + PC["norm_g"], 1)], rg[:, 1, :],
                                                    ALU.mult, ALU.mult)
                last.then_inc(sem("ssd_normed"), 1)
            link.end(SG)
            dve.wait_ge(sem("ssd_normed"), SG + 1)
            rows_bodies("a_out", lambda k: one(xbc, k))

            def layer_norm(n, signal):
                for tt in range(TT):
                    last = dve.tensor_copy(Y[:, tt, :], banks(4 * tt, 4))
                    if tt == 0:
                        link.post(last)
                last.then_inc(sem("y_copied"), 1)
                dve.wait_ge(sem("y_copied"), n + 1)
                for c in range(KC):
                    if c >= 2:
                        dve.wait_ge(sem("gate_spread"), KC * n + c - 1)
                    dve.tensor_scalar(dcol[:, c % 2, :], ident, mod[:, 48 * n + 32 + c:48 * n + 33 + c], None, ALU.mult)\
                        .then_inc(sem("dcol_done"), 1)
                dve.wait_ge(sem("gate_rows_done"), n + 1)
                for tt in range(TT):
                    link(dve.tensor_tensor(Y[:, tt, :], Y[:, tt, :], rows[:, 0, :], ALU.mult))
                    dve.scalar_tensor_tensor(X[:, tt, :], X[:, tt, :], ALPHA, Y[:, tt, :], ALU.mult, ALU.add)\
                        .then_inc(sem("ln_in"), 1)
                for tt in range(TT):
                    dve.wait_ge(sem("ln_sum"), TT * n + tt + 1)
                    link(dve.tensor_scalar(stat[:, 2 + tt:3 + tt], stat[:, tt:tt + 1], -1.0 / D, None, ALU.mult))
                    dve.wait_ge(sem("ln_in"), TT * n + tt + 1)
                    dve.tensor_scalar(X[:, tt, :], X[:, tt, :], stat[:, 2 + tt:3 + tt], None, ALU.add)\
                        .then_inc(sem("ln_centred"), 1)
                dve.wait_ge(sem("ln_root"), n + 1)
                link(dve.reciprocal(stat[:, 8:10], stat[:, 6:8]))
                dve.wait_ge(sem("ln_rows_loaded"), 32 * (n + 1))
                for tt in range(TT):
                    dve.wait_ge(sem("ln_centred"), TT * n + tt + 1)
                    link(dve.scalar_tensor_tensor(X[:, tt, :], X[:, tt, :], stat[:, 8 + tt:9 + tt], rows[:, 1, :],
                                                  ALU.mult, ALU.mult))
                    last = dve.tensor_tensor(X[:, tt, :], X[:, tt, :], rows[:, 2, :], ALU.add)
                    if tt == 0:
                        link.post(last)
                last.then_inc(signal, 1)

            layer_norm(0, sem("x4_done"))
            turned(3, lambda c: 1.0)
            bodies("k2")
            bodies("v2")
            turned(4, lambda c: mod[:, 64 + c:65 + c], lambda c: mod[:, 48 + c:49 + c])
            bodies("q2")
            bodies("z2")

            dve.wait_ge(sem("distances_loaded"), 16)
            dve.wait_ge(sem("z2_out"), 1)
            dve.sem_inc(sem("dist_added"), 1)
            dve.sem_inc(sem("head_out"), 1)
            with dve.Fori(0, DH) as h:
                link.loop(h, 9)
                dve.wait_ge(sem("head_scored"), h + 2)
                dve.wait_ge(sem("head_out"), h + 1)
                for g in range(DG):
                    slope = cd[:, ds(3 * h + (CD["slopes"] + g), 1)]
                    link.post(dve.scalar_tensor_tensor(sc2[:, g * P:(g + 1) * P], cd[:, CD["d0"] + g * P:CD["d0"] + (g + 1) * P],
                                                       slope, PS[:, 0, g * P:(g + 1) * P], ALU.mult, ALU.add))
                for g in range(DG):
                    slope = cd[:, ds(3 * h + (CD["slopes"] + g), 1)]
                    o = 384 + g * S
                    last = dve.scalar_tensor_tensor(sc2[:, o:o + S], cd[:, CD["d1"] + g * S:CD["d1"] + (g + 1) * S],
                                                    slope, PS[:, 1 + g // 2, (g % 2) * S:(g % 2 + 1) * S],
                                                    ALU.mult, ALU.add)
                    if g < DG - 1:
                        link.post(last)
                last.then_inc(sem("dist_added"), 1)
                dve.wait_ge(sem("dist_added"), h + 2)
                link.post(dve.tensor_reduce(sm2[:, 0:1], sc2[:, 0:384], AX.X, ALU.max))
                link(dve.tensor_reduce(sm2[:, 1:2], sc2[:, 384:1152], AX.X, ALU.max))
                dve.tensor_scalar(sm2[:, 2:4], sm2[:, 0:2], -1.0, None, ALU.mult).then_inc(sem("head_max"), 1)
                dve.wait_ge(sem("head_exp"), h + 1)
                link(dve.reciprocal(sm2[:, 6:8], sm2[:, 4:6]))
                dve.wait_ge(sem("head_product"), h + 1)
                for tt in range(TT):
                    z = zn[:, tt, ds(h * P, P)]
                    last = dve.scalar_tensor_tensor(z, PS[:, 6 + tt, 0:P], sm2[:, 6 + tt:7 + tt], z, ALU.mult, ALU.mult)
                    if tt == 0:
                        link.post(last)
                last.then_inc(sem("head_out"), 1)
            link.end(DH)
            dve.wait_ge(sem("oT_done"), 1)
            rows_bodies("b_out", lambda k: one(oT, k))
            layer_norm(1, sem("out_ready"))


def lay_out(i):
    f = np.float32
    c = np.ascontiguousarray

    def columns(v):
        return v.reshape(-1, P).T

    def blocks(w):
        n = w.shape[1] // P
        return c(w.reshape(2, 8, P, n, P).transpose(3, 0, 2, 1, 4)).reshape(2 * n, P, TILE)

    w_in = i["w_in"][0]
    q_end, kv_end = QC, QC + KVC
    a_in = i["a_in_w_2"][0]
    o = {}
    o["x"] = c(i["x"].reshape(TT, P, D).transpose(1, 0, 2))
    o["q"] = c(w_in[:, :q_end]).reshape(KC, P, TILE)
    o["kv"] = c(w_in[:, q_end:kv_end].reshape(8, 2, P, 512).transpose(0, 2, 1, 3)).reshape(8, P, TILE)
    o["gate"] = blocks(w_in[:, kv_end:kv_end + LRU])
    o["rec"] = blocks(w_in[:, kv_end + LRU:])
    o["w_out"] = c(i["w_out"][0]).reshape(KC, P, D)
    o["w_pq"] = blocks(i["w_pq"][0])
    u = i["u_emb"][0].reshape(NK, NK, 2, 8, P)
    o["u_emb"] = c(u.transpose(1, 2, 4, 3, 0)).reshape(2 * NK, P, TILE)
    v = i["v_emb"][0].reshape(NK, NK, 2, TILE)
    o["v_emb"] = c(v.transpose(1, 2, 0, 3)).reshape(2 * NK, P, TILE)
    o["xbc"] = blocks(a_in[:, DI:DI + BC * P])
    o["z"] = blocks(a_in[:, :DI])
    o["w_dt"] = c(a_in[:, DI + BC * P:].reshape(KC, P, SHEADS).transpose(1, 0, 2))
    o["a_out"] = c(i["a_out_w_2"][0]).reshape(XC, P, D)
    kv = i["kv_w_2"]
    W = DG * DH * P
    o["k2"] = blocks(kv[:, :W])
    o["v2"] = c(kv[:, W:].reshape(KC, P, DG, TILE).transpose(2, 0, 1, 3)).reshape(DG * KC, P, TILE)
    b_in = i["b_in_w_2"][0]
    o["q2"] = blocks(b_in[:, :W])
    o["z2"] = c(b_in[:, W:]).reshape(KC, P, TILE)
    o["b_out"] = c(i["b_out_w_2"][0]).reshape(DH, P, D)
    ada = i["ada_w_2"].reshape(2, KC, P, 2, 3, TILE)
    o["ada_w"] = c(ada.transpose(0, 3, 1, 4, 2, 5)).reshape(-1, P, TILE)
    o["gate_w"] = c(np.stack([i[n][0].reshape(LC, 2, 64, 64).transpose(1, 2, 0, 3)
                              for n in ("fwd_wa", "fwd_wx", "bwd_wa", "bwd_wx")]))
    sk = np.stack([i["sub_k1"][0], i["sub_k2"][0]], 1)
    o["skT"] = c(sk.reshape(2 * PH, NK, P).transpose(2, 0, 1))
    o["sink"] = c(i["sink"][0].reshape(NKV, 2, 2).transpose(0, 2, 1)).reshape(NQ)
    o["rows"] = c(np.stack([i["g_final"], i["ln_g_2"][0], i["ln_b_2"][0], i["ln_g_2"][1], i["ln_b_2"][1]]))

    pc = np.zeros((P, PC.n), f)

    def put(name, v):
        pc[:v.shape[0], PC[name]:PC[name] + v.shape[1]] = v

    put("g_mix", columns(i["g_mix"][0]))
    put("g_ffn", columns(i["g_ffn"][0]))
    put("g_attn", columns(i["g_attn_out"][0]))
    put("g_lru", columns(i["g_lru_out"][0]))
    put("conv_w", i["conv_w"][0].reshape(4, LC, P).transpose(2, 1, 0).reshape(P, -1))
    put("conv_b", columns(i["conv_b"][0]))
    put("gate_b", np.concatenate([columns(i[n][0]) for n in ("fwd_ba", "fwd_bx", "bwd_ba", "bwd_bx")], 1))
    put("lam", np.concatenate([columns(i[n][0]) for n in ("fwd_lam", "bwd_lam")], 1))
    put("ada_b", columns(i["ada_b_2"].reshape(-1)))
    put("cond", columns(i["c_2"][0]))
    put("a_conv_w", i["a_conv_w_2"][0].reshape(4, BC, P).transpose(2, 1, 0).reshape(P, -1))
    put("a_conv_b", columns(i["a_conv_b_2"][0]))
    put("norm_g", columns(i["a_norm_g_2"][0]))
    put("skip", columns(np.repeat(i["a_D_2"][0], 64)))
    put("dt_bias", i["a_dt_bias_2"][0][:, None])
    put("a_log", i["a_A_log_2"][0][:, None])
    for name, value in (("eps", EPS), ("ln_eps", LN_EPS), ("tiny", 1e-30)):
        pc[:, PC[name]] = value
    o["pc"] = pc

    cc = np.zeros((P, CC.n), f)
    cc[:, CC["ident"]:CC["ident"] + P] = np.eye(P)
    cc[:, CC["ones"]:CC["ones"] + P] = 1
    cc[:, CC["iota"]:CC["iota"] + P] = np.arange(P)
    cc[:, CC["iota16"]:CC["iota16"] + TOPK] = np.arange(TOPK)
    o["cc"] = cc
    half = HD // 2
    inv = (f(10000.0) ** (-np.arange(half, dtype=f) / f(half))).astype(f)
    ang = (np.arange(S, dtype=f)[:, None] * inv[None]).astype(f)
    pos = np.arange(S)
    cw = np.zeros((P, CW.n), f)
    window = np.where(np.abs(pos[None] - pos[:, None]) <= 128, 0, NEG).astype(f)
    for name, t in (("cos", np.cos(ang)), ("sin", np.sin(ang)), ("window", window)):
        w = t.shape[1] * TT
        cw[:, CW[name]:CW[name] + w] = t.reshape(TT, P, -1).transpose(1, 0, 2).reshape(P, -1)
    o["cw"] = cw
    o["causal"] = np.where(pos[None, :P] >= pos[:P, None], 0, NEG).astype(f)
    far = pos[:, None] - pos[None]
    cd = np.zeros((P, CD.n), f)
    for g, (window, step) in enumerate(((128, 1), (512, 4), (2048, 16))):
        d = np.where((far >= 0) & (far <= window) & (far % step == 0), far, -NEG).astype(f)
        cd[:, CD["d0"] + g * P:CD["d0"] + (g + 1) * P] = d[:P, :P]
        cd[:, CD["d1"] + g * S:CD["d1"] + (g + 1) * S] = d[P:, :]
    n = DG * DH
    slopes = (2.0 ** (-8.0 * np.arange(1, n + 1) / n)).reshape(DG, DH).T.reshape(-1)
    cd[:, CD["slopes"]:CD["slopes"] + n] = -slopes.astype(f)
    o["cd"] = cd
    return o


def kernel(**inputs):
    import concourse.bacc as bacc
    from concourse.bass_utils import run_bass_kernel_spmd

    arrays = lay_out({k: np.asarray(v) for k, v in inputs.items()})
    nc = bacc.Bacc("TRN2", target_bir_lowering=False, num_devices=1)
    aps = {k: nc.dram_tensor(f"in_{k}", v.shape, F32, kind="ExternalInput").ap() for k, v in arrays.items()}
    out = nc.dram_tensor("out", (P, TT, D), F32, kind="ExternalOutput").ap()
    build(nc, aps, out)
    got = run_bass_kernel_spmd(nc, [{f"in_{k}": v for k, v in arrays.items()}], core_ids=[0])
    y = got.results[0]["out"]
    return np.ascontiguousarray(y.transpose(1, 0, 2)).reshape(1, S, D)
```

```python
from contextlib import ExitStack

import numpy as np

import concourse.bass as bass
from concourse import mybir

ALU = mybir.AluOpType
ACT = mybir.ActivationFunctionType
AX = mybir.AxisListType
F32 = mybir.dt.float32
F32R = mybir.dt.float32r
BF16 = mybir.dt.bfloat16
U32 = mybir.dt.uint32
ds = bass.ds

P = 128
S = 256
TT = S // P
D = 2048
KC = D // P
TILE = 1024
EPS = 1e-6
LN_EPS = 1e-5
ALPHA = 4.0 ** 0.25

NQ, HD, NKV = 16, 64, 4
QC = NQ * HD
KVC = 2 * NKV * HD
LRU = 1024
LC = LRU // P
PH = 8
NK = 128
TOPK = 16
QUARTERS = 4
EB = NK // QUARTERS
ADA = 512
DI = 4096
SG, SN, SHEADS = 8, 128, 64
XC = DI // P
BC = XC + 2 * SG
DG, DH = 3, 8

NEG = -1e30


class Columns:

    def __init__(self):
        self.at, self.n = {}, 0

    def add(self, name, width):
        self.at[name] = self.n
        self.n += width

    def __getitem__(self, name):
        return self.at[name]


PC = Columns()
for _name, _w in [
    ("g_mix", KC), ("g_ffn", KC), ("g_attn", LC), ("g_lru", LC),
    ("conv_w", 4 * LC), ("conv_b", LC), ("gate_b", 4 * LC), ("lam", 2 * LC),
    ("ada_b", 96), ("cond", KC), ("a_conv_w", 4 * BC), ("a_conv_b", BC),
    ("norm_g", XC), ("skip", XC), ("dt_bias", 1), ("a_log", 1),
    ("eps", 1), ("ln_eps", 1), ("tiny", 1),
]:
    PC.add(_name, _w)
CC = Columns()
for _name, _w in [("ident", P), ("ones", P), ("iota", P), ("iota16", TOPK)]:
    CC.add(_name, _w)
CW = Columns()
for _name, _w in [("cos", TT * 32), ("sin", TT * 32), ("window", TT * S)]:
    CW.add(_name, _w)
CD = Columns()
for _name, _w in [("d0", DG * P), ("d1", DG * S), ("slopes", DG * DH)]:
    CD.add(_name, _w)

STREAM = [
    ("q", 4), ("kv", 2), ("gate", 4), ("rec", 4), ("w_out", 8), ("w_pq", 8),
    ("up0", 16), ("down0", 16), ("up1", 16), ("down1", 16),
    ("up2", 16), ("down2", 16), ("up3", 16), ("down3", 16),
    ("xbc", 24), ("z", 16), ("a_out", 16), ("k2", 12), ("v2", 12), ("q2", 12), ("z2", 4), ("b_out", 4),
]
FIRST_BODY = {}
BODIES = 0
for _name, _n in STREAM:
    FIRST_BODY[_name] = BODIES
    BODIES += _n
NB = dict(STREAM)


class Chain:

    def __init__(self, eng, sem):
        self.eng, self.sem, self.n = eng, sem, 0
        self.offset = None

    def __call__(self, instruction):
        self.post(instruction)
        self.wait()

    def post(self, instruction):
        instruction.then_inc(self.sem, 1)
        self.n += 1

    def wait(self, back=0):
        n = self.n - back
        self.eng.wait_ge(self.sem, n if self.offset is None else self.offset + n)

    def loop(self, j, per):
        self.start, self.per = self.n, per
        self.offset = j * per

    def end(self, trips):
        assert self.n - self.start == self.per, (self.n - self.start, self.per)
        self.n = self.start + self.per * trips
        self.offset = None


def build(nc, a, out):
    ctx = ExitStack()
    with ctx:
        def psum(name, shape, dt=F32):
            return ctx.enter_context(nc.psum_tensor(name, shape, dt))

        def sb(name, shape, dt=F32, group=None):
            return (group or ctx).enter_context(nc.sbuf_tensor(name, shape, dt))

        names = {}

        def sem(name):
            if name not in names:
                names[name] = ctx.enter_context(nc.semaphore(name))
            return names[name]

        PS = psum("PS", [P, 8, 512])

        X = sb("X", [P, TT, D])
        xt_hi = sb("xt_hi", [P, KC, S], F32R)
        xt_lo = sb("xt_lo", [P, KC, S], F32R)
        raw = sb("raw", [P, 4, TILE])
        w_hi = sb("w_hi", [P, 4, TILE], F32R)
        w_lo = sb("w_lo", [P, 4, TILE], F32R)
        st_hi = sb("st_hi", [P, 2, S], F32R)
        st_lo = sb("st_lo", [P, 2, S], F32R)
        cc = sb("cc", [P, CC.n])
        pc = sb("pc", [P, PC.n])
        diag = sb("diag", [P, TT, P])
        xtmp = sb("xtmp", [P, 2, S])
        stat = sb("stat", [P, 16])
        silu_c = sb("silu_c", [P, KC])
        mod = sb("mod", [P, 96])
        ident = cc[:, CC["ident"]:CC["ident"] + P]
        ones = cc[:, CC["ones"]:CC["ones"] + P]

        mixer = ExitStack()
        yT = sb("yT", [P, KC, S], F32, mixer)
        gateT = sb("gateT", [P, LC, S], F32, mixer)
        convT = sb("convT", [P, LC, S], F32, mixer)
        attn = ExitStack()
        cw = sb("cw", [P, CW.n], F32, attn)
        qn = sb("qn", [P, TT, QC], F32, attn)
        kvn = sb("kvn", [P, TT, KVC], F32, attn)
        kdup = sb("kdup", [P, TT, NKV, 2, HD], F32, attn)
        qT = sb("qT", [P, QC // P, S], F32, attn)
        kT = sb("kT", [P, NKV, S], F32, attn)
        sc = sb("sc", [P, 2, 4, S], F32, attn)
        pr = sb("pr", [P, 4, S], F32, attn)
        pT = sb("pT", [P, 8, P], F32, attn)
        yn = sb("yn", [P, TT, QC], F32, attn)
        rtmp = sc
        sinkb = sb("sinkb", [P, NQ], F32, attn)
        sm = sb("sm", [P, 8, 2, 4], F32, attn)
        attn.close()
        lru = ExitStack()
        wbd = sb("wbd", [P, 4, LC, P], F32, lru)
        rr = sb("rr", [P, LC, S], F32, lru)
        ii = sb("ii", [P, LC, S], F32, lru)
        aa = sb("aa", [P, LC, S], F32, lru)
        hh = sb("hh", [P, 2, LC, S], F32, lru)
        spl = sb("spl", [P, 8, 2 * LC], F32, lru)
        rstdb = sb("rstdb", [P, 2, S], F32, lru)
        lru.close()
        mixer.close()

        peer = ExitStack()
        slotsT = sb("slotsT", [P, 2, S], F32, peer)
        slot_gate = sb("slot_gate", [P, 2, S], F32R, peer)
        hid0 = sb("hid0", [P, EB, S], F32, peer)
        route = ExitStack()
        pqT = sb("pqT", [P, 2 * PH, S], F32, route)
        score = sb("score", [P, TT * 2 * PH, NK], F32, route)
        topv = sb("topv", [P, TT * 2 * PH, TOPK], F32, route)
        topi = sb("topi", [P, TT * 2 * PH, TOPK], U32, route)
        topf = sb("topf", [P, TT * 2 * PH, TOPK], F32, route)
        cand = sb("cand", [P, TT * PH, TOPK, TOPK], F32, route)
        skT = cand[:, 0:PH, :, :].rearrange("p g x y -> p (g x y)").rearrange("p (i n) -> p i n", n=NK)
        pick = sb("pick", [P, TT * PH, TOPK], F32, route)
        seli = sb("seli", [P, TT * PH, TOPK], U32, route)
        selh = sb("selh", [P, 2, TT * PH, TOPK], U32, route)
        self_ = sb("self_", [P, 2, TT * PH, TOPK], F32, route)
        slots = sb("slots", [P, 3, TT * PH, TOPK], F32, route)
        rsum = sb("rsum", [P, TT * PH], F32, route)
        route.close()
        experts = ExitStack()
        hid1 = sb("hid1", [P, EB, S], F32, experts)
        hid = [hid0, hid1]
        hot1 = sb("hot1", [P, 2, 8, NK], F32R, experts)
        hot2, hot2_gate = {}, {}
        hot2[EB] = sb("hot2_one", [P, 2, 8, EB], F32, experts)
        hot2_gate[EB] = sb("hot2_gate_one", [P, 2, 2, 8, EB], F32R, experts)
        ada = sb("ada", [P, 3, ADA], F32, experts)
        two_quarters = ExitStack()
        hot2[2 * EB] = sb("hot2_two", [P, 2, 8, 2 * EB], F32, two_quarters)
        hot2_gate[2 * EB] = sb("hot2_gate_two", [P, 2, 2, 8, 2 * EB], F32R, two_quarters)
        two_quarters.close()
        ada_acc = sb("ada_acc", [P, 2, 3, ADA], F32, experts)
        geluT = xtmp
        experts.close()
        final = ExitStack()
        row = sb("row", [P, D], F32, final)
        final.close()
        peer.close()

        ssd = ExitStack()
        xbc = sb("xbc", [P, BC, S], F32, ssd)
        cbuf = sb("cbuf", [P, 2, S], F32, ssd)
        w_dt = sb("w_dt", [P, KC, SHEADS], F32, ssd)
        causal = sb("causal", [P, P], F32, ssd)
        causal_b = sb("causal_b", [P, P], BF16, ssd)
        ident_b = sb("ident_b", [P, P], BF16, ssd)
        dts = sb("dts", [SHEADS, 8, S], F32, ssd)
        dtn = sb("dtn", [P, TT, SHEADS], F32, ssd)
        nacn = sb("nacn", [P, TT, SHEADS], F32, ssd)
        xs_st = sb("xs_st", [P, 4, S], F32, ssd)
        b_st = sb("b_st", [P, S], F32, ssd)
        pick_h = sb("pick_h", [SHEADS, 8, P], F32, ssd)
        xd = sb("xd", [P, TT, 512], F32, ssd)
        cbm = sb("cbm", [P, 384], F32, ssd)
        ex = sb("ex", [P, 2, 384], F32, ssd)
        ada_z = sb("ada_z", [P, 3, ADA], F32, ssd)
        ada_acc_z = sb("ada_acc_z", [P, 3, ADA], F32, ssd)
        mm_ = sb("mm_", [P, 2, 384], F32, ssd)
        zt = sb("zt", [P, 2, S], F32, ssd)
        sq = xs_st
        rg = sb("rg", [P, 2, S], F32, ssd)
        ssd.close()
        norms = ExitStack()
        Y = sb("Y", [P, TT, D], F32, norms)
        rows = sb("rows", [P, 3, D], F32, norms)
        dcol = sb("dcol", [P, 2, P], F32, norms)
        norms.close()
        dil = ExitStack()
        k2T = sb("k2T", [P, DG * DH, S], F32, dil)
        v2n = sb("v2n", [P, TT, DG * DH * P], F32, dil)
        q2T = sb("q2T", [P, DG * DH, S], F32, dil)
        zn = sb("zn", [P, TT, DH * P], F32, dil)
        cd = sb("cd", [P, CD.n], F32, dil)
        q_st = sb("q_st", [P, DG, S], F32, dil)
        sc2 = sb("sc2", [P, 9 * P], F32, dil)
        pT2 = sb("pT2", [P, 9, P], F32, dil)
        sm2 = sb("sm2", [P, 8], F32, dil)
        dil.close()
        oT = k2T

        raw_loaded = [sem(f"raw_loaded{u}") for u in range(4)]
        hi_done, lo_done, tile_used = sem("hi_done"), sem("lo_done"), sem("tile_used")
        stage_hi_done, stage_lo_done = sem("stage_hi_done"), sem("stage_lo_done")
        consts_loaded, x_loaded, params_loaded = sem("consts_loaded"), sem("x_loaded"), sem("params_loaded")
        xt_turned, xt_hi_done, xt_lo_done = sem("xt_turned"), sem("xt_hi_done"), sem("xt_lo_done")
        act_free, dve_free = sem("act_free"), sem("dve_free")
        ACT_BLOCKS = {"gate": 0, "w_pq": 8, "up0": 24, "up1": 56, "up2": 88, "up3": 120, "z": 152, "k2": 184, "q2": 208}
        DVE_BLOCKS = {"rec": 0, "xbc": 8}
        CHUNKS = {"w_out": 0, "down0": 16, "down1": 48, "down2": 80, "down3": 112, "a_out": 144, "b_out": 176}
        z_bank = (7, 2)
        dve_link, act_link = sem("dve_link"), sem("act_link")

        block = ctx.enter_context(nc.Block())

        def one(tensor, i):
            return tensor[:, ds(i, 1), :].rearrange("p a s -> p (a s)")

        def tile_source(name, j, u):
            if name in ("w_out", "a_out", "b_out"):
                return a[name][2 * j + u // 2][:, (u % 2) * TILE:(u % 2 + 1) * TILE]
            if name[:-1] in ("up", "down"):
                return a[("u" if name[:-1] == "up" else "v") + "_emb"][4 * j + (2 * EB * int(name[-1]) + u)]
            return a[name][4 * j + u]

        @block.sync
        def _(sp):
            sp.dma_start(X[:, :, :], a["x"]).then_inc(x_loaded, 16)
            sp.dma_start(cc[:, :], a["cc"]).then_inc(consts_loaded, 16)
            sp.dma_start(pc[:, :], a["pc"]).then_inc(params_loaded, 16)

            def weight(name, j, u):
                first = name == STREAM[0][0] and type(j) is int
                if not first:
                    sp.wait_ge(lo_done, 4 * (j + FIRST_BODY[name]) + u - 3)
                sp.dma_start(raw[:, u, :], tile_source(name, j, u)).then_inc(raw_loaded[u], 16)

            for name, n in STREAM:
                start = 0
                if name == STREAM[0][0]:
                    for u in range(4):
                        weight(name, 0, u)
                    start = 1
                with sp.Fori(start, n) as j:
                    for u in range(4):
                        weight(name, j, u)
            sp.wait_ge(sem("out_ready"), 1)
            sp.dma_start(out, X[:, :, :]).then_inc(sem("stored"), 16)
            sp.wait_ge(sem("stored"), 16)

        @block.gpsimd
        def _(pool):
            pool.dma_start(cw[:, :], a["cw"]).then_inc(sem("window_loaded"), 16)
            pool.dma_start(sinkb[:, :], a["sink"].partition_broadcast(P)).then_inc(sem("window_loaded"), 16)
            pool.wait_ge(sem("y_attn_done"), 1)
            pool.memset(wbd[:, :, :, :], 0.0).then_inc(sem("bd_zero"), 1)
            pool.wait_ge(sem("bd_zero"), 1)
            for kind in range(4):
                for half in range(2):
                    pool.dma_start(wbd[64 * half:64 * half + 64, kind, :, 64 * half:64 * half + 64],
                                   a["gate_w"][kind, half]).then_inc(sem("bd_loaded"), 16)
            pool.wait_ge(sem("x1_done"), 1)
            pool.dma_start(skT, a["skT"]).then_inc(sem("keys_loaded"), 16)
            def low(body, u):
                pool.wait_ge(hi_done, 4 * body + u + 1)
                pool.tensor_tensor(w_lo[:, u, :], raw[:, u, :], w_hi[:, u, :].bitcast(F32), ALU.subtract)\
                    .then_inc(lo_done, 1)

            def lows(name):
                pool.wait_ge(lo_done, 4 * (FIRST_BODY[name] + 1))
                with pool.Fori(0, NB[name]) as j:
                    for u in range(4):
                        low(j + (FIRST_BODY[name] + 1), u)

            lows("up0")
            pool.wait_ge(sem("route_over"), 2)

            def slot_gates(n, n_before, width, r):
                shape = [P, 2, 8, width]
                pool.wait_ge(sem("keys_matched"), n + (n_before + 1))
                pool.tensor_tensor(hot2_gate[width][:, r, :, :, 0:width],
                                   hot2[width][:, r, :, 0:width].unsqueeze(1).to_broadcast(shape),
                                   slot_gate[:, :, ds(8 * n, 8)].bitcast(F32).unsqueeze(3).to_broadcast(shape),
                                   ALU.mult).then_inc(sem("hot2_done"), 1)

            def ada_tiles(seg, k, buffer):
                for q in range(3):
                    pool.wait_ge(sem("ada_used"), 3 * k + (48 * seg + q + 1))
                    pool.dma_start(buffer[:, q, :], a["ada_w"][3 * k + (48 * seg + q)])\
                        .then_inc(sem(f"ada_loaded{q}"), 16)

            with pool.Fori(0, 16) as j:
                for r in range(2):
                    slot_gates(2 * j + r, 0, 2 * EB, r)
            for quarter in range(QUARTERS):
                if quarter:
                    with pool.Fori(0, 16) as k:
                        ada_tiles(2 * quarter - 1, k, ada)
                        if quarter < QUARTERS - 1:
                            for r in range(2):
                                slot_gates(2 * k + r, 32 * quarter, EB, r)
                with pool.Fori(0, 16) as k:
                    ada_tiles(2 * quarter, k, ada)
            pool.wait_ge(sem("x2_done"), QUARTERS)
            pool.dma_start(row[:, :], a["rows"][0].partition_broadcast(P)).then_inc(sem("row_loaded"), 16)
            pool.wait_ge(sem("x3_done"), 1)
            pool.dma_start(w_dt[:, :, :], a["w_dt"]).then_inc(sem("w_dt_loaded"), 16)
            pool.dma_start(causal[:, :], a["causal"]).then_inc(sem("w_dt_loaded"), 16)
            lows("xbc")
            pool.wait_ge(sem("ssd_ready"), 1)
            with pool.Fori(0, SG) as g:
                pool.wait_ge(sem("xs_turned"), g + 1)
                pool.tensor_copy(xs_st[:, :, :], xbc[:, ds(4 * g, 4), :]).then_inc(sem("xs_staged"), 1)
                pool.wait_ge(sem("cb_product"), g + 1)
                pool.tensor_copy(b_st[:, :], one(xbc, g + XC)).then_inc(sem("b_staged"), 1)
                pool.wait_ge(sem("group_done"), g + 1)
                pool.tensor_copy(pick_h[:, :, :], cc[0:SHEADS, ds(8 * g + CC["ident"], 8)].unsqueeze(2)
                                 .to_broadcast([SHEADS, 8, P])).then_inc(sem("heads_staged"), 1)
                for i in range(2):
                    ada_tiles(7, 2 * g + i, ada_z)
            pool.wait_ge(sem("y_copied"), 1)
            for r in range(2):
                pool.dma_start(rows[:, 1 + r, :], a["rows"][1 + r].partition_broadcast(P))\
                    .then_inc(sem("ln_rows_loaded"), 16)
            pool.wait_ge(sem("x4_done"), 1)
            pool.dma_start(cd[:, :], a["cd"]).then_inc(sem("distances_loaded"), 16)
            pool.wait_ge(act_free, 2 + ACT_BLOCKS["q2"] + 24)
            with pool.Fori(0, DH) as h:
                pool.wait_ge(sem("head_scored"), h + 1)
                pool.tensor_copy(q_st[:, :, :],
                                 q2T[:, :, :].rearrange("p (g h) s -> p g h s", g=DG)[:, :, ds(h, 1), :]
                                 .rearrange("p g o s -> p g (o s)")).then_inc(sem("q_staged"), 1)
            pool.wait_ge(sem("y_copied"), 2)
            for r in range(2):
                pool.dma_start(rows[:, 1 + r, :], a["rows"][3 + r].partition_broadcast(P))\
                    .then_inc(sem("ln_rows_loaded"), 16)

        @block.tensor
        def _(pe):
            def three(o, w_h, w_l, x_h, x_l, start, stop):
                pe.matmul(o, w_h, x_h, start=start, stop=False, skip_group_check=True)
                pe.matmul(o, w_h, x_l, start=False, stop=False, skip_group_check=True)
                return pe.matmul(o, w_l, x_h, start=False, stop=stop, skip_group_check=True)

            def block_product(name, j, b, o):
                for h in range(2):
                    u = 2 * b + h
                    pe.wait_ge(lo_done, 4 * j + (4 * FIRST_BODY[name] + u + 1))
                    for k in range(8):
                        w = slice(k * P, k * P + P)
                        last = three(o, w_hi[:, u, w], w_lo[:, u, w], xt_hi[:, 8 * h + k, :], xt_lo[:, 8 * h + k, :],
                                     h == 0 and k == 0, h == 1 and k == 7)
                    last.then_inc(tile_used, 1)

            def channel_blocks(name, free, before):
                with pe.Fori(0, NB[name]) as j:
                    for b in range(2):
                        pe.wait_ge(free, 2 * j + before + b + 1)
                        block_product(name, j, b, PS[:, b, 0:S])

            def token_columns(tiles, body0, bank0, kpt):
                n = 16 // kpt
                for i in range(n):
                    pe.wait_ge(lo_done, tiles + (body0 * 4 + i + 1))
                    for kk in range(kpt):
                        k = i * kpt + kk
                        for tt in range(TT):
                            for g in range(2 // kpt):
                                c = (kk if kpt == 2 else g) * 512
                                o = PS[:, bank0 + tt * (2 // kpt) + g, :]
                                t = slice(tt * P, tt * P + P)
                                u = i % 4
                                pe.matmul(o, xt_hi[:, k, t], w_hi[:, u, c:c + 512], start=k == 0, stop=False)
                                pe.matmul(o, xt_lo[:, k, t], w_hi[:, u, c:c + 512], start=False, stop=False)
                                last = pe.matmul(o, xt_hi[:, k, t], w_lo[:, u, c:c + 512],
                                                 start=False, stop=k == KC - 1)
                    last.then_inc(tile_used, 1)

            def rows_body(name, j, first, stop):
                for u in range(4):
                    pe.wait_ge(lo_done, 4 * (j + FIRST_BODY[name]) + u + 1)
                    s = u // 2
                    if u % 2 == 0:
                        pe.wait_ge(stage_lo_done, 2 * j + CHUNKS[name] + s + 1)
                    for tt in range(TT):
                        for g in range(2):
                            o = PS[:, tt * 4 + (u % 2) * 2 + g, :]
                            t, c = slice(tt * P, tt * P + P), slice(g * 512, g * 512 + 512)
                            pe.matmul(o, st_hi[:, s, t], w_hi[:, u, c], start=first and s == 0, stop=False,
                                      skip_group_check=True)
                            pe.matmul(o, st_lo[:, s, t], w_hi[:, u, c], start=False, stop=False,
                                      skip_group_check=True)
                            last = pe.matmul(o, st_hi[:, s, t], w_lo[:, u, c], start=False, stop=stop and s == 1,
                                             skip_group_check=True)
                    last.then_inc(tile_used, 1)

            def all_rows(name):
                rows_body(name, 0, True, False)
                if NB[name] > 2:
                    with pe.Fori(1, NB[name] - 1) as j:
                        rows_body(name, j, False, False)
                rows_body(name, NB[name] - 1, False, True)

            def turn(n, by):
                for c in range(KC):
                    if c >= 8:
                        pe.wait_ge(xt_lo_done, KC * n + c - 7)
                    for tt in range(TT):
                        last = pe.matmul(PS[:, c % 8, tt * P:tt * P + P], X[:, tt, c * P:c * P + P], by(tt),
                                         start=True, stop=True)
                    last.then_inc(xt_turned, 1)

            pe.wait_ge(consts_loaded, 16)
            pe.wait_ge(x_loaded, 16)
            pe.wait_ge(sem("diag_done"), 1)
            turn(0, lambda tt: diag[:, tt, :])
            pe.wait_ge(xt_lo_done, KC)
            token_columns(0, FIRST_BODY["q"], 0, 1)
            token_columns(0, FIRST_BODY["kv"], 4, 2)
            pe.wait_ge(sem("qkv_out"), 2)
            channel_blocks("gate", act_free, ACT_BLOCKS["gate"])
            pe.wait_ge(act_free, 2 + ACT_BLOCKS["gate"] + 8)
            channel_blocks("rec", dve_free, DVE_BLOCKS["rec"])

            pe.wait_ge(dve_free, 2 + DVE_BLOCKS["rec"] + 8)
            pe.wait_ge(sem("rope_done"), 1)
            for tt in range(TT):
                for c in range(QC // P):
                    pe.transpose(PS[:, c // 2, (c % 2) * S + tt * P:(c % 2) * S + tt * P + P],
                                 qn[:, tt, c * P:c * P + P], ident)
                for g in range(NKV):
                    last = pe.transpose(PS[:, 4 + g // 2, (g % 2) * S + tt * P:(g % 2) * S + tt * P + P],
                                        kdup[:, tt, g, :, :].rearrange("p a d -> p (a d)"), ident)
            last.then_inc(sem("qk_turned"), 1)

            steps = [(tt, g) for tt in range(TT) for g in range(NKV)]

            def scores(n):
                tt, g = steps[n]
                if n >= 2:
                    pe.wait_ge(sem("scores_read"), n - 1)
                for i in range(2):
                    for par in range(2):
                        h = slice(64 * par, 64 * par + 64)
                        last = pe.matmul(PS[:, 2 * (n % 2) + par, i * S:i * S + S],
                                         qT[h, 2 * g + i, tt * P:tt * P + P], kT[h, g, :], start=True, stop=True)
                last.then_inc(sem("scores_done"), 1)

            pe.wait_ge(sem("qkT_done"), 2)
            scores(0)
            for n, (tt, g) in enumerate(steps):
                if n + 1 < len(steps):
                    scores(n + 1)
                pe.wait_ge(sem("probs_done"), n + 1)
                if n:
                    pe.wait_ge(sem("pT_done"), n)
                for i in range(4):
                    for kc in range(2):
                        last = pe.transpose(PS[:, 4 + i // 2, ((i % 2) * 2 + kc) * P:((i % 2) * 2 + kc + 1) * P],
                                            pr[:, i, kc * P:kc * P + P], ident)
                last.then_inc(sem("p_turned"), 1)
                pe.wait_ge(sem("pT_done"), n + 1)
                if n:
                    pe.wait_ge(sem("attn_out"), n)
                for i in range(4):
                    for kc in range(2):
                        last = pe.matmul(PS[:, 6, i * HD:i * HD + HD], pT[:, 2 * i + kc, :],
                                         kvn[:, kc, NKV * HD + g * HD:NKV * HD + g * HD + HD],
                                         start=kc == 0, stop=kc == 1, skip_group_check=True)
                last.then_inc(sem("pv_done"), 1)
            pe.wait_ge(sem("diag_done"), 2)
            for c in range(LC):
                for tt in range(TT):
                    last = pe.matmul(PS[:, c // 2, (c % 2) * S + tt * P:(c % 2) * S + tt * P + P],
                                     yn[:, tt, c * P:c * P + P], diag[:, tt, :], start=True, stop=True)
            last.then_inc(sem("y_turned"), 1)

            pe.wait_ge(sem("bd_loaded"), 128)
            pe.wait_ge(sem("y_attn_done"), 1)
            for kind in range(4):
                if kind >= 2:
                    pe.wait_ge(sem("gates_read"), kind - 1)
                for c in range(LC):
                    last = pe.matmul(PS[:, 4 * (kind % 2) + c // 2, (c % 2) * S:(c % 2) * S + S],
                                     wbd[:, kind, c, :], convT[:, c, :], start=True, stop=True)
                last.then_inc(sem("gates_done"), 1)
            pe.wait_ge(sem("lru_squared"), 1)
            for c in range(LC):
                last = pe.matmul(PS[:, 0, 0:S], ones, rr[:, c, :], start=c == 0, stop=c == LC - 1)
            last.then_inc(sem("lru_summed"), 1)
            pe.wait_ge(sem("y_lru_done"), 1)
            all_rows("w_out")

            pe.wait_ge(sem("x1_done"), 1)
            pe.wait_ge(sem("diag_done"), 3)
            turn(1, lambda tt: diag[:, tt, :])
            pe.wait_ge(xt_lo_done, 2 * KC)
            channel_blocks("w_pq", act_free, ACT_BLOCKS["w_pq"])
            pe.wait_ge(sem("keys_loaded"), 16)
            pe.wait_ge(act_free, 2 + ACT_BLOCKS["w_pq"] + 16)
            for tt in range(TT):
                for i in range(2 * PH):
                    last = pe.matmul(PS[:, 4 * tt + i // 4, (i % 4) * NK:(i % 4 + 1) * NK],
                                     pqT[:, i, tt * P:tt * P + P], skT[:, i, :], start=True, stop=True)
            last.then_inc(sem("keys_scored"), 1)
            pe.wait_ge(sem("scores_out"), 2)
            channel_blocks("up0", act_free, ACT_BLOCKS["up0"])
            pe.wait_ge(sem("slots_done"), 1)
            for what in range(3):
                for tt in range(TT):
                    last = pe.transpose(PS[:, 2 + what, tt * P:tt * P + P],
                                        slots[:, what, tt * PH:(tt + 1) * PH, :].rearrange("p h k -> p (h k)"), ident)
            last.then_inc(sem("slots_turned"), 1)
            pe.wait_ge(sem("route_over"), 2)
            pe.sem_inc(sem("gates_spread"), 2)

            def spread(n, n_before, width, r):
                pe.wait_ge(sem("hot1_done"), n + (n_before + 1))
                pe.wait_ge(sem("hot2_done"), n + (n_before + 1))
                pe.wait_ge(sem("gates_out"), n + (n_before + 1))
                for t in range(8):
                    for part in range(2):
                        last = pe.matmul(PS[:, 4 + r, t * width:(t + 1) * width], hot1[:, r, t, :],
                                         hot2_gate[width][:, r, part, t, 0:width], start=part == 0, stop=part == 1,
                                         skip_group_check=True)
                last.then_inc(sem("gates_spread"), 1)

            with pe.Fori(0, 16) as j:
                for r in range(2):
                    pe.wait_ge(sem("gates_applied"), 2 * j + (r + 1))
                    spread(2 * j + r, 0, 2 * EB, r)
            for quarter in range(QUARTERS):
                up, down = f"up{quarter}", f"down{quarter}"
                if quarter:
                    with pe.Fori(0, 16) as j:
                        for b in range(2):
                            pe.wait_ge(act_free, 2 * j + (ACT_BLOCKS[up] + b + 1))
                            block_product(up, j, b, PS[:, b, 0:S])
                            if quarter < QUARTERS - 1:
                                spread(2 * j + b, 32 * quarter, EB, b)
                pe.wait_ge(sem("gates_applied"), 34)
                pe.wait_ge(sem("gates_out"), 2 + 32 * min(quarter + 1, 3))
                pe.wait_ge(act_free, 2 + ACT_BLOCKS[up] + EB)
                all_rows(down)
                pe.wait_ge(sem("x2_done"), quarter + 1)
                pe.wait_ge(sem("ada_used"), 48 * (2 * quarter + 1) + 3)
                for layer in range(2 if quarter else 1):
                    for q in range(3):
                        for c in range(4):
                            o = 12 * layer + 4 * q + c
                            last = pe.matmul(PS[:, 7, o:o + 1], ada_acc[:, layer, q, c * P:c * P + P],
                                             ones[:, 0:1], start=True, stop=True, skip_group_check=True)
                last.then_inc(sem("ada_summed"), 1)

            pe.wait_ge(sem("x3_done"), 1)
            turn(2, lambda tt: ident)
            pe.wait_ge(sem("w_dt_loaded"), 32)
            pe.wait_ge(xt_lo_done, 3 * KC)
            for k in range(KC):
                pe.matmul(PS[0:SHEADS, 2, 0:S], w_dt[:, k, :], xt_hi[:, k, :].bitcast(F32), start=k == 0, stop=False)
                last = pe.matmul(PS[0:SHEADS, 2, 0:S], w_dt[:, k, :], xt_lo[:, k, :].bitcast(F32),
                                 start=False, stop=k == KC - 1)
            last.then_inc(sem("dt_product"), 1)
            channel_blocks("xbc", dve_free, DVE_BLOCKS["xbc"])
            pe.wait_ge(sem("decay_done"), 1)
            for tt in range(TT):
                t = slice(tt * P, tt * P + P)
                pe.transpose(PS[:, 3, tt * 64:tt * 64 + 64], dts[:, 0, t], ident[0:SHEADS, 0:SHEADS])
                last = pe.transpose(PS[:, 3, P + tt * 64:P + tt * 64 + 64], dts[:, 1, t], ident[0:SHEADS, 0:SHEADS])
            last.then_inc(sem("dt_turned"), 1)
            pe.wait_ge(sem("ssd_ready"), 1)
            pe.wait_ge(sem("dtn_done"), 1)
            pe.wait_ge(dve_free, 2 + DVE_BLOCKS["xbc"] + BC)
            pe.sem_inc(sem("group_done"), 1)
            pe.sem_inc(sem("xs_turned"), 1)
            pe.sem_inc(sem("cb_product"), 1)
            pe.sem_inc(sem("y_product"), 2)
            pe.wait_ge(sem("mod_done"), 5)
            with pe.Fori(0, SG) as g:
                pe.wait_ge(sem("xs_staged"), g + 1)
                pe.wait_ge(sem("xd_done"), 2 * g + 1)
                for tt in range(TT):
                    for c in range(4):
                        last = pe.transpose(PS[:, tt, c * P:c * P + P], xs_st[:, c, tt * P:tt * P + P], ident)
                last.then_inc(sem("xs_turned"), 1)
                pe.wait_ge(sem("b_staged"), g + 1)
                pe.wait_ge(act_free, 4 * g + (2 + ACT_BLOCKS["z"]))
                pe.matmul(PS[:, 2, 0:S], b_st[:, 0:P], one(xbc, g + XC + SG),
                          start=True, stop=True, skip_group_check=True)
                pe.matmul(PS[:, 2, S:S + P], b_st[:, P:S],
                          xbc[:, ds(g + XC + SG, 1), P:S].rearrange("p a s -> p (a s)"),
                          start=True, stop=True, skip_group_check=True).then_inc(sem("cb_product"), 1)

                def decays(k):
                    pe.wait_ge(sem("decays_read"), 8 * g + k + 1)
                    o = 3 + k % 2
                    pe.matmul(PS[:, o, 0:S], pick_h[:, k, :], dts[:, 2, :], start=True, stop=False,
                              skip_group_check=True)
                    pe.matmul(PS[:, o, S:S + P], pick_h[:, k, :], dts[:, 2, P:S], start=False, stop=False,
                              skip_group_check=True)
                    masked = pe.matmul(PS[:, o, 0:P], ident_b[:, :], causal_b[:, :], start=False, stop=False,
                                       skip_group_check=True)
                    if k == 7:
                        masked.then_inc(sem("group_done"), 1)
                    pe.matmul(PS[:, o, S:S + P], ident_b[:, :], causal_b[:, :], start=False, stop=True,
                              skip_group_check=True).then_inc(sem("decays_spread"), 1)

                pe.wait_ge(sem("heads_staged"), g + 1)
                decays(0)
                for k in range(8):
                    h = k % 2
                    b = k // 2
                    if h == 0:
                        pe.wait_ge(act_free, 4 * g + (ACT_BLOCKS["z"] + b + 1))
                    if k == 2:
                        pe.wait_ge(sem("cb_done"), g + 2)
                    pe.wait_ge(lo_done, 8 * g + (4 * FIRST_BODY["z"] + k + 1))
                    o = PS[:, z_bank[b % 2], 0:S]
                    for kk in range(8):
                        w = slice(kk * P, kk * P + P)
                        last = three(o, w_hi[:, k % 4, w], w_lo[:, k % 4, w],
                                     xt_hi[:, 8 * h + kk, :], xt_lo[:, 8 * h + kk, :],
                                     h == 0 and kk == 0, h == 1 and kk == 7)
                    last.then_inc(tile_used, 1)
                    if k < 7:
                        decays(k + 1)
                    if k == 0:
                        pe.wait_ge(sem("xd_done"), 2 * g + 3)
                    pe.wait_ge(sem("mixed"), 8 * g + k + 3)
                    if k % 2 == 0:
                        pe.wait_ge(sem("y_added"), 4 * g + k // 2 + 1)
                    h = slice(64 * (k % 2), 64 * (k % 2) + 64)
                    o = 5 + (k // 2) % 2
                    pe.matmul(PS[h, o, 0:S], xd[:, 0, k * 64:k * 64 + 64], mm_[:, k % 2, 0:S], start=True, stop=False,
                              skip_group_check=True)
                    pe.matmul(PS[h, o, P:S], xd[:, 1, k * 64:k * 64 + 64], mm_[:, k % 2, S:S + P],
                              start=False, stop=True, skip_group_check=True).then_inc(sem("y_product"), 1)
            pe.wait_ge(sem("ada_used"), 48 * 8 + 3)
            for q in range(3):
                for c in range(4):
                    last = pe.matmul(PS[:, 3, 4 * q + c:4 * q + c + 1], ada_acc_z[:, q, c * P:c * P + P],
                                     ones[:, 0:1], start=True, stop=True, skip_group_check=True)
            last.then_inc(sem("ada_summed"), 1)
            pe.wait_ge(sem("mod_done"), 7)
            with pe.Fori(0, SG) as g:
                pe.wait_ge(sem("group_squared"), g + 1)
                pe.wait_ge(sem("group_root"), g + 1)
                for c in range(4):
                    last = pe.matmul(PS[:, 2, 0:S], ones, sq[:, c, :], start=c == 0, stop=c == 3)
                last.then_inc(sem("group_summed"), 1)
            pe.wait_ge(sem("ssd_normed"), SG + 1)
            all_rows("a_out")

            def gate_rows(layer):
                for c in range(KC):
                    pe.wait_ge(sem("dcol_done"), KC * layer + c + 1)
                    pe.matmul(PS[:, c // 4, (c % 4) * P:(c % 4 + 1) * P], ones, dcol[:, c % 2, :],
                              start=True, stop=True, skip_group_check=True).then_inc(sem("gate_spread"), 1)

            pe.wait_ge(sem("y_copied"), 1)
            gate_rows(0)

            pe.wait_ge(sem("x4_done"), 1)
            turn(3, lambda tt: ident)
            pe.wait_ge(xt_lo_done, 4 * KC)
            channel_blocks("k2", act_free, ACT_BLOCKS["k2"])
            pe.wait_ge(act_free, 2 + ACT_BLOCKS["k2"] + 24)
            with pe.Fori(0, DG) as g:
                pe.wait_ge(sem("v2_out"), g + 1)
                token_columns(16 * g, FIRST_BODY["v2"], 0, 1)
            pe.wait_ge(sem("v2_out"), DG + 1)
            turn(4, lambda tt: ident)
            pe.wait_ge(xt_lo_done, 5 * KC)
            channel_blocks("q2", act_free, ACT_BLOCKS["q2"])
            token_columns(0, FIRST_BODY["z2"], 4, 1)
            pe.wait_ge(sem("z2_out"), 1)
            pe.sem_inc(sem("head_scored"), 1)
            with pe.Fori(0, DH) as h:
                pe.wait_ge(sem("q_staged"), h + 1)
                pe.wait_ge(sem("dist_added"), h + 1)
                for g in range(DG):
                    pe.matmul(PS[:, 0, g * P:g * P + P], q_st[:, g, 0:P],
                              k2T[:, ds(h + g * DH, 1), 0:P].rearrange("p a s -> p (a s)"),
                              start=True, stop=True, skip_group_check=True)
                    last = pe.matmul(PS[:, 1 + g // 2, (g % 2) * S:(g % 2) * S + S], q_st[:, g, P:S],
                                     one(k2T, h + g * DH),
                                     start=True, stop=True, skip_group_check=True)
                last.then_inc(sem("head_scored"), 1)
                pe.wait_ge(sem("head_exp"), h + 1)
                for i in range(9):
                    last = pe.transpose(PS[:, 3 + i // 4, (i % 4) * P:(i % 4 + 1) * P], sc2[:, i * P:i * P + P], ident)
                last.then_inc(sem("head_turned"), 1)
                pe.wait_ge(sem("pT2_done"), h + 1)
                pe.wait_ge(sem("head_out"), h + 1)
                for g in range(DG):
                    pe.matmul(PS[:, 6, 0:P], pT2[:, g, :], v2n[:, 0, ds(h * P + g * 1024, P)],
                              start=g == 0, stop=g == DG - 1, skip_group_check=True)
                for g in range(DG):
                    for kt in range(2):
                        last = pe.matmul(PS[:, 7, 0:P], pT2[:, 3 + 2 * g + kt, :],
                                         v2n[:, kt, ds(h * P + g * 1024, P)],
                                         start=g == 0 and kt == 0, stop=g == DG - 1 and kt == 1,
                                         skip_group_check=True)
                last.then_inc(sem("head_product"), 1)
            pe.wait_ge(sem("head_out"), DH + 1)
            for c in range(DH):
                for tt in range(TT):
                    last = pe.transpose(PS[:, c // 2, (c % 2) * S + tt * P:(c % 2) * S + tt * P + P],
                                        zn[:, tt, c * P:c * P + P], ident)
            last.then_inc(sem("o_turned"), 1)
            pe.wait_ge(sem("oT_done"), 1)
            all_rows("b_out")
            pe.wait_ge(sem("y_copied"), 2)
            gate_rows(1)

        @block.scalar
        def _(act):
            def high(body, u, first=False):
                act.wait_ge(raw_loaded[u], 16 * (body + 1))
                if not first:
                    act.wait_ge(tile_used, 4 * body + u - 3)
                act.activation(w_hi[:, u, :], raw[:, u, :], ACT.Copy).then_inc(hi_done, 1)

            def bodies(name, evac=None, start=0, n=None, last=False):
                n = NB[name] if n is None else n
                with act.Fori(start, start + n) as j:
                    for u in range(4):
                        if not last:
                            high(j + FIRST_BODY[name] + 1, u)
                        if evac and u % 2 == 1:
                            act.wait_ge(tile_used, 4 * (j + FIRST_BODY[name]) + u + 1)
                            evac(2 * j + u // 2, u // 2)

            def stage(name, source, k, s, body):
                act.wait_ge(tile_used, 4 * body + 2 * s + 2)
                act.activation(st_hi[:, s, :], source(k), ACT.Copy).then_inc(stage_hi_done, 1)

            def rows_bodies(name, source):
                f = FIRST_BODY[name]
                n = NB[name]
                act.wait_ge(tile_used, 4 * f)
                for s in range(2):
                    act.activation(st_hi[:, s, :], source(s), ACT.Copy).then_inc(stage_hi_done, 1)
                with act.Fori(0, n - 1) as j:
                    for u in range(4):
                        high(j + f + 1, u)
                        if u % 2 == 1:
                            stage(name, source, 2 * j + 2 + u // 2, u // 2, j + f)
                if name != "b_out":
                    for u in range(4):
                        high(f + n, u)

            def turned(n, scale, bias=None):
                for c in range(KC):
                    act.wait_ge(xt_turned, KC * n + c + 1)
                    act.activation(xt_hi[:, c, :], PS[:, c % 8, 0:S], ACT.Identity, scale=scale(c),
                                   bias=bias(c) if bias else 0.0).then_inc(xt_hi_done, 1)

            def root(o, i, scale, eps):
                return act.activation(o, i, ACT.Sqrt, scale=scale, bias=pc[:, PC[eps]:PC[eps] + 1])

            act.wait_ge(params_loaded, 16)
            act.wait_ge(x_loaded, 16)
            act.sem_inc(act_free, 2)
            for u in range(4):
                high(0, u, first=True)
            for tt in range(TT):
                act.activation(PS[:, 0:4, :].rearrange("p b n -> p (b n)"), X[:, tt, :], ACT.Square,
                               accum_out=stat[:, tt:tt + 1]).then_inc(sem("x_squared"), 1)
                act.wait_ge(sem("x_squared"), tt + 1)
            root(stat[:, 2:4], stat[:, 0:2], 1.0 / D, "eps").then_inc(sem("rms_root"), 1)
            turned(0, lambda c: pc[:, PC["g_mix"] + c:PC["g_mix"] + c + 1])
            with act.Fori(0, NB["q"]) as j:
                for u in range(4):
                    high(j + 1, u)
            act.wait_ge(tile_used, 16)
            for tt in range(TT):
                last = act.activation(qn[:, tt, :], PS[:, 2 * tt:2 * tt + 2, :].rearrange("p b n -> p (b n)"), ACT.Copy)
            last.then_inc(sem("qkv_out"), 1)
            bodies("kv")
            act.wait_ge(tile_used, 24)
            act.activation(kvn[:, :, :], PS[:, 4:6, :], ACT.Copy).then_inc(sem("qkv_out"), 1)
            bodies("gate", lambda i, b: act.activation(
                one(gateT, i), PS[:, b, 0:S],
                ACT.Gelu_apprx_tanh).then_inc(act_free, 1))
            bodies("rec")
            act.wait_ge(sem("qk_turned"), 1)
            act.activation(qT[:, :, :].rearrange("p c s -> p (c s)"), PS[:, 0:4, :].rearrange("p b n -> p (b n)"),
                           ACT.Copy).then_inc(sem("qkT_done"), 1)
            act.activation(kT[:, :, :].rearrange("p c s -> p (c s)"), PS[:, 4:6, :].rearrange("p b n -> p (b n)"),
                           ACT.Copy).then_inc(sem("qkT_done"), 1)
            for n in range(8):
                act.wait_ge(sem("max_done"), n + 1)
                if n:
                    act.wait_ge(sem("p_turned"), n)
                act.activation(sm[:, n, 1, :], sm[:, n, 1, :], ACT.Exp).then_inc(sem("sink_exp"), 1)
                for i in range(4):
                    last = act.activation(pr[:, i, :], sc[:, n % 2, i, :], ACT.Exp, bias=sm[:, n, 0, i:i + 1],
                                          accum_out=stat[:, 4 + 4 * (n % 2) + i:5 + 4 * (n % 2) + i])
                last.then_inc(sem("probs_done"), 1)
                act.wait_ge(sem("p_turned"), n + 1)
                if n:
                    act.wait_ge(sem("pv_done"), n)
                act.activation(pT[:, :, :].rearrange("p c s -> p (c s)"), PS[:, 4:6, :].rearrange("p b n -> p (b n)"),
                               ACT.Copy).then_inc(sem("pT_done"), 1)
            act.wait_ge(sem("attn_out"), 8)
            for tt in range(TT):
                last = act.activation(PS[:, 0:2, :].rearrange("p b n -> p (b n)"), yn[:, tt, :], ACT.Square,
                                      accum_out=stat[:, tt:tt + 1])
                last.then_inc(sem("y_squared"), 1)
                act.wait_ge(sem("y_squared"), tt + 1)
            root(stat[:, 2:4], stat[:, 0:2], 1.0 / QC, "eps").then_inc(sem("rms_root"), 1)
            act.wait_ge(sem("y_turned"), 1)
            for c in range(LC):
                g = pc[:, PC["g_attn"] + c:PC["g_attn"] + c + 1]
                last = act.activation(yT[:, c, :], PS[:, c // 2, (c % 2) * S:(c % 2) * S + S], ACT.Copy, scale=g)
            last.then_inc(sem("y_attn_done"), 1)
            act.wait_ge(sem("lam_ready"), 1)
            act.activation(spl[:, 1, :], spl[:, 1, :], ACT.Exp).then_inc(sem("lam_exp"), 1)
            act.wait_ge(sem("spl_done"), 1)
            for kind in range(4):
                act.wait_ge(sem("gates_done"), kind + 1)
                if kind == 2:
                    act.wait_ge(sem("forward_used"), 1)
                for c in range(LC):
                    b = PC["gate_b"] + kind * LC + c
                    last = act.activation((rr if kind % 2 == 0 else ii)[:, c, :],
                                          PS[:, 4 * (kind % 2) + c // 2, (c % 2) * S:(c % 2) * S + S],
                                          ACT.Sigmoid, bias=pc[:, b:b + 1])
                last.then_inc(sem("gates_read"), 1)
                if kind % 2 == 1:
                    act.wait_ge(sem("gates_read"), kind + 1)
                    dr = kind // 2
                    for c in range(LC):
                        act.activation(aa[:, c, :], rr[:, c, :], ACT.Exp, scale=spl[:, 7, dr * LC + c:dr * LC + c + 1])
                    for c in range(LC):
                        last = act.activation(rr[:, c, :], rr[:, c, :], ACT.Tanh,
                                              scale=spl[:, 6, dr * LC + c:dr * LC + c + 1])
                    last.then_inc(sem("decays_done"), 1)
                    act.wait_ge(sem("one_minus_done"), dr + 1)
                    act.activation(hh[:, dr, :, :], hh[:, dr, :, :], ACT.Sqrt,
                                   bias=pc[:, PC["tiny"]:PC["tiny"] + 1]).then_inc(sem("root_done"), 1)
            act.wait_ge(sem("y_mixed"), 1)
            act.activation(rr[:, :, :], yT[:, LC:2 * LC, :], ACT.Square).then_inc(sem("lru_squared"), 1)
            act.wait_ge(sem("lru_summed"), 1)
            root(rstdb[:, 0, :], PS[:, 0, 0:S], 1.0 / LRU, "eps").then_inc(sem("lru_root"), 1)
            act.wait_ge(sem("y_lru_done"), 1)
            rows_bodies("w_out", lambda k: one(yT, k))
            act.wait_ge(sem("x1_done"), 1)
            for tt in range(TT):
                act.activation(PS[:, 0:4, :].rearrange("p b n -> p (b n)"), X[:, tt, :], ACT.Square,
                               accum_out=stat[:, tt:tt + 1]).then_inc(sem("x_squared"), 1)
                act.wait_ge(sem("x_squared"), 2 + tt + 1)
            root(stat[:, 2:4], stat[:, 0:2], 1.0 / D, "eps").then_inc(sem("rms_root"), 1)
            turned(1, lambda c: pc[:, PC["g_ffn"] + c:PC["g_ffn"] + c + 1])
            bodies("w_pq", lambda i, b: act.activation(
                one(pqT, i), PS[:, b, 0:S], ACT.Copy).then_inc(act_free, 1))
            act.wait_ge(sem("keys_scored"), 1)
            for tt in range(TT):
                last = act.activation(score[:, tt * 16:(tt + 1) * 16, :].rearrange("p c s -> p (c s)"),
                                      PS[:, 4 * tt:4 * tt + 4, :].rearrange("p b n -> p (b n)"), ACT.Copy)
                last.then_inc(sem("scores_out"), 1)
            act.activation(silu_c[:, :], pc[:, PC["cond"]:PC["cond"] + KC], ACT.Silu).then_inc(sem("silu_c_done"), 1)
            bodies("up0", lambda i, b: act.activation(
                one(hid0, i), PS[:, b, 0:S], ACT.Gelu_apprx_tanh).then_inc(act_free, 1))
            act.wait_ge(sem("pick_shifted"), 1)
            act.activation(pick[:, :, :], pick[:, :, :], ACT.Exp).then_inc(sem("pick_exp"), 1)
            act.wait_ge(sem("slots_turned"), 1)
            act.activation(slot_gate[:, 0, :], PS[:, 4, 0:S], ACT.Copy).then_inc(sem("slot_gate_high"), 1)
            act.activation(slotsT[:, :, :], PS[:, 2:4, 0:S], ACT.Copy).then_inc(sem("route_over"), 1)
            def gates_out(n, n_before, o, r, first):
                act.wait_ge(sem("gates_spread"), n + (n_before + 3))
                width = 2 * EB if first else EB
                src = PS[:, 4 + r, 0:8 * width].rearrange("p (t b) -> p b t", t=8)[:, width - EB:width, :]
                act.activation(o[:, :, ds(8 * n, 8)], src, ACT.Copy).then_inc(sem("gates_out"), 1)

            act.sem_inc(sem("gates_out"), 2)
            with act.Fori(0, 16) as j:
                for r in range(2):
                    gates_out(2 * j + r, 0, hid[1], r, True)
            for quarter in range(QUARTERS):
                up, down = f"up{quarter}", f"down{quarter}"
                if quarter:
                    with act.Fori(0, 16) as j:
                        for u in range(4):
                            high(j + (FIRST_BODY[up] + 1), u)
                            if u % 2 == 1:
                                b = u // 2
                                act.wait_ge(tile_used, 4 * j + (4 * FIRST_BODY[up] + u + 1))
                                act.wait_ge(sem("gated"), 2 * j + (EB * (quarter - 1) + b + 1))
                                act.activation(geluT[:, b, :], PS[:, b, 0:S], ACT.Gelu_apprx_tanh).then_inc(act_free, 1)
                                if quarter < QUARTERS - 1:
                                    gates_out(2 * j + b, 32 * quarter, hid[(quarter + 1) % 2], b, False)
                    act.wait_ge(sem("gated"), EB * quarter + 2)
                else:
                    act.wait_ge(sem("gates_applied"), 34)
                rows_bodies(down, lambda k: one(hid[quarter % 2], k))
            act.wait_ge(sem("x2_done"), QUARTERS)
            for tt in range(TT):
                act.activation(PS[:, 0:4, :].rearrange("p b n -> p (b n)"), X[:, tt, :], ACT.Square,
                               accum_out=stat[:, tt:tt + 1]).then_inc(sem("x_squared"), 1)
                act.wait_ge(sem("x_squared"), 4 + tt + 1)
            root(stat[:, 2:4], stat[:, 0:2], 1.0 / D, "eps").then_inc(sem("rms_root"), 1)
            act.wait_ge(sem("mod_done"), 5)
            turned(2, lambda c: mod[:, 16 + c:17 + c], lambda c: mod[:, c:c + 1])
            act.wait_ge(sem("dt_abs"), 1)
            act.activation(dts[:, 3, :], dts[:, 3, :], ACT.Exp).then_inc(sem("dt_exp"), 1)
            act.activation(stat[0:SHEADS, 12:13], pc[0:SHEADS, PC["a_log"]:PC["a_log"] + 1], ACT.Exp)\
                .then_inc(sem("dt_exp"), 1)
            act.sem_inc(sem("conv_read"), 2)
            with act.Fori(0, NB["xbc"]) as j:
                def silu(b):
                    i = 2 * j + b
                    act.wait_ge(sem("conv_done"), i + 1)
                    act.activation(one(xbc, i), cbuf[:, b, :], ACT.Silu,
                                   bias=pc[:, ds(i + PC["a_conv_b"], 1)]).then_inc(sem("conv_read"), 1)

                for u in range(4):
                    high(j + FIRST_BODY["xbc"] + 1, u)
                    if u >= 2:
                        silu(u - 2)
            act.activation(ident_b[:, :], ident, ACT.Copy)
            act.activation(causal_b[:, :], causal[:, :], ACT.Copy).then_inc(sem("masks_done"), 1)
            act.wait_ge(sem("dt_turned"), 1)
            act.activation(dtn[:, :, :].rearrange("p a s -> p (a s)"), PS[:, 3, 0:P], ACT.Copy)
            act.activation(nacn[:, :, :].rearrange("p a s -> p (a s)"), PS[:, 3, P:2 * P], ACT.Copy, scale=-1.0)\
                .then_inc(sem("dtn_done"), 1)
            act.wait_ge(sem("conv_read"), BC + 2)
            act.wait_ge(sem("masks_done"), 1)
            act.wait_ge(sem("dtn_done"), 1)
            act.sem_inc(sem("ssd_ready"), 1)
            act.sem_inc(sem("cb_done"), 1)
            act.sem_inc(sem("decays_read"), 2)
            with act.Fori(0, SG) as g:
                act.wait_ge(sem("cb_product"), g + 2)
                act.wait_ge(sem("mixed"), 8 * g + 2)
                act.activation(cbm[:, :], PS[:, 2, 0:384], ACT.Copy).then_inc(sem("cb_done"), 1)
                for k in range(8):
                    act.wait_ge(sem("decays_spread"), 8 * g + k + 1)
                    act.wait_ge(sem("mixed"), 8 * g + k + 1)
                    o = 3 + k % 2
                    act.activation(ex[:, k % 2, 0:S], PS[:, o, 0:S], ACT.Exp, bias=nacn[:, 0, ds(8 * g + k, 1)])
                    act.activation(ex[:, k % 2, S:384], PS[:, o, S:384], ACT.Exp, bias=nacn[:, 1, ds(8 * g + k, 1)])\
                        .then_inc(sem("decays_read"), 1)
                    high(2 * g + (FIRST_BODY["z"] + k // 4 + 1), k % 4)
                    if k % 2 == 1:
                        b = k // 2
                        act.wait_ge(tile_used, 8 * g + (4 * FIRST_BODY["z"] + k + 1))
                        act.wait_ge(sem("y_gated"), 4 * g + b + 1)
                        act.activation(zt[:, b % 2, :], PS[:, z_bank[b % 2], 0:S], ACT.Silu)\
                            .then_inc(act_free, 1)
            act.wait_ge(sem("y_gated"), XC + 2)
            act.sem_inc(sem("group_root"), 1)
            with act.Fori(0, SG) as g:
                act.activation(sq[:, :, :], xbc[:, ds(4 * g, 4), :], ACT.Square).then_inc(sem("group_squared"), 1)
                act.wait_ge(sem("group_summed"), g + 1)
                act.wait_ge(sem("ssd_normed"), g + 1)
                root(rg[:, 0, :], PS[:, 2, 0:S], 1.0 / 512, "ln_eps").then_inc(sem("group_root"), 1)
            act.wait_ge(sem("ssd_normed"), SG + 1)
            rows_bodies("a_out", lambda k: one(xbc, k))

            def layer_norm(n):
                act.wait_ge(sem("y_copied"), n + 1)
                act.wait_ge(sem("gate_spread"), KC * (n + 1))
                act.activation(rows[:, 0, :], PS[:, 0:4, :].rearrange("p b n -> p (b n)"), ACT.Copy)\
                    .then_inc(sem("gate_rows_done"), 1)
                for tt in range(TT):
                    act.wait_ge(sem("ln_in"), TT * n + tt + 1)
                    act.activation(PS[:, 0:4, :].rearrange("p b n -> p (b n)"), X[:, tt, :], ACT.Copy,
                                   accum_out=stat[:, tt:tt + 1]).then_inc(sem("ln_sum"), 1)
                    act.wait_ge(sem("ln_sum"), TT * n + tt + 1)
                for tt in range(TT):
                    act.wait_ge(sem("ln_centred"), TT * n + tt + 1)
                    act.activation(PS[:, 0:4, :].rearrange("p b n -> p (b n)"), X[:, tt, :], ACT.Square,
                                   accum_out=stat[:, 4 + tt:5 + tt]).then_inc(sem("ln_squared"), 1)
                    act.wait_ge(sem("ln_squared"), TT * n + tt + 1)
                root(stat[:, 6:8], stat[:, 4:6], 1.0 / D, "ln_eps").then_inc(sem("ln_root"), 1)

            layer_norm(0)
            turned(3, lambda c: 1.0)
            bodies("k2", lambda i, b: act.activation(
                one(k2T, i), PS[:, b, 0:S], ACT.Copy).then_inc(act_free, 1))
            act.sem_inc(sem("v2_out"), 1)
            with act.Fori(0, DG) as g:
                for i in range(4):
                    for u in range(4):
                        high(4 * g + (FIRST_BODY["v2"] + i + 1), u)
                act.wait_ge(tile_used, 16 * g + 4 * FIRST_BODY["v2"] + 16)
                for tt in range(TT):
                    last = act.activation(v2n[:, tt, ds(g * 1024, 1024)],
                                          PS[:, 2 * tt:2 * tt + 2, :].rearrange("p b n -> p (b n)"), ACT.Copy)
                last.then_inc(sem("v2_out"), 1)
            turned(4, lambda c: mod[:, 64 + c:65 + c], lambda c: mod[:, 48 + c:49 + c])

            def queries(i, b):
                act.activation(one(q2T, i), PS[:, b, 0:S], ACT.Copy,
                               scale=float(P) ** -0.5).then_inc(act_free, 1)

            bodies("q2", queries)
            bodies("z2")
            act.wait_ge(tile_used, 4 * FIRST_BODY["b_out"])
            for tt in range(TT):
                last = act.activation(zn[:, tt, :], PS[:, 4 + 2 * tt:6 + 2 * tt, :].rearrange("p b n -> p (b n)"), ACT.Silu)
            last.then_inc(sem("z2_out"), 1)
            with act.Fori(0, DH) as h:
                act.wait_ge(sem("head_max"), h + 1)
                act.activation(sc2[:, 0:384], sc2[:, 0:384], ACT.Exp, bias=sm2[:, 2:3], accum_out=sm2[:, 4:5])
                act.activation(sc2[:, 384:1152], sc2[:, 384:1152], ACT.Exp, bias=sm2[:, 3:4], accum_out=sm2[:, 5:6])\
                    .then_inc(sem("head_exp"), 1)
                act.wait_ge(sem("head_turned"), h + 1)
                act.activation(pT2[:, 0:8, :].rearrange("p c s -> p (c s)"),
                               PS[:, 3:5, :].rearrange("p b n -> p (b n)"), ACT.Copy)
                act.activation(pT2[:, 8, :], PS[:, 5, 0:P], ACT.Copy).then_inc(sem("pT2_done"), 1)
            act.wait_ge(sem("o_turned"), 1)
            act.activation(oT[:, 0:DH, :].rearrange("p c s -> p (c s)"), PS[:, 0:4, :].rearrange("p b n -> p (b n)"),
                           ACT.Copy).then_inc(sem("oT_done"), 1)
            act.wait_ge(sem("oT_done"), 1)
            rows_bodies("b_out", lambda k: one(oT, k))
            layer_norm(1)

        @block.vector
        def _(dve):
            link = Chain(dve, dve_link)

            def low(body, u):
                dve.wait_ge(hi_done, 4 * body + u + 1)
                dve.tensor_tensor(w_lo[:, u, :], raw[:, u, :], w_hi[:, u, :].bitcast(F32), ALU.subtract)\
                    .then_inc(lo_done, 1)

            def bodies(name, evac=None):
                with dve.Fori(0, NB[name]) as j:
                    if evac:
                        link.loop(j, evac.links * 2)
                    for u in range(4):
                        low(j + FIRST_BODY[name] + 1, u)
                        if evac and u % 2 == 1:
                            dve.wait_ge(tile_used, 4 * j + (4 * FIRST_BODY[name] + u + 1))
                            evac(2 * j + u // 2, u // 2)
                if evac:
                    link.end(NB[name])

            def stage(source, k, s, name):
                dve.wait_ge(stage_hi_done, k + (CHUNKS[name] + 1))
                dve.tensor_tensor(st_lo[:, s, :], source(k), st_hi[:, s, :].bitcast(F32), ALU.subtract)\
                    .then_inc(stage_lo_done, 1)

            def rows_bodies(name, source):
                for s in range(2):
                    stage(source, s, s, name)
                with dve.Fori(0, NB[name] - 1) as j:
                    for u in range(4):
                        low(j + (FIRST_BODY[name] + 1), u)
                        if u % 2 == 1:
                            stage(source, 2 * j + (2 + u // 2), u // 2, name)
                if name != "b_out":
                    for u in range(4):
                        low(FIRST_BODY[name] + NB[name], u)
                dve.wait_ge(tile_used, 4 * (FIRST_BODY[name] + NB[name]))

            def banks(first, n):
                return PS[:, first:first + n, :].rearrange("p b n -> p (b n)")

            def turned(n, scale, bias=None):
                for c in range(KC):
                    src = PS[:, c % 8, 0:S]
                    hi = xt_hi[:, c, :].bitcast(F32)
                    dve.wait_ge(xt_hi_done, KC * n + c + 1)
                    if bias:
                        link(dve.tensor_scalar(xtmp[:, c % 2, :], src, scale(c), bias(c), ALU.mult, ALU.add))
                        o = dve.tensor_tensor(xt_lo[:, c, :], xtmp[:, c % 2, :], hi, ALU.subtract)
                    else:
                        o = dve.scalar_tensor_tensor(xt_lo[:, c, :], src, scale(c), hi, ALU.mult, ALU.subtract)
                    o.then_inc(xt_lo_done, 1)

            def row_norms(n):
                dve.wait_ge(sem("rms_root"), n)
                link(dve.reciprocal(stat[:, 12:14], stat[:, 2:4]))
                for tt in range(TT):
                    last = dve.tensor_scalar(diag[:, tt, :], ident, stat[:, 12 + tt:13 + tt], None, ALU.mult)
                last.then_inc(sem("diag_done"), 1)

            def softplus(o, x, e, t1, t2, t3):
                link(dve.tensor_scalar(t1, e, 2.0, None, ALU.add))
                link(dve.reciprocal(t1, t1))
                link(dve.tensor_tensor(t1, t1, e, ALU.mult))
                link(dve.tensor_tensor(t2, t1, t1, ALU.mult))
                link(dve.tensor_scalar(t3, t2, 1.0 / 17, None, ALU.mult))
                for n in range(15, 1, -2):
                    link(dve.scalar_tensor_tensor(t3, t3, 1.0 / n, t2, ALU.add, ALU.mult))
                link(dve.scalar_tensor_tensor(t3, t3, 1.0, t1, ALU.add, ALU.mult))
                link(dve.tensor_scalar(t1, x, 0.0, None, ALU.max))
                link(dve.scalar_tensor_tensor(o, t3, 2.0, t1, ALU.mult, ALU.add))

            def convolve(o, src, weight, centre):
                link(dve.tensor_scalar(o, src, weight(centre), None, ALU.mult))
                for t in range(4):
                    d = t - centre
                    if d < 0:
                        link(dve.scalar_tensor_tensor(o[:, -d:S], src[:, 0:S + d], weight(t), o[:, -d:S], ALU.mult, ALU.add))
                    if d > 0:
                        link(dve.scalar_tensor_tensor(o[:, 0:S - d], src[:, d:S], weight(t), o[:, 0:S - d], ALU.mult, ALU.add))

            dve.sem_inc(dve_free, 2)
            for u in range(4):
                low(0, u)
            dve.wait_ge(consts_loaded, 16)
            dve.wait_ge(params_loaded, 16)
            row_norms(1)
            turned(0, lambda c: pc[:, PC["g_mix"] + c:PC["g_mix"] + c + 1])
            for name in ("q", "kv", "gate"):
                bodies(name)

            def recurrent(i, b):
                convolve(one(convT, i), PS[:, b, 0:S], lambda t: pc[:, ds(4 * i + (PC["conv_w"] + t), 1)], 2)
                link(dve.tensor_scalar(one(convT, i), one(convT, i), pc[:, ds(i + PC["conv_b"], 1)], None, ALU.add))
                dve.sem_inc(dve_free, 1)

            recurrent.links = 5
            bodies("rec", recurrent)

            dve.wait_ge(sem("window_loaded"), 32)
            dve.wait_ge(sem("qkv_out"), 2)
            flat = rtmp[:, :, :, :].rearrange("p a b s -> p (a b s)")
            for tt in range(TT):
                def angles(name, shape):
                    return cw[:, CW[name] + tt * 32:CW[name] + tt * 32 + 32].unsqueeze(1).to_broadcast(shape)

                for src, heads, outs in (
                    (qn[:, tt, :], NQ, [qn[:, tt, :].rearrange("p (h d) -> p h d", d=HD)]),
                    (kvn[:, tt, 0:NKV * HD], NKV, [kdup[:, tt, :, r, :] for r in range(2)]),
                ):
                    x = src.rearrange("p (h d) -> p h d", d=HD)
                    n = heads * 32
                    tmp = [flat[:, i * n:(i + 1) * n].rearrange("p (h d) -> p h d", d=32) for i in range(4)]
                    cos, sin = angles("cos", [P, heads, 32]), angles("sin", [P, heads, 32])
                    link.post(dve.tensor_tensor(tmp[0], x[:, :, 0:32], cos, ALU.mult))
                    link.post(dve.tensor_tensor(tmp[1], x[:, :, 32:64], sin, ALU.mult))
                    link.post(dve.tensor_tensor(tmp[2], x[:, :, 32:64], cos, ALU.mult))
                    link(dve.tensor_tensor(tmp[3], x[:, :, 0:32], sin, ALU.mult))
                    for o in outs:
                        link.post(dve.tensor_tensor(o[:, :, 0:32], tmp[0], tmp[1], ALU.subtract))
                        link(dve.tensor_tensor(o[:, :, 32:64], tmp[2], tmp[3], ALU.add))
            dve.sem_inc(sem("rope_done"), 1)

            steps = [(tt, g) for tt in range(TT) for g in range(NKV)]

            def maxima(n):
                tt, g = steps[n]
                dve.wait_ge(sem("scores_done"), n + 1)
                if n >= 2:
                    dve.wait_ge(sem("probs_done"), n - 1)
                window = cw[:, CW["window"] + tt * S:CW["window"] + (tt + 1) * S].unsqueeze(1).to_broadcast([P, 4, S])
                dve.scalar_tensor_tensor(sc[:, n % 2, :, :], banks(2 * (n % 2), 2).rearrange("p (h s) -> p h s", s=S),
                                         HD ** -0.5, window, ALU.mult, ALU.add).then_inc(sem("scores_read"), 1)
                dve.wait_ge(sem("scores_read"), n + 1)
                link(dve.tensor_reduce(sm[:, n, 0, :], sc[:, n % 2, :, :], AX.X, ALU.max))
                link(dve.tensor_tensor(sm[:, n, 0, :], sm[:, n, 0, :], sinkb[:, 4 * g:4 * g + 4], ALU.max))
                link(dve.tensor_tensor(sm[:, n, 1, :], sinkb[:, 4 * g:4 * g + 4], sm[:, n, 0, :], ALU.subtract))
                dve.tensor_scalar(sm[:, n, 0, :], sm[:, n, 0, :], -1.0, None, ALU.mult).then_inc(sem("max_done"), 1)

            maxima(0)
            for n, (tt, g) in enumerate(steps):
                if n + 1 < len(steps):
                    maxima(n + 1)
                dve.wait_ge(sem("probs_done"), n + 1)
                link(dve.tensor_tensor(sm[:, n, 1, :], sm[:, n, 1, :], stat[:, 4 + 4 * (n % 2):8 + 4 * (n % 2)], ALU.add))
                link(dve.reciprocal(sm[:, n, 1, :], sm[:, n, 1, :]))
                dve.wait_ge(sem("pv_done"), n + 1)
                o = yn[:, tt, g * S:(g + 1) * S].rearrange("p (i r d) -> p r i d", i=2, r=2)
                dve.tensor_tensor(o, PS[:, 6, 0:S].rearrange("p (r i d) -> p r i d", r=2, i=2),
                                  sm[:, n, 1, :].rearrange("p (r i) -> p r i", r=2).unsqueeze(3)
                                  .to_broadcast([P, 2, 2, HD]), ALU.mult).then_inc(sem("attn_out"), 1)
            row_norms(2)

            dve.wait_ge(sem("y_attn_done"), 1)
            lam = pc[:, PC["lam"]:PC["lam"] + 2 * LC]
            link(dve.tensor_scalar(spl[:, 0, :], lam, -1.0, None, ALU.mult))
            dve.scalar_tensor_tensor(spl[:, 1, :], lam, -1.0, lam, ALU.mult, ALU.min).then_inc(sem("lam_ready"), 1)
            dve.wait_ge(sem("lam_exp"), 1)
            softplus(spl[:, 5, :], spl[:, 0, :], spl[:, 1, :], spl[:, 2, :], spl[:, 3, :], spl[:, 4, :])
            link(dve.tensor_scalar(spl[:, 6, :], spl[:, 5, :], 8.0, None, ALU.mult))
            dve.tensor_scalar(spl[:, 7, :], spl[:, 5, :], -8.0, None, ALU.mult).then_inc(sem("spl_done"), 1)
            for dr in range(2):
                wide = lambda t: t.rearrange("p c s -> p (c s)")
                dve.wait_ge(sem("decays_done"), dr + 1)
                h = hh[:, dr, :, :]
                link(dve.tensor_tensor(h, aa[:, :, :], aa[:, :, :], ALU.mult))
                dve.scalar_tensor_tensor(wide(h), wide(h), 1.0, wide(rr[:, :, :]), ALU.add, ALU.mult)\
                    .then_inc(sem("one_minus_done"), 1)
                link(dve.tensor_tensor(ii[:, :, :], ii[:, :, :], convT[:, :, :], ALU.mult))
                edge = 0 if dr == 0 else S - 1
                link(dve.memset(aa[:, :, edge:edge + 1], 0.0))
                dve.wait_ge(sem("root_done"), dr + 1)
                link(dve.tensor_tensor(ii[:, :, :], ii[:, :, :], h, ALU.mult))
                a0, u0, o0 = wide(aa[:, :, :]), wide(ii[:, :, :]), wide(h)
                if dr:
                    a0, u0, o0 = a0[:, ::-1], u0[:, ::-1], o0[:, ::-1]
                dve.tensor_tensor_scan(o0, a0, u0, 0.0, ALU.mult, ALU.add).then_inc(sem("forward_used"), 1)
                dve.wait_ge(sem("forward_used"), dr + 1)
            link(dve.tensor_tensor(hh[:, 0, :, :], hh[:, 0, :, :], hh[:, 1, :, :], ALU.add))
            dve.tensor_tensor(yT[:, LC:2 * LC, :], hh[:, 0, :, :], gateT[:, :, :], ALU.mult).then_inc(sem("y_mixed"), 1)
            dve.wait_ge(sem("lru_root"), 1)
            link(dve.reciprocal(rstdb[:, 1, :], rstdb[:, 0, :]))
            for c in range(LC):
                last = dve.scalar_tensor_tensor(yT[:, LC + c, :], yT[:, LC + c, :], pc[:, PC["g_lru"] + c:PC["g_lru"] + c + 1],
                                                rstdb[:, 1, :], ALU.mult, ALU.mult)
            last.then_inc(sem("y_lru_done"), 1)
            dve.wait_ge(sem("y_lru_done"), 1)

            def add_product(signal):
                for tt in range(TT):
                    last = dve.tensor_tensor(X[:, tt, :], X[:, tt, :], banks(4 * tt, 4), ALU.add)
                    if tt == 0:
                        link.post(last)
                last.then_inc(signal, 1)

            rows_bodies("w_out", lambda k: one(yT, k))
            add_product(sem("x1_done"))
            dve.wait_ge(sem("x1_done"), 1)
            row_norms(3)
            turned(1, lambda c: pc[:, PC["g_ffn"] + c:PC["g_ffn"] + c + 1])
            bodies("w_pq")

            def best(values, left, o_values, o_indices, n):
                for i in range(n):
                    link.post(dve.max(o_values(i)[:, 0:8], values(i)))
                link.wait()
                for i in range(n):
                    link.post(dve.max_index(o_indices(i)[:, 0:8], o_values(i)[:, 0:8], values(i)))
                    link.post(dve.match_replace(left(i), o_values(i)[:, 0:8], values(i), -3.0e38))
                link.wait()
                for i in range(n):
                    link.post(dve.max(o_values(i)[:, 8:16], left(i)))
                link.wait()
                for i in range(n):
                    link.post(dve.max_index(o_indices(i)[:, 8:16], o_values(i)[:, 8:16], left(i)))
                link.wait()

            dve.wait_ge(sem("scores_out"), 2)
            workk = pqT[:, :, :].rearrange("p c s -> p (c s)").rearrange("p (i n) -> p i n", n=NK)
            best(lambda i: score[:, i, :], lambda i: workk[:, i, :], lambda i: topv[:, i, :], lambda i: topi[:, i, :],
                 TT * 2 * PH)
            v = topv[:, :, :].rearrange("p (g h) k -> p g h k", h=2)
            G = TT * PH
            for tt in range(TT):
                g = slice(tt * PH, (tt + 1) * PH)
                link.post(dve.tensor_tensor(cand[:, g, :, :],
                                            v[:, g, 0, :].unsqueeze(3).to_broadcast([P, PH, TOPK, TOPK]),
                                            v[:, g, 1, :].unsqueeze(2).to_broadcast([P, PH, TOPK, TOPK]), ALU.add))
            link(dve.tensor_copy(topf[:, :, :], topi[:, :, :]))
            left = score[:, :, :].rearrange("p c s -> p (c s)").rearrange("p (i n) -> p i n", n=TOPK * TOPK)
            best(lambda i: cand[:, i, :, :].rearrange("p x y -> p (x y)"), lambda i: left[:, i, :],
                 lambda i: pick[:, i, :], lambda i: seli[:, i, :], G)
            link.post(dve.tensor_scalar(selh[:, 0, :, :], seli[:, :, :], 4, None, ALU.logical_shift_right))
            link(dve.tensor_scalar(selh[:, 1, :, :], seli[:, :, :], 15, None, ALU.bitwise_and))
            link(dve.tensor_copy(self_[:, :, :, :], selh[:, :, :, :]))
            link(dve.tensor_tensor(selh[:, 0, :, :].bitcast(F32), pick[:, :, :],
                                   pick[:, :, 0:1].to_broadcast([P, G, TOPK]), ALU.subtract))
            dve.tensor_copy(pick[:, :, :], selh[:, 0, :, :].bitcast(F32)).then_inc(sem("pick_shifted"), 1)
            f = topf[:, :, :].rearrange("p (g h) k -> p g h k", h=2)
            match = pqT[:, :, :].rearrange("p c s -> p (c s)").rearrange("p (i x y) -> p i x y", x=TOPK, y=TOPK)
            sixteen = cc[:, CC["iota16"]:CC["iota16"] + TOPK]
            for h in range(2):
                link(dve.tensor_tensor(match, sixteen.unsqueeze(1).unsqueeze(1).to_broadcast([P, G, TOPK, TOPK]),
                                       self_[:, h, :, :].unsqueeze(3).to_broadcast([P, G, TOPK, TOPK]), ALU.is_equal))
                link(dve.tensor_tensor(match, match, f[:, :, h, :].unsqueeze(2).to_broadcast([P, G, TOPK, TOPK]), ALU.mult))
                link(dve.tensor_reduce(slots[:, h, :, :], match, AX.X, ALU.add))
            dve.wait_ge(sem("pick_exp"), 1)
            link(dve.tensor_reduce(rsum[:, :], pick[:, :, :], AX.X, ALU.add))
            link(dve.reciprocal(rsum[:, :], rsum[:, :]))
            dve.tensor_tensor(slots[:, 2, :, :], pick[:, :, :], rsum[:, :].unsqueeze(2).to_broadcast([P, G, TOPK]),
                              ALU.mult).then_inc(sem("slots_done"), 1)
            dve.wait_ge(sem("silu_c_done"), 1)
            dve.wait_ge(sem("slot_gate_high"), 1)
            dve.tensor_tensor(slot_gate[:, 1, :], PS[:, 4, 0:S], slot_gate[:, 0, :].bitcast(F32), ALU.subtract)\
                .then_inc(sem("route_over"), 1)
            dve.wait_ge(sem("route_over"), 2)
            dve.sem_inc(sem("ada_used"), 3)
            dve.sem_inc(sem("gates_applied"), 2)
            dve.sem_inc(sem("gated"), 2)

            def key_rows(n, n_before, base, width, r):
                dve.wait_ge(sem("gates_spread"), n + (n_before + 1))

                def match(o, first, w, row):
                    keys = cc[:, CC["iota"] + first:CC["iota"] + first + w].unsqueeze(1).to_broadcast([P, 8, w])
                    return dve.tensor_tensor(o, keys, slotsT[:, row, ds(8 * n, 8)].unsqueeze(2).to_broadcast([P, 8, w]),
                                             ALU.is_equal)

                match(hot2[width][:, r, :, 0:width], base, width, 1).then_inc(sem("keys_matched"), 1)
                match(hot1[:, r, :, :], 0, NK, 0).then_inc(sem("hot1_done"), 1)

            def ada_product(seg, k, q, buffer, acc):
                dve.wait_ge(sem(f"ada_loaded{q}"), 16 * k + 16 * (16 * seg + 1))
                dve.wait_ge(sem("ada_used"), 3 * k + (48 * seg + q + 1))
                dve.scalar_tensor_tensor(acc[:, q, :], buffer[:, q, :], silu_c[:, ds(k, 1)], acc[:, q, :],
                                         ALU.mult, ALU.add).then_inc(sem("ada_used"), 1)

            def gates_onto_first(n, r):
                dve.wait_ge(sem("gates_out"), n + 3)
                x = hid0[:, :, ds(8 * n, 8)]
                dve.tensor_tensor(x, x, PS[:, 4 + r, :].rearrange("p (t b) -> p b t", t=8)[:, 0:EB, :], ALU.mult)\
                    .then_inc(sem("gates_applied"), 1)

            for r in range(2):
                key_rows(r, 0, 0, 2 * EB, r)
            with dve.Fori(0, 15) as j:
                for r in range(2):
                    key_rows(2 * j + (2 + r), 0, 0, 2 * EB, r)
                    gates_onto_first(2 * j + r, r)
            for r in range(2):
                gates_onto_first(30 + r, r)
            dve.wait_ge(sem("gates_applied"), 34)
            dve.wait_ge(lo_done, 4 * (FIRST_BODY["down0"] + 1))

            for quarter in range(QUARTERS):
                up, down = f"up{quarter}", f"down{quarter}"
                if quarter:
                    link(dve.memset(ada_acc[:, 1, :, :], 0.0))
                    with dve.Fori(0, 16) as j:
                        for u in range(4):
                            b = u // 2
                            if u % 2 == 0 and quarter < QUARTERS - 1:
                                key_rows(2 * j + b, 32 * quarter, (quarter + 1) * EB, EB, b)
                            low(j + (FIRST_BODY[up] + 1), u)
                            if u % 2 == 1:
                                i = 2 * j + b
                                dve.wait_ge(act_free, i + (2 + ACT_BLOCKS[up] + 1))
                                x = one(hid[quarter % 2], i)
                                dve.tensor_tensor(x, x, geluT[:, b, :], ALU.mult).then_inc(sem("gated"), 1)
                            if u:
                                ada_product(2 * quarter - 1, j, u - 1, ada, ada_acc[:, 1, :, :])
                    dve.wait_ge(sem("gated"), EB * quarter + 2)
                link(dve.memset(ada_acc[:, 0, :, :], 0.0))
                source = lambda k: one(hid[quarter % 2], k)
                for s in range(2):
                    stage(source, s, s, down)
                with dve.Fori(0, 15) as j:
                    for u in range(4):
                        low(j + (FIRST_BODY[down] + 1), u)
                        if u % 2 == 1:
                            stage(source, 2 * j + (2 + u // 2), u // 2, down)
                        if u:
                            ada_product(2 * quarter, j, u - 1, ada, ada_acc[:, 0, :, :])
                for u in range(4):
                    low(FIRST_BODY[down] + 16, u)
                    if u:
                        ada_product(2 * quarter, 15, u - 1, ada, ada_acc[:, 0, :, :])
                dve.wait_ge(tile_used, 4 * (FIRST_BODY[down] + 16))
                add_product(sem("x2_done"))
                dve.wait_ge(sem("x2_done"), quarter + 1)
                dve.wait_ge(sem("ada_summed"), quarter + 1)
                for layer in range(2 if quarter else 1):
                    m = 48 * layer + 12 * (quarter - layer)
                    last = dve.tensor_tensor(mod[:, m:m + 12], PS[:, 7, 12 * layer:12 * layer + 12],
                                             pc[:, PC["ada_b"] + m:PC["ada_b"] + m + 12], ALU.add)
                    if layer == 0 and quarter:
                        link.post(last)
                last.then_inc(sem("mod_done"), 1)
            dve.wait_ge(sem("mod_done"), 4)
            dve.tensor_scalar(mod[:, 16:48], mod[:, 16:48], 1.0, None, ALU.add).then_inc(sem("mod_done"), 1)
            dve.wait_ge(sem("rms_root"), 4)
            link(dve.reciprocal(stat[:, 12:14], stat[:, 2:4]))
            dve.wait_ge(sem("row_loaded"), 16)
            for tt in range(TT):
                last = dve.scalar_tensor_tensor(X[:, tt, :], X[:, tt, :], stat[:, 12 + tt:13 + tt], row[:, :],
                                                ALU.mult, ALU.mult)
            last.then_inc(sem("x3_done"), 1)
            dve.wait_ge(sem("mod_done"), 5)
            turned(2, lambda c: mod[:, 16 + c:17 + c], lambda c: mod[:, c:c + 1])

            dve.wait_ge(sem("dt_product"), 1)
            hp = slice(0, SHEADS)
            link(dve.tensor_scalar(dts[:, 4, :], PS[hp, 2, 0:S], pc[hp, PC["dt_bias"]:PC["dt_bias"] + 1], None, ALU.add))
            dve.scalar_tensor_tensor(dts[:, 3, :], dts[:, 4, :], -1.0, dts[:, 4, :], ALU.mult, ALU.min).then_inc(sem("dt_abs"), 1)
            dve.wait_ge(sem("dt_exp"), 2)
            softplus(dts[:, 0, :], dts[:, 4, :], dts[:, 3, :], dts[:, 5, :], dts[:, 6, :], dts[:, 7, :])
            link(dve.tensor_scalar(stat[hp, 13:14], stat[hp, 12:13], -1.0, None, ALU.mult))
            link(dve.tensor_scalar(dts[:, 5, :], dts[:, 0, :], stat[hp, 13:14], None, ALU.mult))
            link(dve.memset(dts[:, 6, :], 1.0))
            link(dve.tensor_tensor_scan(dts[:, 2, :], dts[:, 6, :], dts[:, 5, :], 0.0, ALU.mult, ALU.add))
            dve.tensor_copy(dts[:, 1, :], dts[:, 2, :]).then_inc(sem("decay_done"), 1)

            with dve.Fori(0, NB["xbc"]) as j:
                link.loop(j, 8)
                for b in range(2):
                    i = 2 * j + b
                    dve.wait_ge(tile_used, 4 * j + (4 * FIRST_BODY["xbc"] + 2 * b + 2))
                    dve.wait_ge(sem("conv_read"), i + 1)
                    convolve(cbuf[:, b, :], PS[:, b, 0:S], lambda t: pc[:, ds(4 * i + (PC["a_conv_w"] + t), 1)], 3)
                    dve.sem_inc(dve_free, 1)
                    dve.sem_inc(sem("conv_done"), 1)
            link.end(NB["xbc"])

            dve.wait_ge(sem("ssd_ready"), 1)
            dve.sem_inc(sem("xd_done"), 1)
            dve.sem_inc(sem("mixed"), 2)
            dve.sem_inc(sem("y_added"), 2)
            dve.sem_inc(sem("y_gated"), 2)
            dve.wait_ge(lo_done, 4 * (FIRST_BODY["z"] + 1))
            link(dve.memset(ada_acc_z[:, :, :], 0.0))
            with dve.Fori(0, SG) as g:
                dve.wait_ge(sem("xs_turned"), g + 2)
                dve.wait_ge(sem("y_product"), 8 * g + 2)
                for tt in range(TT):
                    dve.tensor_tensor(xd[:, tt, :].rearrange("p (h d) -> p h d", d=64),
                                      PS[:, tt, :].rearrange("p (h d) -> p h d", d=64),
                                      dtn[:, tt, ds(8 * g, 8)].unsqueeze(2).to_broadcast([P, 8, 64]), ALU.mult)\
                        .then_inc(sem("xd_done"), 1)
                dve.wait_ge(sem("cb_done"), g + 2)

                def add(k):
                    c = 4 * g + k // 2
                    dve.wait_ge(sem("y_product"), 8 * g + (k + 4))
                    dve.scalar_tensor_tensor(one(xbc, c), one(xbc, c), pc[:, ds(c + PC["skip"], 1)],
                                             PS[:, 5 + (k // 2) % 2, 0:S], ALU.mult, ALU.add)\
                        .then_inc(sem("y_added"), 1)
                    dve.wait_ge(act_free, c + (2 + ACT_BLOCKS["z"] + 1))
                    dve.wait_ge(sem("y_added"), c + 3)
                    dve.tensor_tensor(one(xbc, c), one(xbc, c), zt[:, (k // 2) % 2, :], ALU.mult)\
                        .then_inc(sem("y_gated"), 1)

                for k in range(8):
                    dve.wait_ge(sem("decays_read"), 8 * g + (k + 3))
                    dve.wait_ge(sem("y_product"), 8 * g + (k + 1))
                    dve.tensor_tensor(mm_[:, k % 2, :], ex[:, k % 2, :], cbm[:, :], ALU.mult).then_inc(sem("mixed"), 1)
                    low(2 * g + (FIRST_BODY["z"] + k // 4 + 1), k % 4)
                    if k % 4:
                        ada_product(7, 2 * g + k // 4, k % 4 - 1, ada_z, ada_acc_z)
                    if k in (2, 4, 6):
                        add(k - 2)
                add(6)
            dve.wait_ge(sem("y_gated"), XC + 2)
            dve.wait_ge(sem("ada_summed"), QUARTERS + 1)
            b = PC["ada_b"] + 84
            dve.tensor_tensor(mod[:, 84:96], PS[:, 3, 0:12], pc[:, b:b + 12], ALU.add).then_inc(sem("mod_done"), 1)
            dve.wait_ge(sem("mod_done"), 6)
            dve.tensor_scalar(mod[:, 64:96], mod[:, 64:96], 1.0, None, ALU.add).then_inc(sem("mod_done"), 1)
            dve.sem_inc(sem("ssd_normed"), 1)
            with dve.Fori(0, SG) as g:
                link.loop(g, 1)
                dve.wait_ge(sem("group_root"), g + 2)
                link(dve.reciprocal(rg[:, 1, :], rg[:, 0, :]))
                for c in range(4):
                    i = 4 * g + c
                    last = dve.scalar_tensor_tensor(one(xbc, i), one(xbc, i), pc[:, ds(i + PC["norm_g"], 1)], rg[:, 1, :],
                                                    ALU.mult, ALU.mult)
                last.then_inc(sem("ssd_normed"), 1)
            link.end(SG)
            dve.wait_ge(sem("ssd_normed"), SG + 1)
            rows_bodies("a_out", lambda k: one(xbc, k))

            def layer_norm(n, signal):
                for tt in range(TT):
                    last = dve.tensor_copy(Y[:, tt, :], banks(4 * tt, 4))
                    if tt == 0:
                        link.post(last)
                last.then_inc(sem("y_copied"), 1)
                dve.wait_ge(sem("y_copied"), n + 1)
                for c in range(KC):
                    if c >= 2:
                        dve.wait_ge(sem("gate_spread"), KC * n + c - 1)
                    dve.tensor_scalar(dcol[:, c % 2, :], ident, mod[:, 48 * n + 32 + c:48 * n + 33 + c], None, ALU.mult)\
                        .then_inc(sem("dcol_done"), 1)
                dve.wait_ge(sem("gate_rows_done"), n + 1)
                for tt in range(TT):
                    link(dve.tensor_tensor(Y[:, tt, :], Y[:, tt, :], rows[:, 0, :], ALU.mult))
                    dve.scalar_tensor_tensor(X[:, tt, :], X[:, tt, :], ALPHA, Y[:, tt, :], ALU.mult, ALU.add)\
                        .then_inc(sem("ln_in"), 1)
                for tt in range(TT):
                    dve.wait_ge(sem("ln_sum"), TT * n + tt + 1)
                    link(dve.tensor_scalar(stat[:, 2 + tt:3 + tt], stat[:, tt:tt + 1], -1.0 / D, None, ALU.mult))
                    dve.wait_ge(sem("ln_in"), TT * n + tt + 1)
                    dve.tensor_scalar(X[:, tt, :], X[:, tt, :], stat[:, 2 + tt:3 + tt], None, ALU.add)\
                        .then_inc(sem("ln_centred"), 1)
                dve.wait_ge(sem("ln_root"), n + 1)
                link(dve.reciprocal(stat[:, 8:10], stat[:, 6:8]))
                dve.wait_ge(sem("ln_rows_loaded"), 32 * (n + 1))
                for tt in range(TT):
                    dve.wait_ge(sem("ln_centred"), TT * n + tt + 1)
                    link(dve.scalar_tensor_tensor(X[:, tt, :], X[:, tt, :], stat[:, 8 + tt:9 + tt], rows[:, 1, :],
                                                  ALU.mult, ALU.mult))
                    last = dve.tensor_tensor(X[:, tt, :], X[:, tt, :], rows[:, 2, :], ALU.add)
                    if tt == 0:
                        link.post(last)
                last.then_inc(signal, 1)

            layer_norm(0, sem("x4_done"))
            turned(3, lambda c: 1.0)
            bodies("k2")
            bodies("v2")
            turned(4, lambda c: mod[:, 64 + c:65 + c], lambda c: mod[:, 48 + c:49 + c])
            bodies("q2")
            bodies("z2")

            dve.wait_ge(sem("distances_loaded"), 16)
            dve.wait_ge(sem("z2_out"), 1)
            dve.sem_inc(sem("dist_added"), 1)
            dve.sem_inc(sem("head_out"), 1)
            with dve.Fori(0, DH) as h:
                link.loop(h, 9)
                dve.wait_ge(sem("head_scored"), h + 2)
                dve.wait_ge(sem("head_out"), h + 1)
                for g in range(DG):
                    slope = cd[:, ds(3 * h + (CD["slopes"] + g), 1)]
                    link.post(dve.scalar_tensor_tensor(sc2[:, g * P:(g + 1) * P], cd[:, CD["d0"] + g * P:CD["d0"] + (g + 1) * P],
                                                       slope, PS[:, 0, g * P:(g + 1) * P], ALU.mult, ALU.add))
                for g in range(DG):
                    slope = cd[:, ds(3 * h + (CD["slopes"] + g), 1)]
                    o = 384 + g * S
                    last = dve.scalar_tensor_tensor(sc2[:, o:o + S], cd[:, CD["d1"] + g * S:CD["d1"] + (g + 1) * S],
                                                    slope, PS[:, 1 + g // 2, (g % 2) * S:(g % 2 + 1) * S],
                                                    ALU.mult, ALU.add)
                    if g < DG - 1:
                        link.post(last)
                last.then_inc(sem("dist_added"), 1)
                dve.wait_ge(sem("dist_added"), h + 2)
                link.post(dve.tensor_reduce(sm2[:, 0:1], sc2[:, 0:384], AX.X, ALU.max))
                link(dve.tensor_reduce(sm2[:, 1:2], sc2[:, 384:1152], AX.X, ALU.max))
                dve.tensor_scalar(sm2[:, 2:4], sm2[:, 0:2], -1.0, None, ALU.mult).then_inc(sem("head_max"), 1)
                dve.wait_ge(sem("head_exp"), h + 1)
                link(dve.reciprocal(sm2[:, 6:8], sm2[:, 4:6]))
                dve.wait_ge(sem("head_product"), h + 1)
                for tt in range(TT):
                    z = zn[:, tt, ds(h * P, P)]
                    last = dve.scalar_tensor_tensor(z, PS[:, 6 + tt, 0:P], sm2[:, 6 + tt:7 + tt], z, ALU.mult, ALU.mult)
                    if tt == 0:
                        link.post(last)
                last.then_inc(sem("head_out"), 1)
            link.end(DH)
            dve.wait_ge(sem("oT_done"), 1)
            rows_bodies("b_out", lambda k: one(oT, k))
            layer_norm(1, sem("out_ready"))


def lay_out(i):
    f = np.float32
    c = np.ascontiguousarray

    def columns(v):
        return v.reshape(-1, P).T

    def blocks(w):
        n = w.shape[1] // P
        return c(w.reshape(2, 8, P, n, P).transpose(3, 0, 2, 1, 4)).reshape(2 * n, P, TILE)

    w_in = i["w_in"][0]
    q_end, kv_end = QC, QC + KVC
    a_in = i["a_in_w_2"][0]
    o = {}
    o["x"] = c(i["x"].reshape(TT, P, D).transpose(1, 0, 2))
    o["q"] = c(w_in[:, :q_end]).reshape(KC, P, TILE)
    o["kv"] = c(w_in[:, q_end:kv_end].reshape(8, 2, P, 512).transpose(0, 2, 1, 3)).reshape(8, P, TILE)
    o["gate"] = blocks(w_in[:, kv_end:kv_end + LRU])
    o["rec"] = blocks(w_in[:, kv_end + LRU:])
    o["w_out"] = c(i["w_out"][0]).reshape(KC, P, D)
    o["w_pq"] = blocks(i["w_pq"][0])
    u = i["u_emb"][0].reshape(NK, NK, 2, 8, P)
    o["u_emb"] = c(u.transpose(1, 2, 4, 3, 0)).reshape(2 * NK, P, TILE)
    v = i["v_emb"][0].reshape(NK, NK, 2, TILE)
    o["v_emb"] = c(v.transpose(1, 2, 0, 3)).reshape(2 * NK, P, TILE)
    o["xbc"] = blocks(a_in[:, DI:DI + BC * P])
    o["z"] = blocks(a_in[:, :DI])
    o["w_dt"] = c(a_in[:, DI + BC * P:].reshape(KC, P, SHEADS).transpose(1, 0, 2))
    o["a_out"] = c(i["a_out_w_2"][0]).reshape(XC, P, D)
    kv = i["kv_w_2"]
    W = DG * DH * P
    o["k2"] = blocks(kv[:, :W])
    o["v2"] = c(kv[:, W:].reshape(KC, P, DG, TILE).transpose(2, 0, 1, 3)).reshape(DG * KC, P, TILE)
    b_in = i["b_in_w_2"][0]
    o["q2"] = blocks(b_in[:, :W])
    o["z2"] = c(b_in[:, W:]).reshape(KC, P, TILE)
    o["b_out"] = c(i["b_out_w_2"][0]).reshape(DH, P, D)
    ada = i["ada_w_2"].reshape(2, KC, P, 4, 3, ADA)
    o["ada_w"] = c(ada.transpose(3, 0, 1, 4, 2, 5)).reshape(-1, P, ADA)
    o["gate_w"] = c(np.stack([i[n][0].reshape(LC, 2, 64, 64).transpose(1, 2, 0, 3)
                              for n in ("fwd_wa", "fwd_wx", "bwd_wa", "bwd_wx")]))
    sk = np.stack([i["sub_k1"][0], i["sub_k2"][0]], 1)
    o["skT"] = c(sk.reshape(2 * PH, NK, P).transpose(2, 0, 1))
    o["sink"] = c(i["sink"][0].reshape(NKV, 2, 2).transpose(0, 2, 1)).reshape(NQ)
    o["rows"] = c(np.stack([i["g_final"], i["ln_g_2"][0], i["ln_b_2"][0], i["ln_g_2"][1], i["ln_b_2"][1]]))

    pc = np.zeros((P, PC.n), f)

    def put(name, v):
        pc[:v.shape[0], PC[name]:PC[name] + v.shape[1]] = v

    put("g_mix", columns(i["g_mix"][0]))
    put("g_ffn", columns(i["g_ffn"][0]))
    put("g_attn", columns(i["g_attn_out"][0]))
    put("g_lru", columns(i["g_lru_out"][0]))
    put("conv_w", i["conv_w"][0].reshape(4, LC, P).transpose(2, 1, 0).reshape(P, -1))
    put("conv_b", columns(i["conv_b"][0]))
    put("gate_b", np.concatenate([columns(i[n][0]) for n in ("fwd_ba", "fwd_bx", "bwd_ba", "bwd_bx")], 1))
    put("lam", np.concatenate([columns(i[n][0]) for n in ("fwd_lam", "bwd_lam")], 1))
    put("ada_b", columns(i["ada_b_2"].reshape(-1)))
    put("cond", columns(i["c_2"][0]))
    put("a_conv_w", i["a_conv_w_2"][0].reshape(4, BC, P).transpose(2, 1, 0).reshape(P, -1))
    put("a_conv_b", columns(i["a_conv_b_2"][0]))
    put("norm_g", columns(i["a_norm_g_2"][0]))
    put("skip", columns(np.repeat(i["a_D_2"][0], 64)))
    put("dt_bias", i["a_dt_bias_2"][0][:, None])
    put("a_log", i["a_A_log_2"][0][:, None])
    for name, value in (("eps", EPS), ("ln_eps", LN_EPS), ("tiny", 1e-30)):
        pc[:, PC[name]] = value
    o["pc"] = pc

    cc = np.zeros((P, CC.n), f)
    cc[:, CC["ident"]:CC["ident"] + P] = np.eye(P)
    cc[:, CC["ones"]:CC["ones"] + P] = 1
    cc[:, CC["iota"]:CC["iota"] + P] = np.arange(P)
    cc[:, CC["iota16"]:CC["iota16"] + TOPK] = np.arange(TOPK)
    o["cc"] = cc
    half = HD // 2
    inv = (f(10000.0) ** (-np.arange(half, dtype=f) / f(half))).astype(f)
    ang = (np.arange(S, dtype=f)[:, None] * inv[None]).astype(f)
    pos = np.arange(S)
    cw = np.zeros((P, CW.n), f)
    window = np.where(np.abs(pos[None] - pos[:, None]) <= 128, 0, NEG).astype(f)
    for name, t in (("cos", np.cos(ang)), ("sin", np.sin(ang)), ("window", window)):
        w = t.shape[1] * TT
        cw[:, CW[name]:CW[name] + w] = t.reshape(TT, P, -1).transpose(1, 0, 2).reshape(P, -1)
    o["cw"] = cw
    o["causal"] = np.where(pos[None, :P] >= pos[:P, None], 0, NEG).astype(f)
    far = pos[:, None] - pos[None]
    cd = np.zeros((P, CD.n), f)
    for g, (window, step) in enumerate(((128, 1), (512, 4), (2048, 16))):
        d = np.where((far >= 0) & (far <= window) & (far % step == 0), far, -NEG).astype(f)
        cd[:, CD["d0"] + g * P:CD["d0"] + (g + 1) * P] = d[:P, :P]
        cd[:, CD["d1"] + g * S:CD["d1"] + (g + 1) * S] = d[P:, :]
    n = DG * DH
    slopes = (2.0 ** (-8.0 * np.arange(1, n + 1) / n)).reshape(DG, DH).T.reshape(-1)
    cd[:, CD["slopes"]:CD["slopes"] + n] = -slopes.astype(f)
    o["cd"] = cd
    return o


def kernel(**inputs):
    import concourse.bacc as bacc
    from concourse.bass_utils import run_bass_kernel_spmd

    arrays = lay_out({k: np.asarray(v) for k, v in inputs.items()})
    nc = bacc.Bacc("TRN2", target_bir_lowering=False, num_devices=1)
    aps = {k: nc.dram_tensor(f"in_{k}", v.shape, F32, kind="ExternalInput").ap() for k, v in arrays.items()}
    out = nc.dram_tensor("out", (P, TT, D), F32, kind="ExternalOutput").ap()
    build(nc, aps, out)
    got = run_bass_kernel_spmd(nc, [{f"in_{k}": v for k, v in arrays.items()}], core_ids=[0])
    y = got.results[0]["out"]
    return np.ascontiguousarray(y.transpose(1, 0, 2)).reshape(1, S, D)
```

```python
from contextlib import ExitStack

import numpy as np

import concourse.bass as bass
from concourse import mybir

ALU = mybir.AluOpType
ACT = mybir.ActivationFunctionType
AX = mybir.AxisListType
F32 = mybir.dt.float32
F32R = mybir.dt.float32r
BF16 = mybir.dt.bfloat16
U32 = mybir.dt.uint32
ds = bass.ds

P = 128
S = 256
TT = S // P
D = 2048
KC = D // P
TILE = 1024
EPS = 1e-6
LN_EPS = 1e-5
ALPHA = 4.0 ** 0.25

NQ, HD, NKV = 16, 64, 4
QC = NQ * HD
KVC = 2 * NKV * HD
LRU = 1024
LC = LRU // P
PH = 8
NK = 128
TOPK = 16
QUARTERS = 4
EB = NK // QUARTERS
ADA = 512
DI = 4096
SG, SN, SHEADS = 8, 128, 64
XC = DI // P
BC = XC + 2 * SG
DG, DH = 3, 8

NEG = -1e30


class Columns:

    def __init__(self):
        self.at, self.n = {}, 0

    def add(self, name, width):
        self.at[name] = self.n
        self.n += width

    def __getitem__(self, name):
        return self.at[name]


PC = Columns()
for _name, _w in [
    ("g_mix", KC), ("g_ffn", KC), ("g_attn", LC), ("g_lru", LC),
    ("conv_w", 4 * LC), ("conv_b", LC), ("gate_b", 4 * LC), ("lam", 2 * LC),
    ("ada_b", 96), ("cond", KC), ("a_conv_w", 4 * BC), ("a_conv_b", BC),
    ("norm_g", XC), ("skip", XC), ("dt_bias", 1), ("a_log", 1),
    ("eps", 1), ("ln_eps", 1), ("tiny", 1),
]:
    PC.add(_name, _w)
CC = Columns()
for _name, _w in [("ident", P), ("ones", P), ("iota", P), ("iota16", TOPK)]:
    CC.add(_name, _w)
CW = Columns()
for _name, _w in [("cos", TT * 32), ("sin", TT * 32), ("window", TT * S)]:
    CW.add(_name, _w)
CD = Columns()
for _name, _w in [("d0", DG * P), ("d1", DG * S), ("slopes", DG * DH)]:
    CD.add(_name, _w)

STREAM = [
    ("q", 4), ("kv", 2), ("gate", 4), ("rec", 4), ("w_out", 8), ("w_pq", 8),
    ("up0", 16), ("down0", 16), ("up1", 16), ("down1", 16),
    ("up2", 16), ("down2", 16), ("up3", 16), ("down3", 16),
    ("xbc", 24), ("z", 16), ("a_out", 16), ("k2", 12), ("v2", 12), ("q2", 12), ("z2", 4), ("b_out", 4),
]
FIRST_BODY = {}
BODIES = 0
for _name, _n in STREAM:
    FIRST_BODY[_name] = BODIES
    BODIES += _n
NB = dict(STREAM)


class Chain:

    def __init__(self, eng, sem):
        self.eng, self.sem, self.n = eng, sem, 0
        self.offset = None

    def __call__(self, instruction):
        self.post(instruction)
        self.wait()

    def post(self, instruction):
        instruction.then_inc(self.sem, 1)
        self.n += 1

    def wait(self, back=0):
        n = self.n - back
        self.eng.wait_ge(self.sem, n if self.offset is None else self.offset + n)

    def loop(self, j, per):
        self.start, self.per = self.n, per
        self.offset = j * per

    def end(self, trips):
        assert self.n - self.start == self.per, (self.n - self.start, self.per)
        self.n = self.start + self.per * trips
        self.offset = None


def build(nc, a, out):
    ctx = ExitStack()
    with ctx:
        def psum(name, shape, dt=F32):
            return ctx.enter_context(nc.psum_tensor(name, shape, dt))

        def sb(name, shape, dt=F32, group=None):
            return (group or ctx).enter_context(nc.sbuf_tensor(name, shape, dt))

        names = {}

        def sem(name):
            if name not in names:
                names[name] = ctx.enter_context(nc.semaphore(name))
            return names[name]

        PS = psum("PS", [P, 8, 512])

        X = sb("X", [P, TT, D])
        for_hh, for_pT2 = ExitStack(), ExitStack()
        hh = sb("hh", [P, 2, LC, S], F32, for_hh)
        for_hh.close()
        pT2 = sb("pT2", [P, 9, P], F32, for_pT2)
        for_pT2.close()
        xt_hi = sb("xt_hi", [P, KC, S], F32R)
        xt_lo = sb("xt_lo", [P, KC, S], F32R)
        raw = sb("raw", [P, 4, TILE])
        w_hi = sb("w_hi", [P, 4, TILE], F32R)
        w_lo = sb("w_lo", [P, 4, TILE], F32R)
        st_hi = sb("st_hi", [P, 2, S], F32R)
        st_lo = sb("st_lo", [P, 2, S], F32R)
        cc = sb("cc", [P, CC.n])
        pc = sb("pc", [P, PC.n])
        diag = sb("diag", [P, TT, P])
        xtmp = sb("xtmp", [P, 2, S])
        stat = sb("stat", [P, 16])
        silu_c = sb("silu_c", [P, KC])
        gate_part = sb("gate_part", [P, 2, 2, KC], F32R)
        ones_r = sb("ones_r", [P, P], F32R)
        mod = sb("mod", [P, 96])
        ident = cc[:, CC["ident"]:CC["ident"] + P]
        ones = cc[:, CC["ones"]:CC["ones"] + P]

        mixer = ExitStack()
        yT = sb("yT", [P, KC, S], F32, mixer)
        gateT = sb("gateT", [P, LC, S], F32, mixer)
        convT = sb("convT", [P, LC, S], F32, mixer)
        wbd = sb("wbd", [P, 4, LC, P], F32, mixer)
        spl = sb("spl", [P, 8, 2 * LC], F32, mixer)
        attn = ExitStack()
        cw = sb("cw", [P, CW.n], F32, attn)
        qn = sb("qn", [P, TT, QC], F32, attn)
        kvn = sb("kvn", [P, TT, KVC], F32, attn)
        kdup = sb("kdup", [P, TT, NKV, 2, HD], F32, attn)
        qT = sb("qT", [P, QC // P, S], F32, attn)
        kT = sb("kT", [P, NKV, S], F32, attn)
        sc = sb("sc", [P, 2, 4, S], F32, attn)
        pr = sb("pr", [P, 4, S], F32, attn)
        pT = sb("pT", [P, 8, P], F32, attn)
        yn = qn
        rtmp = sc
        sinkb = sb("sinkb", [P, NQ], F32, attn)
        sm = sb("sm", [P, 8, 2, 4], F32, attn)
        attn.close()
        lru = ExitStack()
        rr = sb("rr", [P, 2, LC, S], F32, lru)
        ii = sb("ii", [P, 2, LC, S], F32, lru)
        aa = sb("aa", [P, 2, LC, S], F32, lru)
        rstdb = sb("rstdb", [P, 2, S], F32, lru)
        lru.close()
        mixer.close()

        peer = ExitStack()
        slotsT = sb("slotsT", [P, 2, S], BF16, peer)
        slot_gate = sb("slot_gate", [P, 3, S], BF16, peer)
        iota_b = sb("iota_b", [P, NK], BF16, peer)
        hid0 = sb("hid0", [P, EB, S], F32, peer)
        route = ExitStack()
        pqT = sb("pqT", [P, 2 * PH, S], F32, route)
        score = sb("score", [P, TT * 2 * PH, NK], F32, route)
        topv = sb("topv", [P, TT * 2 * PH, TOPK], F32, route)
        topi = sb("topi", [P, TT * 2 * PH, TOPK], U32, route)
        topf = sb("topf", [P, TT * 2 * PH, TOPK], F32, route)
        cand = sb("cand", [P, TT * PH, TOPK, TOPK], F32, route)
        skT = cand[:, 0:PH, :, :].rearrange("p g x y -> p (g x y)").rearrange("p (i n) -> p i n", n=NK)
        pick = sb("pick", [P, TT * PH, TOPK], F32, route)
        seli = sb("seli", [P, TT * PH, TOPK], U32, route)
        selh = sb("selh", [P, 2, TT * PH, TOPK], U32, route)
        self_ = sb("self_", [P, 2, TT * PH, TOPK], F32, route)
        slots = sb("slots", [P, 3, TT * PH, TOPK], F32, route)
        rsum = sb("rsum", [P, TT * PH], F32, route)
        route.close()
        experts = ExitStack()
        hid1 = sb("hid1", [P, EB, S], F32, experts)
        hid = [hid0, hid1]
        hot1 = sb("hot1", [P, 2, 8, NK], BF16, experts)
        hot2, hot2_gate = {}, {}
        hot2[EB] = sb("hot2_one", [P, 2, 8, EB], BF16, experts)
        hot2_gate[EB] = sb("hot2_gate_one", [P, 2, 3, 8, EB], BF16, experts)
        ada = sb("ada", [P, 3, ADA], F32, experts)
        two_quarters = ExitStack()
        hot2[2 * EB] = sb("hot2_two", [P, 2, 8, 2 * EB], BF16, two_quarters)
        hot2_gate[2 * EB] = sb("hot2_gate_two", [P, 2, 3, 8, 2 * EB], BF16, two_quarters)
        two_quarters.close()
        ada_acc = sb("ada_acc", [P, 2, 3, ADA], F32, experts)
        geluT = xtmp
        experts.close()
        final = ExitStack()
        row = sb("row", [P, D], F32, final)
        final.close()
        peer.close()

        ssd = ExitStack()
        xbc = sb("xbc", [P, BC, S], F32, ssd)
        spreading = ExitStack()
        gate_diag = sb("gate_diag", [P, 2, D], F32R, spreading)
        spreading.close()
        cbuf = sb("cbuf", [P, 2, S], F32, ssd)
        w_dt = sb("w_dt", [P, KC, SHEADS], F32, ssd)
        causal = sb("causal", [P, P], F32, ssd)
        causal_b = sb("causal_b", [P, P], BF16, ssd)
        ident_b = sb("ident_b", [P, P], BF16, ssd)
        dts = sb("dts", [SHEADS, 3, S], F32, ssd)
        step = ExitStack()
        dtt = sb("dtt", [SHEADS, 5, S], F32, step)
        step.close()
        decay_part = sb("decay_part", [SHEADS, 2, S + P], F32R, ssd)
        zt = sb("zt", [P, 2, S], F32, ssd)
        dtn = sb("dtn", [P, TT, SHEADS], F32, ssd)
        nacn = sb("nacn", [P, TT, SHEADS], F32, ssd)
        xs_st = sb("xs_st", [P, 4, S], F32, ssd)
        b_st = sb("b_st", [P, S], F32, ssd)
        pick_h = sb("pick_h", [SHEADS, 8, P], F32R, ssd)
        xd = sb("xd", [P, TT, 512], F32, ssd)
        cbm = sb("cbm", [P, 384], F32, ssd)
        ex = sb("ex", [P, 2, 384], F32, ssd)
        roots = ExitStack()
        rg = sb("rg", [P, SG * S], F32, roots)
        roots.close()
        ada_z = sb("ada_z", [P, 3, ADA], F32, ssd)
        ada_acc_z = sb("ada_acc_z", [P, 3, ADA], F32, ssd)
        mm_ = sb("mm_", [P, 2, 384], F32, ssd)
        sq = [xs_st[:, :, :], xd[:, :, :].rearrange("p t n -> p (t n)").rearrange("p (c s) -> p c s", s=S)]
        ssd.close()
        norms = ExitStack()
        Y = sb("Y", [P, TT, D], F32, norms)
        rows = sb("rows", [P, 2, D], F32, norms)
        norms.close()
        dil = ExitStack()
        k2T = sb("k2T", [P, DG * DH, S], F32, dil)
        v2n = sb("v2n", [P, TT, DG * DH * P], F32, dil)
        q2T = sb("q2T", [P, DG * DH, S], F32, dil)
        zn = sb("zn", [P, TT, DH * P], F32, dil)
        cd = sb("cd", [P, CD.n], F32, dil)
        q_st = sb("q_st", [P, DG, S], F32, dil)
        sc2 = sb("sc2", [P, 2, 9 * P], F32, dil)
        sm2 = sb("sm2", [P, 2, 8], F32, dil)
        dil.close()
        oT = k2T

        raw_loaded = [sem(f"raw_loaded{u}") for u in range(4)]
        hi_done, lo_done, tile_used = sem("hi_done"), sem("lo_done"), sem("tile_used")
        stage_hi_done, stage_lo_done = sem("stage_hi_done"), sem("stage_lo_done")
        consts_loaded, x_loaded, params_loaded = sem("consts_loaded"), sem("x_loaded"), sem("params_loaded")
        xt_turned, xt_hi_done, xt_lo_done = sem("xt_turned"), sem("xt_hi_done"), sem("xt_lo_done")
        act_free, dve_free = sem("act_free"), sem("dve_free")
        ACT_BLOCKS = {"gate": 0, "w_pq": 8, "up0": 24, "up1": 56, "up2": 88, "up3": 120, "z": 152, "k2": 184, "q2": 208}
        DVE_BLOCKS = {"rec": 0, "xbc": 8}
        CHUNKS = {"w_out": 0, "down0": 16, "down1": 48, "down2": 80, "down3": 112, "a_out": 144, "b_out": 176}
        z_bank = (7, 2)
        dve_link, pool_link = sem("dve_link"), sem("pool_link")

        block = ctx.enter_context(nc.Block())

        def one(tensor, i):
            return tensor[:, ds(i, 1), :].rearrange("p a s -> p (a s)")

        def tile_source(name, j, u):
            if name in ("w_out", "a_out", "b_out"):
                return a[name][2 * j + u // 2][:, (u % 2) * TILE:(u % 2 + 1) * TILE]
            if name[:-1] in ("up", "down"):
                return a[("u" if name[:-1] == "up" else "v") + "_emb"][4 * j + (2 * EB * int(name[-1]) + u)]
            return a[name][4 * j + u]

        @block.sync
        def _(sp):
            sp.dma_start(X[:, :, :], a["x"]).then_inc(x_loaded, 16)
            sp.dma_start(cc[:, :], a["cc"]).then_inc(consts_loaded, 16)
            sp.dma_start(pc[:, :], a["pc"]).then_inc(params_loaded, 16)

            def weight(name, j, u):
                first = name == STREAM[0][0] and type(j) is int
                if not first:
                    sp.wait_ge(lo_done, 4 * (j + FIRST_BODY[name]) + u - 3)
                sp.dma_start(raw[:, u, :], tile_source(name, j, u)).then_inc(raw_loaded[u], 16)

            for name, n in STREAM:
                start = 0
                if name == STREAM[0][0]:
                    for u in range(4):
                        weight(name, 0, u)
                    start = 1
                with sp.Fori(start, n) as j:
                    for u in range(4):
                        weight(name, j, u)
            sp.wait_ge(sem("half_normed"), 2)
            sp.dma_start(out[:, 0, :], X[:, 0, :]).then_inc(sem("stored"), 16)
            sp.wait_ge(sem("out_ready"), 1)
            sp.dma_start(out[:, 1, :], X[:, 1, :]).then_inc(sem("stored"), 16)
            sp.wait_ge(sem("stored"), 32)

        @block.gpsimd
        def _(pool):
            pool.dma_start(cw[:, :], a["cw"]).then_inc(sem("window_loaded"), 16)
            pool.dma_start(sinkb[:, :], a["sink"].partition_broadcast(P)).then_inc(sem("window_loaded"), 16)
            pool.memset(wbd[:, :, :, :], 0.0).then_inc(sem("bd_zero"), 1)
            pool.wait_ge(sem("bd_zero"), 1)
            for kind in range(4):
                for half in range(2):
                    pool.dma_start(wbd[64 * half:64 * half + 64, kind, :, 64 * half:64 * half + 64],
                                   a["gate_w"][kind, half]).then_inc(sem("bd_loaded"), 16)
            link = Chain(pool, pool_link)
            pool.wait_ge(sem("window_loaded"), 32)
            pool.wait_ge(sem("qkv_out"), 2)
            flat = rtmp[:, :, :, :].rearrange("p a b s -> p (a b s)")
            for tt in range(TT):
                def angles(name, shape):
                    return cw[:, CW[name] + tt * 32:CW[name] + tt * 32 + 32].unsqueeze(1).to_broadcast(shape)

                for src, heads, outs in (
                    (qn[:, tt, :], NQ, [qn[:, tt, :].rearrange("p (h d) -> p h d", d=HD)]),
                    (kvn[:, tt, 0:NKV * HD], NKV, [kdup[:, tt, :, r, :] for r in range(2)]),
                ):
                    x = src.rearrange("p (h d) -> p h d", d=HD)
                    n = heads * 32
                    tmp = [flat[:, i * n:(i + 1) * n].rearrange("p (h d) -> p h d", d=32) for i in range(4)]
                    cos, sin = angles("cos", [P, heads, 32]), angles("sin", [P, heads, 32])
                    link.post(pool.tensor_tensor(tmp[0], x[:, :, 0:32], cos, ALU.mult))
                    link.post(pool.tensor_tensor(tmp[1], x[:, :, 32:64], sin, ALU.mult))
                    link.post(pool.tensor_tensor(tmp[2], x[:, :, 32:64], cos, ALU.mult))
                    link(pool.tensor_tensor(tmp[3], x[:, :, 0:32], sin, ALU.mult))
                    for o in outs:
                        link.post(pool.tensor_tensor(o[:, :, 0:32], tmp[0], tmp[1], ALU.subtract))
                        link(pool.tensor_tensor(o[:, :, 32:64], tmp[2], tmp[3], ALU.add))
            pool.sem_inc(sem("rope_done"), 1)
            pool.wait_ge(sem("x1_done"), 1)
            pool.dma_start(skT, a["skT"]).then_inc(sem("keys_loaded"), 16)

            def low(body, u):
                pool.wait_ge(hi_done, 4 * body + u + 1)
                pool.tensor_tensor(w_lo[:, u, :], raw[:, u, :], w_hi[:, u, :].bitcast(F32), ALU.subtract)\
                    .then_inc(lo_done, 1)

            def lows(name):
                pool.wait_ge(lo_done, 4 * (FIRST_BODY[name] + 1))
                with pool.Fori(0, NB[name]) as j:
                    for u in range(4):
                        low(j + (FIRST_BODY[name] + 1), u)

            lows("up0")
            pool.wait_ge(sem("route_over"), 2)

            def slot_gates(n, n_before, width, r):
                shape = [P, 2, 8, width]
                pool.wait_ge(sem("keys_matched"), n + (n_before + 1))
                pool.tensor_tensor(hot2_gate[width][:, r, 1:3, :, :],
                                   hot2[width][:, r, :, 0:width].unsqueeze(1).to_broadcast(shape),
                                   slot_gate[:, 1:3, ds(8 * n, 8)].unsqueeze(3).to_broadcast(shape),
                                   ALU.mult).then_inc(sem("hot2_done"), 1)

            def ada_tiles(seg, k, buffer):
                for q in range(3):
                    pool.wait_ge(sem("ada_used"), 3 * k + (48 * seg + q + 1))
                    pool.dma_start(buffer[:, q, :], a["ada_w"][3 * k + (48 * seg + q)])\
                        .then_inc(sem(f"ada_loaded{q}"), 16)

            with pool.Fori(0, 16) as j:
                for r in range(2):
                    slot_gates(2 * j + r, 0, 2 * EB, r)
            for quarter in range(QUARTERS):
                if quarter:
                    with pool.Fori(0, 16) as k:
                        ada_tiles(2 * quarter - 1, k, ada)
                        if quarter < QUARTERS - 1:
                            for r in range(2):
                                slot_gates(2 * k + r, 32 * quarter, EB, r)
                with pool.Fori(0, 16) as k:
                    ada_tiles(2 * quarter, k, ada)
            pool.wait_ge(sem("x2_done"), QUARTERS)
            pool.dma_start(row[:, :], a["rows"][0].partition_broadcast(P)).then_inc(sem("row_loaded"), 16)
            pool.wait_ge(sem("x3_done"), 1)
            pool.dma_start(w_dt[:, :, :], a["w_dt"]).then_inc(sem("w_dt_loaded"), 16)
            pool.dma_start(causal[:, :], a["causal"]).then_inc(sem("w_dt_loaded"), 16)
            lows("xbc")
            pool.wait_ge(sem("ssd_ready"), 1)
            with pool.Fori(0, SG) as g:
                pool.wait_ge(sem("xs_turned"), g + 1)
                pool.tensor_copy(xs_st[:, :, :], xbc[:, ds(4 * g, 4), :]).then_inc(sem("xs_staged"), 1)
                pool.wait_ge(sem("cb_product"), g + 1)
                pool.tensor_copy(b_st[:, :], one(xbc, g + XC)).then_inc(sem("b_staged"), 1)
                pool.wait_ge(sem("group_done"), g + 1)
                pool.tensor_copy(pick_h[:, :, :], cc[0:SHEADS, ds(8 * g + CC["ident"], 8)].unsqueeze(2)
                                 .to_broadcast([SHEADS, 8, P])).then_inc(sem("heads_staged"), 1)
                for i in range(2):
                    ada_tiles(7, 2 * g + i, ada_z)
            with pool.Fori(0, SG // 2) as j:
                for r in range(2):
                    pool.wait_ge(sem("group_squared"), 2 * j + r + 1)
                    pool.tensor_tensor(sq[r][:, 0:2, :], sq[r][:, 0:2, :], sq[r][:, 2:4, :], ALU.add)\
                        .then_inc(sem("pairs_summed"), 1)
                    pool.wait_ge(sem("pairs_summed"), 2 * j + r + 1)
                    pool.tensor_tensor(sq[r][:, 0, :], sq[r][:, 0, :], sq[r][:, 1, :], ALU.add)\
                        .then_inc(sem("chunks_summed"), 1)

            def norm_operands(n):
                for part in range(2):
                    pool.tensor_tensor(gate_diag[:, part, :].rearrange("p (c k) -> p c k", k=P),
                                       ident.unsqueeze(1).to_broadcast([P, KC, P]),
                                       gate_part[:, n, part, :].bitcast(F32).unsqueeze(2).to_broadcast([P, KC, P]),
                                       ALU.mult).then_inc(sem("gates_diagonal"), 1)
                pool.wait_ge(sem("y_copied"), n + 1)
                for r in range(2):
                    pool.dma_start(rows[:, r, :], a["rows"][1 + 2 * n + r].partition_broadcast(P))\
                        .then_inc(sem("ln_rows_loaded"), 16)

            pool.wait_ge(sem("group_root"), 1)
            pool.wait_ge(sem("gates_split"), 1)
            norm_operands(0)
            pool.wait_ge(sem("x4_done"), 1)
            pool.dma_start(cd[:, :], a["cd"]).then_inc(sem("distances_loaded"), 16)
            pool.wait_ge(act_free, 2 + ACT_BLOCKS["q2"] + 24)
            with pool.Fori(0, DH) as h:
                pool.wait_ge(sem("head_scored"), h + 1)
                pool.tensor_copy(q_st[:, :, :],
                                 q2T[:, :, :].rearrange("p (g h) s -> p g h s", g=DG)[:, :, ds(h, 1), :]
                                 .rearrange("p g o s -> p g (o s)")).then_inc(sem("q_staged"), 1)
            pool.wait_ge(sem("q_staged"), DH)
            norm_operands(1)

        @block.tensor
        def _(pe):
            def three(o, w_h, w_l, x_h, x_l, start, stop):
                pe.matmul(o, w_h, x_h, start=start, stop=False, skip_group_check=True)
                pe.matmul(o, w_h, x_l, start=False, stop=False, skip_group_check=True)
                return pe.matmul(o, w_l, x_h, start=False, stop=stop, skip_group_check=True)

            def block_product(name, j, b, o):
                for h in range(2):
                    u = 2 * b + h
                    pe.wait_ge(lo_done, 4 * j + (4 * FIRST_BODY[name] + u + 1))
                    for k in range(8):
                        w = slice(k * P, k * P + P)
                        last = three(o, w_hi[:, u, w], w_lo[:, u, w], xt_hi[:, 8 * h + k, :], xt_lo[:, 8 * h + k, :],
                                     h == 0 and k == 0, h == 1 and k == 7)
                    last.then_inc(tile_used, 1)

            def channel_blocks(name, free, before):
                with pe.Fori(0, NB[name]) as j:
                    for b in range(2):
                        pe.wait_ge(free, 2 * j + before + b + 1)
                        block_product(name, j, b, PS[:, b, 0:S])

            def token_columns(tiles, body0, bank0, kpt):
                n = 16 // kpt
                for i in range(n):
                    pe.wait_ge(lo_done, tiles + (body0 * 4 + i + 1))
                    for kk in range(kpt):
                        k = i * kpt + kk
                        for tt in range(TT):
                            for g in range(2 // kpt):
                                c = (kk if kpt == 2 else g) * 512
                                o = PS[:, bank0 + tt * (2 // kpt) + g, :]
                                t = slice(tt * P, tt * P + P)
                                u = i % 4
                                pe.matmul(o, xt_hi[:, k, t], w_hi[:, u, c:c + 512], start=k == 0, stop=False)
                                pe.matmul(o, xt_lo[:, k, t], w_hi[:, u, c:c + 512], start=False, stop=False)
                                last = pe.matmul(o, xt_hi[:, k, t], w_lo[:, u, c:c + 512],
                                                 start=False, stop=k == KC - 1)
                    last.then_inc(tile_used, 1)

            def rows_body(name, j, first, stop):
                for u in range(4):
                    pe.wait_ge(lo_done, 4 * (j + FIRST_BODY[name]) + u + 1)
                    s = u // 2
                    if u % 2 == 0:
                        pe.wait_ge(stage_lo_done, 2 * j + CHUNKS[name] + s + 1)
                    for tt in range(TT):
                        for g in range(2):
                            o = PS[:, tt * 4 + (u % 2) * 2 + g, :]
                            t, c = slice(tt * P, tt * P + P), slice(g * 512, g * 512 + 512)
                            pe.matmul(o, st_hi[:, s, t], w_hi[:, u, c], start=first and s == 0, stop=False,
                                      skip_group_check=True)
                            pe.matmul(o, st_lo[:, s, t], w_hi[:, u, c], start=False, stop=False,
                                      skip_group_check=True)
                            last = pe.matmul(o, st_hi[:, s, t], w_lo[:, u, c], start=False, stop=stop and s == 1,
                                             skip_group_check=True)
                    last.then_inc(tile_used, 1)

            def all_rows(name):
                rows_body(name, 0, True, False)
                if NB[name] > 2:
                    with pe.Fori(1, NB[name] - 1) as j:
                        rows_body(name, j, False, False)
                rows_body(name, NB[name] - 1, False, True)

            def turn(n, by=None):
                for c in range(KC):
                    if c >= 8:
                        pe.wait_ge(xt_lo_done, KC * n + c - 7)
                    for tt in range(TT):
                        o, x = PS[:, c % 8, tt * P:tt * P + P], X[:, tt, c * P:c * P + P]
                        if by:
                            last = pe.matmul(o, x, by(tt), start=True, stop=True)
                        else:
                            last = pe.transpose(o, x, ident)
                    last.then_inc(xt_turned, 1)

            pe.wait_ge(consts_loaded, 16)
            pe.wait_ge(x_loaded, 16)
            pe.wait_ge(sem("diag_done"), 1)
            turn(0, lambda tt: diag[:, tt, :])
            pe.wait_ge(xt_lo_done, KC)
            token_columns(0, FIRST_BODY["q"], 0, 1)
            token_columns(0, FIRST_BODY["kv"], 4, 2)
            pe.wait_ge(sem("qkv_out"), 2)
            channel_blocks("gate", act_free, ACT_BLOCKS["gate"])
            pe.wait_ge(act_free, 2 + ACT_BLOCKS["gate"] + 8)
            channel_blocks("rec", dve_free, DVE_BLOCKS["rec"])

            pe.wait_ge(dve_free, 2 + DVE_BLOCKS["rec"] + 8)
            pe.wait_ge(sem("rope_done"), 1)
            for tt in range(TT):
                for c in range(QC // P):
                    pe.transpose(PS[:, c // 2, (c % 2) * S + tt * P:(c % 2) * S + tt * P + P],
                                 qn[:, tt, c * P:c * P + P], ident)
                for g in range(NKV):
                    last = pe.transpose(PS[:, 4 + g // 2, (g % 2) * S + tt * P:(g % 2) * S + tt * P + P],
                                        kdup[:, tt, g, :, :].rearrange("p a d -> p (a d)"), ident)
            last.then_inc(sem("qk_turned"), 1)

            steps = [(tt, g) for tt in range(TT) for g in range(NKV)]

            def scores(n):
                tt, g = steps[n]
                if n >= 2:
                    pe.wait_ge(sem("scores_read"), n - 1)
                for i in range(2):
                    for par in range(2):
                        h = slice(64 * par, 64 * par + 64)
                        last = pe.matmul(PS[:, 2 * (n % 2) + par, i * S:i * S + S],
                                         qT[h, 2 * g + i, tt * P:tt * P + P], kT[h, g, :], start=True, stop=True)
                last.then_inc(sem("scores_done"), 1)

            pe.wait_ge(sem("qkT_done"), 2)
            scores(0)
            for n, (tt, g) in enumerate(steps):
                if n + 1 < len(steps):
                    scores(n + 1)
                pe.wait_ge(sem("probs_done"), n + 1)
                if n:
                    pe.wait_ge(sem("pT_done"), n)
                for i in range(4):
                    for kc in range(2):
                        last = pe.transpose(PS[:, 4 + i // 2, ((i % 2) * 2 + kc) * P:((i % 2) * 2 + kc + 1) * P],
                                            pr[:, i, kc * P:kc * P + P], ident)
                last.then_inc(sem("p_turned"), 1)
                pe.wait_ge(sem("pT_done"), n + 1)
                if n:
                    pe.wait_ge(sem("attn_out"), n)
                for i in range(4):
                    for kc in range(2):
                        last = pe.matmul(PS[:, 6, i * HD:i * HD + HD], pT[:, 2 * i + kc, :],
                                         kvn[:, kc, NKV * HD + g * HD:NKV * HD + g * HD + HD],
                                         start=kc == 0, stop=kc == 1, skip_group_check=True)
                last.then_inc(sem("pv_done"), 1)
            pe.wait_ge(sem("diag_done"), 2)
            for c in range(LC):
                for tt in range(TT):
                    last = pe.matmul(PS[:, c // 2, (c % 2) * S + tt * P:(c % 2) * S + tt * P + P],
                                     yn[:, tt, c * P:c * P + P], diag[:, tt, :], start=True, stop=True)
            last.then_inc(sem("y_turned"), 1)

            pe.wait_ge(sem("bd_loaded"), 128)
            pe.wait_ge(sem("y_attn_done"), 1)
            for kind in range(4):
                if kind >= 2:
                    pe.wait_ge(sem("gates_read"), kind - 1)
                for c in range(LC):
                    last = pe.matmul(PS[:, 4 * (kind % 2) + c // 2, (c % 2) * S:(c % 2) * S + S],
                                     wbd[:, kind, c, :], convT[:, c, :], start=True, stop=True)
                last.then_inc(sem("gates_done"), 1)
            pe.wait_ge(sem("lru_squared"), 1)
            for c in range(LC):
                last = pe.matmul(PS[:, 0, 0:S], ones, rr[:, 0, c, :], start=c == 0, stop=c == LC - 1)
            last.then_inc(sem("lru_summed"), 1)
            pe.wait_ge(sem("y_lru_done"), 1)
            all_rows("w_out")

            pe.wait_ge(sem("x1_done"), 1)
            pe.wait_ge(sem("diag_done"), 3)
            turn(1, lambda tt: diag[:, tt, :])
            pe.wait_ge(xt_lo_done, 2 * KC)
            channel_blocks("w_pq", act_free, ACT_BLOCKS["w_pq"])
            pe.wait_ge(sem("keys_loaded"), 16)
            pe.wait_ge(act_free, 2 + ACT_BLOCKS["w_pq"] + 16)
            for tt in range(TT):
                for i in range(2 * PH):
                    last = pe.matmul(PS[:, 4 * tt + i // 4, (i % 4) * NK:(i % 4 + 1) * NK],
                                     pqT[:, i, tt * P:tt * P + P], skT[:, i, :], start=True, stop=True)
            last.then_inc(sem("keys_scored"), 1)
            pe.wait_ge(sem("scores_out"), 2)
            channel_blocks("up0", act_free, ACT_BLOCKS["up0"])
            pe.wait_ge(sem("slots_done"), 1)
            for what in range(3):
                for tt in range(TT):
                    last = pe.transpose(PS[:, 2 + what, tt * P:tt * P + P],
                                        slots[:, what, tt * PH:(tt + 1) * PH, :].rearrange("p h k -> p (h k)"), ident)
            last.then_inc(sem("slots_turned"), 1)
            pe.wait_ge(sem("route_over"), 2)
            pe.sem_inc(sem("gates_spread"), 2)

            def spread(n, n_before, width, r):
                pe.wait_ge(sem("hot_done"), 2 * n + (2 * n_before + 2))
                pe.wait_ge(sem("hot2_done"), n + (n_before + 1))
                pe.wait_ge(sem("gates_out"), n + (n_before + 1))
                for t in range(8):
                    for part in range(3):
                        last = pe.matmul(PS[:, 4 + r, t * width:(t + 1) * width], hot1[:, r, t, :],
                                         hot2_gate[width][:, r, part, t, 0:width], start=part == 0, stop=part == 2,
                                         skip_group_check=True)
                last.then_inc(sem("gates_spread"), 1)

            with pe.Fori(0, 16) as j:
                for r in range(2):
                    pe.wait_ge(sem("gates_applied"), 2 * j + (r + 1))
                    spread(2 * j + r, 0, 2 * EB, r)
            for quarter in range(QUARTERS):
                up, down = f"up{quarter}", f"down{quarter}"
                if quarter:
                    with pe.Fori(0, 16) as j:
                        for b in range(2):
                            pe.wait_ge(act_free, 2 * j + (ACT_BLOCKS[up] + b + 1))
                            block_product(up, j, b, PS[:, b, 0:S])
                            if quarter < QUARTERS - 1:
                                spread(2 * j + b, 32 * quarter, EB, b)
                pe.wait_ge(sem("gates_applied"), 34)
                pe.wait_ge(sem("gates_out"), 2 + 32 * min(quarter + 1, 3))
                pe.wait_ge(act_free, 2 + ACT_BLOCKS[up] + EB)
                all_rows(down)
                pe.wait_ge(sem("half_added"), quarter + 2)
                pe.wait_ge(sem("ada_used"), 48 * (2 * quarter + 1) + 3)
                for layer in range(2 if quarter else 1):
                    for q in range(3):
                        for c in range(4):
                            o = 12 * layer + 4 * q + c
                            last = pe.matmul(PS[:, 3, o:o + 1], ada_acc[:, layer, q, c * P:c * P + P],
                                             ones[:, 0:1], start=True, stop=True, skip_group_check=True)
                last.then_inc(sem("ada_summed"), 1)

            pe.wait_ge(sem("x3_done"), 1)
            turn(2)
            pe.wait_ge(sem("w_dt_loaded"), 32)
            pe.wait_ge(xt_lo_done, 3 * KC)
            for k in range(KC):
                pe.matmul(PS[0:SHEADS, 2, 0:S], w_dt[:, k, :], xt_hi[:, k, :].bitcast(F32), start=k == 0, stop=False)
                last = pe.matmul(PS[0:SHEADS, 2, 0:S], w_dt[:, k, :], xt_lo[:, k, :].bitcast(F32),
                                 start=False, stop=k == KC - 1)
            last.then_inc(sem("dt_product"), 1)
            channel_blocks("xbc", dve_free, DVE_BLOCKS["xbc"])
            pe.wait_ge(sem("decay_done"), 1)
            for tt in range(TT):
                t = slice(tt * P, tt * P + P)
                pe.transpose(PS[:, 3, tt * 64:tt * 64 + 64], dts[:, 0, t], ident[0:SHEADS, 0:SHEADS])
                last = pe.transpose(PS[:, 3, P + tt * 64:P + tt * 64 + 64], dts[:, 1, t], ident[0:SHEADS, 0:SHEADS])
            last.then_inc(sem("dt_turned"), 1)
            pe.wait_ge(sem("ssd_ready"), 1)
            pe.wait_ge(sem("dtn_done"), 1)
            pe.wait_ge(dve_free, 2 + DVE_BLOCKS["xbc"] + BC)
            pe.sem_inc(sem("group_done"), 1)
            pe.sem_inc(sem("xs_turned"), 1)
            pe.sem_inc(sem("cb_product"), 1)
            pe.sem_inc(sem("y_product"), 2)
            pe.wait_ge(sem("mod_done"), 5)
            pe.wait_ge(sem("decays_low"), 2)
            with pe.Fori(0, SG) as g:
                pe.wait_ge(sem("xs_staged"), g + 1)
                pe.wait_ge(sem("xd_done"), 2 * g + 1)
                for tt in range(TT):
                    for c in range(4):
                        last = pe.transpose(PS[:, tt, c * P:c * P + P], xs_st[:, c, tt * P:tt * P + P], ident)
                last.then_inc(sem("xs_turned"), 1)
                pe.wait_ge(sem("b_staged"), g + 1)
                pe.wait_ge(sem("z_taken"), 4 * g + 2)
                pe.matmul(PS[:, 2, 0:S], b_st[:, 0:P], one(xbc, g + XC + SG),
                          start=True, stop=True, skip_group_check=True)
                pe.matmul(PS[:, 2, S:S + P], b_st[:, P:S],
                          xbc[:, ds(g + XC + SG, 1), P:S].rearrange("p a s -> p (a s)"),
                          start=True, stop=True, skip_group_check=True).then_inc(sem("cb_product"), 1)

                def decays(k):
                    pe.wait_ge(sem("decays_read"), 8 * g + k + 1)
                    o = 3 + k % 2
                    for part in range(2):
                        pe.matmul(PS[:, o, 0:S + P], pick_h[:, k, :], decay_part[:, part, :],
                                  start=part == 0, stop=False, skip_group_check=True)
                    masked = pe.matmul(PS[:, o, 0:P], ident_b[:, :], causal_b[:, :], start=False, stop=False,
                                       skip_group_check=True)
                    if k == 7:
                        masked.then_inc(sem("group_done"), 1)
                    pe.matmul(PS[:, o, S:S + P], ident_b[:, :], causal_b[:, :], start=False, stop=True,
                              skip_group_check=True).then_inc(sem("decays_spread"), 1)

                pe.wait_ge(sem("heads_staged"), g + 1)
                decays(0)
                for k in range(8):
                    h = k % 2
                    b = k // 2
                    if h == 0:
                        pe.wait_ge(sem("z_taken"), 4 * g + b + 1)
                    if k == 2:
                        pe.wait_ge(sem("cb_done"), g + 2)
                    pe.wait_ge(lo_done, 8 * g + (4 * FIRST_BODY["z"] + k + 1))
                    o = PS[:, z_bank[b % 2], 0:S]
                    for kk in range(8):
                        w = slice(kk * P, kk * P + P)
                        last = three(o, w_hi[:, k % 4, w], w_lo[:, k % 4, w],
                                     xt_hi[:, 8 * h + kk, :], xt_lo[:, 8 * h + kk, :],
                                     h == 0 and kk == 0, h == 1 and kk == 7)
                    last.then_inc(tile_used, 1)
                    if k < 7:
                        decays(k + 1)
                    if k == 0:
                        pe.wait_ge(sem("xd_done"), 2 * g + 3)
                    pe.wait_ge(sem("mixed"), 8 * g + k + 3)
                    if k % 2 == 0:
                        pe.wait_ge(sem("y_added"), 4 * g + k // 2 + 1)
                    h = slice(64 * (k % 2), 64 * (k % 2) + 64)
                    o = 5 + (k // 2) % 2
                    pe.matmul(PS[h, o, 0:S], xd[:, 0, k * 64:k * 64 + 64], mm_[:, k % 2, 0:S], start=True, stop=False,
                              skip_group_check=True)
                    pe.matmul(PS[h, o, P:S], xd[:, 1, k * 64:k * 64 + 64], mm_[:, k % 2, S:S + P],
                              start=False, stop=True, skip_group_check=True).then_inc(sem("y_product"), 1)
            pe.wait_ge(sem("ada_used"), 48 * 8 + 3)
            for q in range(3):
                for c in range(4):
                    last = pe.matmul(PS[:, 3, 4 * q + c:4 * q + c + 1], ada_acc_z[:, q, c * P:c * P + P],
                                     ones[:, 0:1], start=True, stop=True, skip_group_check=True)
            last.then_inc(sem("ada_summed"), 1)
            pe.wait_ge(sem("mod_done"), 7)
            with pe.Fori(0, SG // 2) as j:
                for r in range(2):
                    pe.wait_ge(sem("chunks_summed"), 2 * j + r + 1)
                    pe.matmul(PS[:, ds(j + 3, 1), r * S:r * S + S].rearrange("p a s -> p (a s)"), ones, sq[r][:, 0, :],
                              start=True, stop=True, skip_group_check=True).then_inc(sem("group_summed"), 1)
            pe.wait_ge(sem("group_root"), 1)
            all_rows("a_out")

            def gate_rows(n):
                pe.wait_ge(sem("gates_diagonal"), 2 * n + 2)
                pe.wait_ge(sem("y_copied"), n + 1)
                for g in range(4):
                    for part in range(2):
                        last = pe.matmul(PS[:, g, :], ones_r[:, :], gate_diag[:, part, g * 512:(g + 1) * 512],
                                         start=part == 0, stop=part == 1)
                last.then_inc(sem("gate_spread"), 1)

            gate_rows(0)

            pe.wait_ge(sem("x4_done"), 1)
            turn(3)
            pe.wait_ge(xt_lo_done, 4 * KC)
            channel_blocks("k2", act_free, ACT_BLOCKS["k2"])
            pe.wait_ge(act_free, 2 + ACT_BLOCKS["k2"] + 24)
            with pe.Fori(0, DG) as g:
                pe.wait_ge(sem("v2_out"), g + 1)
                token_columns(16 * g, FIRST_BODY["v2"], 0, 1)
            pe.wait_ge(sem("v2_out"), DG + 1)
            turn(4)
            pe.wait_ge(xt_lo_done, 5 * KC)
            channel_blocks("q2", act_free, ACT_BLOCKS["q2"])
            token_columns(0, FIRST_BODY["z2"], 4, 1)
            pe.wait_ge(sem("z2_out"), 1)
            pe.sem_inc(sem("head_scored"), 1)
            pe.sem_inc(sem("head_turned"), 2)

            def head_scores(h):
                pe.wait_ge(sem("q_staged"), h + 1)
                pe.wait_ge(sem("dist_added"), h + 1)
                for g in range(DG):
                    pe.matmul(PS[:, 0, g * P:g * P + P], q_st[:, g, 0:P],
                              k2T[:, ds(h + g * DH, 1), 0:P].rearrange("p a s -> p (a s)"),
                              start=True, stop=True, skip_group_check=True)
                    last = pe.matmul(PS[:, 1 + g // 2, (g % 2) * S:(g % 2) * S + S], q_st[:, g, P:S],
                                     one(k2T, h + g * DH),
                                     start=True, stop=True, skip_group_check=True)
                last.then_inc(sem("head_scored"), 1)

            def head_values(h, r):
                pe.wait_ge(sem("head_exp"), h + 1)
                for i in range(9):
                    last = pe.transpose(PS[:, 3 + i // 4, (i % 4) * P:(i % 4 + 1) * P], sc2[:, r, i * P:i * P + P], ident)
                last.then_inc(sem("head_turned"), 1)
                pe.wait_ge(sem("pT2_done"), h + 1)
                pe.wait_ge(sem("head_out"), h + 1)
                for g in range(DG):
                    pe.matmul(PS[:, 6, 0:P], pT2[:, g, :], v2n[:, 0, ds(h * P + g * 1024, P)],
                              start=g == 0, stop=g == DG - 1, skip_group_check=True)
                for g in range(DG):
                    for kt in range(2):
                        last = pe.matmul(PS[:, 7, 0:P], pT2[:, 3 + 2 * g + kt, :],
                                         v2n[:, kt, ds(h * P + g * 1024, P)],
                                         start=g == 0 and kt == 0, stop=g == DG - 1 and kt == 1,
                                         skip_group_check=True)
                last.then_inc(sem("head_product"), 1)

            head_scores(0)
            with pe.Fori(0, DH // 2 - 1) as j:
                for r in range(2):
                    head_scores(2 * j + (r + 1))
                    head_values(2 * j + r, r)
            head_scores(DH - 1)
            for r in range(2):
                head_values(DH - 2 + r, r)
            pe.wait_ge(sem("head_out"), DH + 1)
            for c in range(DH):
                for tt in range(TT):
                    last = pe.transpose(PS[:, c // 2, (c % 2) * S + tt * P:(c % 2) * S + tt * P + P],
                                        zn[:, tt, c * P:c * P + P], ident)
            last.then_inc(sem("o_turned"), 1)
            pe.wait_ge(sem("oT_done"), 1)
            all_rows("b_out")
            gate_rows(1)

        @block.scalar
        def _(act):
            def high(body, u, first=False):
                act.wait_ge(raw_loaded[u], 16 * (body + 1))
                if not first:
                    act.wait_ge(tile_used, 4 * body + u - 3)
                act.activation(w_hi[:, u, :], raw[:, u, :], ACT.Copy).then_inc(hi_done, 1)

            def bodies(name, evac=None, start=0, n=None, last=False):
                n = NB[name] if n is None else n
                with act.Fori(start, start + n) as j:
                    for u in range(4):
                        if not last:
                            high(j + FIRST_BODY[name] + 1, u)
                        if evac and u % 2 == 1:
                            act.wait_ge(tile_used, 4 * (j + FIRST_BODY[name]) + u + 1)
                            evac(2 * j + u // 2, u // 2)

            def stage(name, source, k, s, body):
                act.wait_ge(tile_used, 4 * body + 2 * s + 2)
                act.activation(st_hi[:, s, :], source(k), ACT.Copy).then_inc(stage_hi_done, 1)

            def rows_bodies(name, source):
                f = FIRST_BODY[name]
                n = NB[name]
                act.wait_ge(tile_used, 4 * f)
                for s in range(2):
                    act.activation(st_hi[:, s, :], source(s), ACT.Copy).then_inc(stage_hi_done, 1)
                with act.Fori(0, n - 1) as j:
                    for u in range(4):
                        high(j + f + 1, u)
                        if u % 2 == 1:
                            stage(name, source, 2 * j + 2 + u // 2, u // 2, j + f)
                if name != "b_out":
                    for u in range(4):
                        high(f + n, u)

            def turned(n, scale, bias=None):
                for c in range(KC):
                    act.wait_ge(xt_turned, KC * n + c + 1)
                    act.activation(xt_hi[:, c, :], PS[:, c % 8, 0:S], ACT.Identity, scale=scale(c),
                                   bias=bias(c) if bias else 0.0).then_inc(xt_hi_done, 1)

            def root(o, i, scale, eps):
                return act.activation(o, i, ACT.Sqrt, scale=scale, bias=pc[:, PC[eps]:PC[eps] + 1])

            act.wait_ge(params_loaded, 16)
            act.wait_ge(x_loaded, 16)
            act.sem_inc(act_free, 2)
            for tt in range(TT):
                act.activation(PS[:, 0:4, :].rearrange("p b n -> p (b n)"), X[:, tt, :], ACT.Square,
                               accum_out=stat[:, tt:tt + 1]).then_inc(sem("x_squared"), 1)
                act.wait_ge(sem("x_squared"), tt + 1)
            root(stat[:, 2:4], stat[:, 0:2], 1.0 / D, "eps").then_inc(sem("rms_root"), 1)
            for u in range(4):
                high(0, u, first=True)
            turned(0, lambda c: pc[:, PC["g_mix"] + c:PC["g_mix"] + c + 1])
            act.wait_ge(sem("lam_ready"), 1)
            act.activation(spl[:, 1, :], spl[:, 1, :], ACT.Exp).then_inc(sem("lam_exp"), 1)
            with act.Fori(0, NB["q"]) as j:
                for u in range(4):
                    high(j + 1, u)
            act.wait_ge(tile_used, 16)
            for tt in range(TT):
                last = act.activation(qn[:, tt, :], PS[:, 2 * tt:2 * tt + 2, :].rearrange("p b n -> p (b n)"), ACT.Copy)
            last.then_inc(sem("qkv_out"), 1)
            bodies("kv")
            act.wait_ge(tile_used, 24)
            act.activation(kvn[:, :, :], PS[:, 4:6, :], ACT.Copy).then_inc(sem("qkv_out"), 1)
            bodies("gate", lambda i, b: act.activation(
                one(gateT, i), PS[:, b, 0:S],
                ACT.Gelu_apprx_tanh).then_inc(act_free, 1))
            bodies("rec")
            act.wait_ge(sem("qk_turned"), 1)
            act.activation(qT[:, :, :].rearrange("p c s -> p (c s)"), PS[:, 0:4, :].rearrange("p b n -> p (b n)"),
                           ACT.Copy).then_inc(sem("qkT_done"), 1)
            act.activation(kT[:, :, :].rearrange("p c s -> p (c s)"), PS[:, 4:6, :].rearrange("p b n -> p (b n)"),
                           ACT.Copy).then_inc(sem("qkT_done"), 1)
            for n in range(8):
                act.wait_ge(sem("max_done"), n + 1)
                if n:
                    act.wait_ge(sem("p_turned"), n)
                act.activation(sm[:, n, 1, :], sm[:, n, 1, :], ACT.Exp).then_inc(sem("sink_exp"), 1)
                for i in range(4):
                    last = act.activation(pr[:, i, :], sc[:, n % 2, i, :], ACT.Exp, bias=sm[:, n, 0, i:i + 1],
                                          accum_out=stat[:, 4 + 4 * (n % 2) + i:5 + 4 * (n % 2) + i])
                last.then_inc(sem("probs_done"), 1)
                act.wait_ge(sem("p_turned"), n + 1)
                if n:
                    act.wait_ge(sem("pv_done"), n)
                act.activation(pT[:, :, :].rearrange("p c s -> p (c s)"), PS[:, 4:6, :].rearrange("p b n -> p (b n)"),
                               ACT.Copy).then_inc(sem("pT_done"), 1)
            act.wait_ge(sem("attn_out"), 8)
            for tt in range(TT):
                last = act.activation(PS[:, 0:2, :].rearrange("p b n -> p (b n)"), yn[:, tt, :], ACT.Square,
                                      accum_out=stat[:, tt:tt + 1])
                last.then_inc(sem("y_squared"), 1)
                act.wait_ge(sem("y_squared"), tt + 1)
            root(stat[:, 2:4], stat[:, 0:2], 1.0 / QC, "eps").then_inc(sem("rms_root"), 1)
            act.wait_ge(sem("y_turned"), 1)
            for c in range(LC):
                g = pc[:, PC["g_attn"] + c:PC["g_attn"] + c + 1]
                last = act.activation(yT[:, c, :], PS[:, c // 2, (c % 2) * S:(c % 2) * S + S], ACT.Copy, scale=g)
            last.then_inc(sem("y_attn_done"), 1)
            act.wait_ge(sem("spl_done"), 1)
            for kind in range(4):
                act.wait_ge(sem("gates_done"), kind + 1)
                for c in range(LC):
                    b = PC["gate_b"] + kind * LC + c
                    last = act.activation((rr if kind % 2 == 0 else ii)[:, kind // 2, c, :],
                                          PS[:, 4 * (kind % 2) + c // 2, (c % 2) * S:(c % 2) * S + S],
                                          ACT.Sigmoid, bias=pc[:, b:b + 1])
                last.then_inc(sem("gates_read"), 1)
                if kind % 2 == 1:
                    act.wait_ge(sem("gates_read"), kind + 1)
                    dr = kind // 2
                    for c in range(LC):
                        act.activation(aa[:, dr, c, :], rr[:, dr, c, :], ACT.Exp, scale=spl[:, 7, dr * LC + c:dr * LC + c + 1])
                    for c in range(LC):
                        last = act.activation(rr[:, dr, c, :], rr[:, dr, c, :], ACT.Tanh,
                                              scale=spl[:, 6, dr * LC + c:dr * LC + c + 1])
                    last.then_inc(sem("decays_done"), 1)
            for dr in range(2):
                act.wait_ge(sem("one_minus_done"), dr + 1)
                act.activation(hh[:, dr, :, :], hh[:, dr, :, :], ACT.Sqrt,
                               bias=pc[:, PC["tiny"]:PC["tiny"] + 1]).then_inc(sem("root_done"), 1)
            act.wait_ge(sem("y_mixed"), 1)
            act.activation(rr[:, 0, :, :], yT[:, LC:2 * LC, :], ACT.Square).then_inc(sem("lru_squared"), 1)
            act.wait_ge(sem("lru_summed"), 1)
            root(rstdb[:, 0, :], PS[:, 0, 0:S], 1.0 / LRU, "eps").then_inc(sem("lru_root"), 1)
            act.wait_ge(sem("y_lru_done"), 1)
            rows_bodies("w_out", lambda k: one(yT, k))
            for tt in range(TT):
                act.wait_ge(sem("x1_done" if tt else "half_added"), 1)
                act.activation(PS[:, 0:4, :].rearrange("p b n -> p (b n)"), X[:, tt, :], ACT.Square,
                               accum_out=stat[:, tt:tt + 1]).then_inc(sem("x_squared"), 1)
                act.wait_ge(sem("x_squared"), 2 + tt + 1)
            root(stat[:, 2:4], stat[:, 0:2], 1.0 / D, "eps").then_inc(sem("rms_root"), 1)
            turned(1, lambda c: pc[:, PC["g_ffn"] + c:PC["g_ffn"] + c + 1])
            bodies("w_pq", lambda i, b: act.activation(
                one(pqT, i), PS[:, b, 0:S], ACT.Copy).then_inc(act_free, 1))
            act.wait_ge(sem("keys_scored"), 1)
            for tt in range(TT):
                last = act.activation(score[:, tt * 16:(tt + 1) * 16, :].rearrange("p c s -> p (c s)"),
                                      PS[:, 4 * tt:4 * tt + 4, :].rearrange("p b n -> p (b n)"), ACT.Copy)
                last.then_inc(sem("scores_out"), 1)
            act.activation(silu_c[:, :], pc[:, PC["cond"]:PC["cond"] + KC], ACT.Silu).then_inc(sem("silu_c_done"), 1)
            bodies("up0", lambda i, b: act.activation(
                one(hid0, i), PS[:, b, 0:S], ACT.Gelu_apprx_tanh).then_inc(act_free, 1))
            act.wait_ge(sem("pick_shifted"), 1)
            act.activation(pick[:, :, :], pick[:, :, :], ACT.Exp).then_inc(sem("pick_exp"), 1)
            act.wait_ge(sem("slots_turned"), 1)
            act.activation(slot_gate[:, 0, :], PS[:, 4, 0:S], ACT.Copy).then_inc(sem("slot_gate_high"), 1)
            act.activation(iota_b[:, :], cc[:, CC["iota"]:CC["iota"] + NK], ACT.Copy)
            act.activation(slotsT[:, :, :], PS[:, 2:4, 0:S], ACT.Copy).then_inc(sem("route_over"), 1)

            def gates_out(n, n_before, o, r, first):
                act.wait_ge(sem("gates_spread"), n + (n_before + 3))
                width = 2 * EB if first else EB
                src = PS[:, 4 + r, 0:8 * width].rearrange("p (t b) -> p b t", t=8)[:, width - EB:width, :]
                act.activation(o[:, :, ds(8 * n, 8)], src, ACT.Copy).then_inc(sem("gates_out"), 1)

            act.sem_inc(sem("gates_out"), 2)
            with act.Fori(0, 16) as j:
                for r in range(2):
                    gates_out(2 * j + r, 0, hid[1], r, True)
            for quarter in range(QUARTERS):
                up, down = f"up{quarter}", f"down{quarter}"
                if quarter:
                    with act.Fori(0, 16) as j:
                        for u in range(4):
                            high(j + (FIRST_BODY[up] + 1), u)
                            if u % 2 == 1:
                                b = u // 2
                                act.wait_ge(tile_used, 4 * j + (4 * FIRST_BODY[up] + u + 1))
                                act.wait_ge(sem("gated"), 2 * j + (EB * (quarter - 1) + b + 1))
                                act.activation(geluT[:, b, :], PS[:, b, 0:S], ACT.Gelu_apprx_tanh).then_inc(act_free, 1)
                                if quarter < QUARTERS - 1:
                                    gates_out(2 * j + b, 32 * quarter, hid[(quarter + 1) % 2], b, False)
                    act.wait_ge(sem("gated"), EB * quarter + 2)
                else:
                    act.wait_ge(sem("gates_applied"), 34)
                rows_bodies(down, lambda k: one(hid[quarter % 2], k))
            act.wait_ge(sem("x2_done"), QUARTERS)
            for tt in range(TT):
                act.activation(PS[:, 4:8, :].rearrange("p b n -> p (b n)"), X[:, tt, :], ACT.Square,
                               accum_out=stat[:, tt:tt + 1]).then_inc(sem("x_squared"), 1)
                act.wait_ge(sem("x_squared"), 4 + tt + 1)
            root(stat[:, 2:4], stat[:, 0:2], 1.0 / D, "eps").then_inc(sem("rms_root"), 1)
            act.wait_ge(sem("mod_done"), 5)
            turned(2, lambda c: mod[:, 16 + c:17 + c], lambda c: mod[:, c:c + 1])
            act.wait_ge(sem("dt_abs"), 1)
            act.activation(dtt[:, 0, :], dtt[:, 0, :], ACT.Exp).then_inc(sem("dt_exp"), 1)
            act.activation(stat[0:SHEADS, 12:13], pc[0:SHEADS, PC["a_log"]:PC["a_log"] + 1], ACT.Exp)\
                .then_inc(sem("dt_exp"), 1)
            act.sem_inc(sem("conv_read"), 2)
            with act.Fori(0, NB["xbc"]) as j:
                def silu(b):
                    i = 2 * j + b
                    act.wait_ge(sem("conv_done"), i + 1)
                    act.activation(one(xbc, i), cbuf[:, b, :], ACT.Silu,
                                   bias=pc[:, ds(i + PC["a_conv_b"], 1)]).then_inc(sem("conv_read"), 1)

                for u in range(4):
                    high(j + FIRST_BODY["xbc"] + 1, u)
                    if u >= 2:
                        silu(u - 2)
            act.wait_ge(sem("decay_done"), 1)
            act.activation(decay_part[:, 0, 0:S], dts[:, 2, :], ACT.Copy)
            act.activation(decay_part[:, 0, S:S + P], dts[:, 2, P:S], ACT.Copy).then_inc(sem("decays_high"), 1)
            act.activation(ident_b[:, :], ident, ACT.Copy)
            act.activation(causal_b[:, :], causal[:, :], ACT.Copy).then_inc(sem("masks_done"), 1)
            act.wait_ge(sem("dt_turned"), 1)
            act.activation(dtn[:, :, :].rearrange("p a s -> p (a s)"), PS[:, 3, 0:P], ACT.Copy)
            act.activation(nacn[:, :, :].rearrange("p a s -> p (a s)"), PS[:, 3, P:2 * P], ACT.Copy, scale=-1.0)\
                .then_inc(sem("dtn_done"), 1)
            act.wait_ge(sem("conv_read"), BC + 2)
            act.wait_ge(sem("masks_done"), 1)
            act.wait_ge(sem("dtn_done"), 1)
            act.sem_inc(sem("ssd_ready"), 1)
            act.sem_inc(sem("cb_done"), 1)
            act.sem_inc(sem("decays_read"), 2)
            with act.Fori(0, SG) as g:
                act.wait_ge(sem("cb_product"), g + 2)
                act.wait_ge(sem("mixed"), 8 * g + 2)
                act.activation(cbm[:, :], PS[:, 2, 0:384], ACT.Copy).then_inc(sem("cb_done"), 1)
                for k in range(8):
                    act.wait_ge(sem("decays_spread"), 8 * g + k + 1)
                    act.wait_ge(sem("mixed"), 8 * g + k + 1)
                    o = 3 + k % 2
                    act.activation(ex[:, k % 2, 0:S], PS[:, o, 0:S], ACT.Exp, bias=nacn[:, 0, ds(8 * g + k, 1)])
                    act.activation(ex[:, k % 2, S:384], PS[:, o, S:384], ACT.Exp, bias=nacn[:, 1, ds(8 * g + k, 1)])\
                        .then_inc(sem("decays_read"), 1)
                    high(2 * g + (FIRST_BODY["z"] + k // 4 + 1), k % 4)
                    if k % 2 == 1:
                        b = k // 2
                        act.wait_ge(tile_used, 8 * g + (4 * FIRST_BODY["z"] + k + 1))
                        act.wait_ge(sem("y_gated"), 4 * g + b + 1)
                        act.activation(zt[:, b % 2, :], PS[:, z_bank[b % 2], 0:S], ACT.Tanh, scale=0.5)\
                            .then_inc(act_free, 1)
            act.wait_ge(sem("y_gated"), XC + 2)
            act.wait_ge(sem("ssd_normed"), 1)
            act.wait_ge(sem("mod_done"), 7)
            act.activation(ones_r[:, :], ones, ACT.Copy)
            for n in range(2):
                last = act.activation(gate_part[:, n, 0, :], mod[:, 48 * n + 32:48 * n + 48], ACT.Copy)
            last.then_inc(sem("gates_high"), 1)
            act.sem_inc(sem("group_summed"), 2)
            with act.Fori(0, SG // 2) as j:
                for r in range(2):
                    act.wait_ge(sem("group_summed"), 2 * j + r + 1)
                    act.activation(sq[r], xbc[:, ds(8 * j + 4 * r, 4), :], ACT.Square)\
                        .then_inc(sem("group_squared"), 1)
            act.wait_ge(sem("group_summed"), SG + 2)
            root(rg[:, :], PS[:, 3:7, :].rearrange("p b n -> p (b n)"), 1.0 / 512, "ln_eps")\
                .then_inc(sem("group_root"), 1)
            f = FIRST_BODY["a_out"]
            act.wait_ge(tile_used, 4 * f)
            act.wait_ge(sem("ssd_normed"), 2)
            for s in range(2):
                act.activation(st_hi[:, s, :], one(xbc, s), ACT.Copy).then_inc(stage_hi_done, 1)

            def normed_body(j, group=None):
                for u in range(4):
                    high(j + (f + 1), u)
                    if u % 2 == 1:
                        if group is not None and u == 1:
                            act.wait_ge(sem("ssd_normed"), group)
                        stage("a_out", lambda k: one(xbc, k), 2 * j + (2 + u // 2), u // 2, j + f)

            with act.Fori(0, SG - 1) as g:
                normed_body(2 * g)
                normed_body(2 * g + 1, g + 3)
            normed_body(2 * SG - 2)
            for u in range(4):
                high(f + 2 * SG, u)

            def layer_norm(n, name):
                scrap = PS[:, 4:8, :].rearrange("p b n -> p (b n)")
                act.wait_ge(tile_used, 4 * (FIRST_BODY[name] + NB[name]))
                act.activation(Y[:, 1, :], scrap, ACT.Copy).then_inc(sem("y_half_copied"), 1)
                act.wait_ge(sem("y_half_copied"), n + 1)
                for tt in range(TT):
                    act.wait_ge(sem("ln_in"), TT * n + tt + 1)
                    act.activation(scrap, X[:, tt, :], ACT.Copy, accum_out=stat[:, tt:tt + 1]).then_inc(sem("ln_sum"), 1)
                    act.wait_ge(sem("ln_sum"), TT * n + tt + 1)
                for tt in range(TT):
                    act.wait_ge(sem("ln_mean"), TT * n + tt + 1)
                    act.activation(scrap, X[:, tt, :], ACT.Square, bias=stat[:, 2 + tt:3 + tt],
                                   accum_out=stat[:, 4 + tt:5 + tt]).then_inc(sem("ln_squared"), 1)
                    act.wait_ge(sem("ln_squared"), TT * n + tt + 1)
                root(stat[:, 6:8], stat[:, 4:6], 1.0 / D, "ln_eps").then_inc(sem("ln_root"), 1)

            layer_norm(0, "a_out")
            turned(3, lambda c: 1.0)
            bodies("k2", lambda i, b: act.activation(
                one(k2T, i), PS[:, b, 0:S], ACT.Copy).then_inc(act_free, 1))
            act.sem_inc(sem("v2_out"), 1)
            with act.Fori(0, DG) as g:
                for i in range(4):
                    for u in range(4):
                        high(4 * g + (FIRST_BODY["v2"] + i + 1), u)
                act.wait_ge(tile_used, 16 * g + 4 * FIRST_BODY["v2"] + 16)
                for tt in range(TT):
                    last = act.activation(v2n[:, tt, ds(g * 1024, 1024)],
                                          PS[:, 2 * tt:2 * tt + 2, :].rearrange("p b n -> p (b n)"), ACT.Copy)
                last.then_inc(sem("v2_out"), 1)
            turned(4, lambda c: mod[:, 64 + c:65 + c], lambda c: mod[:, 48 + c:49 + c])

            def queries(i, b):
                act.activation(one(q2T, i), PS[:, b, 0:S], ACT.Copy,
                               scale=float(P) ** -0.5).then_inc(act_free, 1)

            bodies("q2", queries)
            bodies("z2")
            act.wait_ge(tile_used, 4 * FIRST_BODY["b_out"])
            for tt in range(TT):
                last = act.activation(zn[:, tt, :], PS[:, 4 + 2 * tt:6 + 2 * tt, :].rearrange("p b n -> p (b n)"), ACT.Silu)
            last.then_inc(sem("z2_out"), 1)
            with act.Fori(0, DH // 2) as j:
                for r in range(2):
                    h = 2 * j + r
                    act.wait_ge(sem("head_max"), h + 1)
                    act.activation(sc2[:, r, 0:384], sc2[:, r, 0:384], ACT.Exp, bias=sm2[:, r, 2:3],
                                   accum_out=sm2[:, r, 4:5])
                    act.activation(sc2[:, r, 384:1152], sc2[:, r, 384:1152], ACT.Exp, bias=sm2[:, r, 3:4],
                                   accum_out=sm2[:, r, 5:6]).then_inc(sem("head_exp"), 1)
                    act.wait_ge(sem("head_turned"), h + 3)
                    act.activation(pT2[:, 0:8, :].rearrange("p c s -> p (c s)"),
                                   PS[:, 3:5, :].rearrange("p b n -> p (b n)"), ACT.Copy)
                    act.activation(pT2[:, 8, :], PS[:, 5, 0:P], ACT.Copy).then_inc(sem("pT2_done"), 1)
            act.wait_ge(sem("o_turned"), 1)
            act.activation(oT[:, 0:DH, :].rearrange("p c s -> p (c s)"), PS[:, 0:4, :].rearrange("p b n -> p (b n)"),
                           ACT.Copy).then_inc(sem("oT_done"), 1)
            act.wait_ge(sem("oT_done"), 1)
            rows_bodies("b_out", lambda k: one(oT, k))
            layer_norm(1, "b_out")

        @block.vector
        def _(dve):
            link = Chain(dve, dve_link)

            def low(body, u):
                dve.wait_ge(hi_done, 4 * body + u + 1)
                dve.tensor_tensor(w_lo[:, u, :], raw[:, u, :], w_hi[:, u, :].bitcast(F32), ALU.subtract)\
                    .then_inc(lo_done, 1)

            def bodies(name, evac=None):
                with dve.Fori(0, NB[name]) as j:
                    if evac:
                        link.loop(j, evac.links * 2)
                    for u in range(4):
                        low(j + FIRST_BODY[name] + 1, u)
                        if evac and u % 2 == 1:
                            dve.wait_ge(tile_used, 4 * j + (4 * FIRST_BODY[name] + u + 1))
                            evac(2 * j + u // 2, u // 2)
                if evac:
                    link.end(NB[name])

            def stage(source, k, s, name):
                dve.wait_ge(stage_hi_done, k + (CHUNKS[name] + 1))
                dve.tensor_tensor(st_lo[:, s, :], source(k), st_hi[:, s, :].bitcast(F32), ALU.subtract)\
                    .then_inc(stage_lo_done, 1)

            def rows_bodies(name, source):
                for s in range(2):
                    stage(source, s, s, name)
                with dve.Fori(0, NB[name] - 1) as j:
                    for u in range(4):
                        low(j + (FIRST_BODY[name] + 1), u)
                        if u % 2 == 1:
                            stage(source, 2 * j + (2 + u // 2), u // 2, name)
                if name != "b_out":
                    for u in range(4):
                        low(FIRST_BODY[name] + NB[name], u)
                dve.wait_ge(tile_used, 4 * (FIRST_BODY[name] + NB[name]))

            def banks(first, n):
                return PS[:, first:first + n, :].rearrange("p b n -> p (b n)")

            def turned(n, scale, bias=None):
                if not bias:
                    for c in range(KC):
                        dve.wait_ge(xt_hi_done, KC * n + c + 1)
                        dve.scalar_tensor_tensor(xt_lo[:, c, :], PS[:, c % 8, 0:S], scale(c),
                                                 xt_hi[:, c, :].bitcast(F32), ALU.mult, ALU.subtract)\
                            .then_inc(xt_lo_done, 1)
                    return

                def shifted(c):
                    dve.wait_ge(xt_hi_done, KC * n + c + 1)
                    if c >= 2:
                        dve.wait_ge(xt_lo_done, KC * n + c - 1)
                    link.post(dve.tensor_scalar(xtmp[:, c % 2, :], PS[:, c % 8, 0:S], scale(c), bias(c),
                                                ALU.mult, ALU.add))

                shifted(0)
                for c in range(KC):
                    if c + 1 < KC:
                        shifted(c + 1)
                    link.wait(1 if c + 1 < KC else 0)
                    dve.tensor_tensor(xt_lo[:, c, :], xtmp[:, c % 2, :], xt_hi[:, c, :].bitcast(F32), ALU.subtract)\
                        .then_inc(xt_lo_done, 1)

            def row_norms(n):
                dve.wait_ge(sem("rms_root"), n)
                link(dve.reciprocal(stat[:, 12:14], stat[:, 2:4]))
                for tt in range(TT):
                    last = dve.tensor_scalar(diag[:, tt, :], ident, stat[:, 12 + tt:13 + tt], None, ALU.mult)
                last.then_inc(sem("diag_done"), 1)

            def softplus(o, x, e, t1, t2, t3):
                link(dve.tensor_scalar(t1, e, 2.0, None, ALU.add))
                link(dve.reciprocal(t1, t1))
                link(dve.tensor_tensor(t1, t1, e, ALU.mult))
                link(dve.tensor_tensor(t2, t1, t1, ALU.mult))
                link(dve.tensor_scalar(t3, t2, 1.0 / 17, None, ALU.mult))
                for n in range(15, 1, -2):
                    link(dve.scalar_tensor_tensor(t3, t3, 1.0 / n, t2, ALU.add, ALU.mult))
                link(dve.scalar_tensor_tensor(t3, t3, 1.0, t1, ALU.add, ALU.mult))
                link(dve.tensor_scalar(t1, x, 0.0, None, ALU.max))
                link(dve.scalar_tensor_tensor(o, t3, 2.0, t1, ALU.mult, ALU.add))

            def convolve(o, src, weight, centre):
                link(dve.tensor_scalar(o, src, weight(centre), None, ALU.mult))
                for t in range(4):
                    d = t - centre
                    if d < 0:
                        link(dve.scalar_tensor_tensor(o[:, -d:S], src[:, 0:S + d], weight(t), o[:, -d:S], ALU.mult, ALU.add))
                    if d > 0:
                        link(dve.scalar_tensor_tensor(o[:, 0:S - d], src[:, d:S], weight(t), o[:, 0:S - d], ALU.mult, ALU.add))

            dve.sem_inc(dve_free, 2)
            dve.wait_ge(consts_loaded, 16)
            dve.wait_ge(params_loaded, 16)
            row_norms(1)
            for u in range(4):
                low(0, u)
            turned(0, lambda c: pc[:, PC["g_mix"] + c:PC["g_mix"] + c + 1])
            lam = pc[:, PC["lam"]:PC["lam"] + 2 * LC]
            link(dve.tensor_scalar(spl[:, 0, :], lam, -1.0, None, ALU.mult))
            dve.scalar_tensor_tensor(spl[:, 1, :], lam, -1.0, lam, ALU.mult, ALU.min).then_inc(sem("lam_ready"), 1)
            dve.wait_ge(sem("lam_exp"), 1)
            softplus(spl[:, 5, :], spl[:, 0, :], spl[:, 1, :], spl[:, 2, :], spl[:, 3, :], spl[:, 4, :])
            link(dve.tensor_scalar(spl[:, 6, :], spl[:, 5, :], 8.0, None, ALU.mult))
            dve.tensor_scalar(spl[:, 7, :], spl[:, 5, :], -8.0, None, ALU.mult).then_inc(sem("spl_done"), 1)
            for name in ("q", "kv", "gate"):
                bodies(name)

            def recurrent(i, b):
                convolve(one(convT, i), PS[:, b, 0:S], lambda t: pc[:, ds(4 * i + (PC["conv_w"] + t), 1)], 2)
                link(dve.tensor_scalar(one(convT, i), one(convT, i), pc[:, ds(i + PC["conv_b"], 1)], None, ALU.add))
                dve.sem_inc(dve_free, 1)

            recurrent.links = 5
            bodies("rec", recurrent)

            steps = [(tt, g) for tt in range(TT) for g in range(NKV)]

            def maxima(n):
                tt, g = steps[n]
                dve.wait_ge(sem("scores_done"), n + 1)
                if n >= 2:
                    dve.wait_ge(sem("probs_done"), n - 1)
                window = cw[:, CW["window"] + tt * S:CW["window"] + (tt + 1) * S].unsqueeze(1).to_broadcast([P, 4, S])
                dve.scalar_tensor_tensor(sc[:, n % 2, :, :], banks(2 * (n % 2), 2).rearrange("p (h s) -> p h s", s=S),
                                         HD ** -0.5, window, ALU.mult, ALU.add).then_inc(sem("scores_read"), 1)
                dve.wait_ge(sem("scores_read"), n + 1)
                link(dve.tensor_reduce(sm[:, n, 0, :], sc[:, n % 2, :, :], AX.X, ALU.max))
                link(dve.tensor_tensor(sm[:, n, 0, :], sm[:, n, 0, :], sinkb[:, 4 * g:4 * g + 4], ALU.max))
                link(dve.tensor_tensor(sm[:, n, 1, :], sinkb[:, 4 * g:4 * g + 4], sm[:, n, 0, :], ALU.subtract))
                dve.tensor_scalar(sm[:, n, 0, :], sm[:, n, 0, :], -1.0, None, ALU.mult).then_inc(sem("max_done"), 1)

            maxima(0)
            for n, (tt, g) in enumerate(steps):
                if n + 1 < len(steps):
                    maxima(n + 1)
                dve.wait_ge(sem("probs_done"), n + 1)
                link(dve.tensor_tensor(sm[:, n, 1, :], sm[:, n, 1, :], stat[:, 4 + 4 * (n % 2):8 + 4 * (n % 2)], ALU.add))
                link(dve.reciprocal(sm[:, n, 1, :], sm[:, n, 1, :]))
                dve.wait_ge(sem("pv_done"), n + 1)
                o = yn[:, tt, g * S:(g + 1) * S].rearrange("p (i r d) -> p r i d", i=2, r=2)
                dve.tensor_tensor(o, PS[:, 6, 0:S].rearrange("p (r i d) -> p r i d", r=2, i=2),
                                  sm[:, n, 1, :].rearrange("p (r i) -> p r i", r=2).unsqueeze(3)
                                  .to_broadcast([P, 2, 2, HD]), ALU.mult).then_inc(sem("attn_out"), 1)
            row_norms(2)

            wide = lambda t: t.rearrange("p c s -> p (c s)")

            def one_minus(dr):
                h, a_ = hh[:, dr, :, :], aa[:, dr, :, :]
                dve.wait_ge(sem("decays_done"), dr + 1)
                link(dve.tensor_tensor(h, a_, a_, ALU.mult))
                dve.scalar_tensor_tensor(wide(h), wide(h), 1.0, wide(rr[:, dr, :, :]), ALU.add, ALU.mult)\
                    .then_inc(sem("one_minus_done"), 1)
                x = ii[:, dr, :, :]
                link(dve.tensor_tensor(x, x, convT[:, :, :], ALU.mult))
                edge = 0 if dr == 0 else S - 1
                link(dve.memset(aa[:, dr, :, edge:edge + 1], 0.0))

            one_minus(0)
            one_minus(1)
            for dr in range(2):
                h, x = hh[:, dr, :, :], ii[:, dr, :, :]
                dve.wait_ge(sem("root_done"), dr + 1)
                link(dve.tensor_tensor(x, x, h, ALU.mult))
                a0, u0, o0 = wide(aa[:, dr, :, :]), wide(x), wide(h)
                if dr:
                    a0, u0, o0 = a0[:, ::-1], u0[:, ::-1], o0[:, ::-1]
                link(dve.tensor_tensor_scan(o0, a0, u0, 0.0, ALU.mult, ALU.add))
            link(dve.tensor_tensor(hh[:, 0, :, :], hh[:, 0, :, :], hh[:, 1, :, :], ALU.add))
            dve.tensor_tensor(yT[:, LC:2 * LC, :], hh[:, 0, :, :], gateT[:, :, :], ALU.mult).then_inc(sem("y_mixed"), 1)
            dve.wait_ge(sem("lru_root"), 1)
            link(dve.reciprocal(rstdb[:, 1, :], rstdb[:, 0, :]))
            for c in range(LC):
                last = dve.scalar_tensor_tensor(yT[:, LC + c, :], yT[:, LC + c, :], pc[:, PC["g_lru"] + c:PC["g_lru"] + c + 1],
                                                rstdb[:, 1, :], ALU.mult, ALU.mult)
            last.then_inc(sem("y_lru_done"), 1)
            dve.wait_ge(sem("y_lru_done"), 1)

            def add_product(signal):
                for tt in range(TT):
                    last = dve.tensor_tensor(X[:, tt, :], X[:, tt, :], banks(4 * tt, 4), ALU.add)
                    if tt == 0:
                        last.then_inc(sem("half_added"), 1)
                last.then_inc(signal, 1)

            rows_bodies("w_out", lambda k: one(yT, k))
            add_product(sem("x1_done"))
            dve.wait_ge(sem("x1_done"), 1)
            row_norms(3)
            turned(1, lambda c: pc[:, PC["g_ffn"] + c:PC["g_ffn"] + c + 1])
            bodies("w_pq")

            def best(values, left, o_values, o_indices, n):
                for i in range(n):
                    link.post(dve.max(o_values(i)[:, 0:8], values(i)))
                link.wait()
                for i in range(n):
                    link.post(dve.max_index(o_indices(i)[:, 0:8], o_values(i)[:, 0:8], values(i)))
                    link.post(dve.match_replace(left(i), o_values(i)[:, 0:8], values(i), -3.0e38))
                link.wait()
                for i in range(n):
                    link.post(dve.max(o_values(i)[:, 8:16], left(i)))
                link.wait()
                for i in range(n):
                    link.post(dve.max_index(o_indices(i)[:, 8:16], o_values(i)[:, 8:16], left(i)))
                link.wait()

            dve.wait_ge(sem("scores_out"), 2)
            workk = pqT[:, :, :].rearrange("p c s -> p (c s)").rearrange("p (i n) -> p i n", n=NK)
            best(lambda i: score[:, i, :], lambda i: workk[:, i, :], lambda i: topv[:, i, :], lambda i: topi[:, i, :],
                 TT * 2 * PH)
            v = topv[:, :, :].rearrange("p (g h) k -> p g h k", h=2)
            G = TT * PH
            for tt in range(TT):
                g = slice(tt * PH, (tt + 1) * PH)
                link.post(dve.tensor_tensor(cand[:, g, :, :],
                                            v[:, g, 0, :].unsqueeze(3).to_broadcast([P, PH, TOPK, TOPK]),
                                            v[:, g, 1, :].unsqueeze(2).to_broadcast([P, PH, TOPK, TOPK]), ALU.add))
            link(dve.tensor_copy(topf[:, :, :], topi[:, :, :]))
            left = score[:, :, :].rearrange("p c s -> p (c s)").rearrange("p (i n) -> p i n", n=TOPK * TOPK)
            best(lambda i: cand[:, i, :, :].rearrange("p x y -> p (x y)"), lambda i: left[:, i, :],
                 lambda i: pick[:, i, :], lambda i: seli[:, i, :], G)
            link.post(dve.tensor_scalar(selh[:, 0, :, :], seli[:, :, :], 4, None, ALU.logical_shift_right))
            link(dve.tensor_scalar(selh[:, 1, :, :], seli[:, :, :], 15, None, ALU.bitwise_and))
            link(dve.tensor_copy(self_[:, :, :, :], selh[:, :, :, :]))
            link(dve.tensor_tensor(selh[:, 0, :, :].bitcast(F32), pick[:, :, :],
                                   pick[:, :, 0:1].to_broadcast([P, G, TOPK]), ALU.subtract))
            dve.tensor_copy(pick[:, :, :], selh[:, 0, :, :].bitcast(F32)).then_inc(sem("pick_shifted"), 1)
            f = topf[:, :, :].rearrange("p (g h) k -> p g h k", h=2)
            match = pqT[:, :, :].rearrange("p c s -> p (c s)").rearrange("p (i x y) -> p i x y", x=TOPK, y=TOPK)
            sixteen = cc[:, CC["iota16"]:CC["iota16"] + TOPK]
            for h in range(2):
                link(dve.tensor_tensor(match, sixteen.unsqueeze(1).unsqueeze(1).to_broadcast([P, G, TOPK, TOPK]),
                                       self_[:, h, :, :].unsqueeze(3).to_broadcast([P, G, TOPK, TOPK]), ALU.is_equal))
                link(dve.tensor_tensor(match, match, f[:, :, h, :].unsqueeze(2).to_broadcast([P, G, TOPK, TOPK]), ALU.mult))
                link(dve.tensor_reduce(slots[:, h, :, :], match, AX.X, ALU.add))
            dve.wait_ge(sem("pick_exp"), 1)
            link(dve.tensor_reduce(rsum[:, :], pick[:, :, :], AX.X, ALU.add))
            link(dve.reciprocal(rsum[:, :], rsum[:, :]))
            dve.tensor_tensor(slots[:, 2, :, :], pick[:, :, :], rsum[:, :].unsqueeze(2).to_broadcast([P, G, TOPK]),
                              ALU.mult).then_inc(sem("slots_done"), 1)
            dve.wait_ge(sem("silu_c_done"), 1)
            dve.wait_ge(sem("slot_gate_high"), 1)
            rest = xtmp[:, 0, :]
            link(dve.tensor_tensor(rest, PS[:, 4, 0:S], slot_gate[:, 0, :], ALU.subtract))
            link(dve.tensor_copy(slot_gate[:, 1, :], rest))
            dve.tensor_tensor(slot_gate[:, 2, :], rest, slot_gate[:, 1, :], ALU.subtract)\
                .then_inc(sem("route_over"), 1)
            dve.wait_ge(sem("route_over"), 2)
            dve.sem_inc(sem("ada_used"), 3)
            dve.sem_inc(sem("gates_applied"), 2)
            dve.sem_inc(sem("gated"), 2)

            def key_rows(n, n_before, base, width, r):
                dve.wait_ge(sem("gates_spread"), n + (n_before + 1))

                def match(o, first, w, row):
                    keys = iota_b[:, first:first + w].unsqueeze(1).to_broadcast([P, 8, w])
                    return dve.tensor_tensor(o, keys, slotsT[:, row, ds(8 * n, 8)].unsqueeze(2).to_broadcast([P, 8, w]),
                                             ALU.is_equal)

                match(hot2[width][:, r, :, 0:width], base, width, 1).then_inc(sem("keys_matched"), 1)
                match(hot1[:, r, :, :], 0, NK, 0).then_inc(sem("hot_done"), 1)
                dve.wait_ge(sem("keys_matched"), n + (n_before + 1))
                dve.tensor_tensor(hot2_gate[width][:, r, 0, :, :], hot2[width][:, r, :, :],
                                  slot_gate[:, 0, ds(8 * n, 8)].unsqueeze(2).to_broadcast([P, 8, width]), ALU.mult)\
                    .then_inc(sem("hot_done"), 1)

            def ada_product(seg, k, q, buffer, acc):
                dve.wait_ge(sem(f"ada_loaded{q}"), 16 * k + 16 * (16 * seg + 1))
                dve.wait_ge(sem("ada_used"), 3 * k + (48 * seg + q + 1))
                dve.scalar_tensor_tensor(acc[:, q, :], buffer[:, q, :], silu_c[:, ds(k, 1)], acc[:, q, :],
                                         ALU.mult, ALU.add).then_inc(sem("ada_used"), 1)

            def gates_onto_first(n, r):
                dve.wait_ge(sem("gates_out"), n + 3)
                x = hid0[:, :, ds(8 * n, 8)]
                dve.tensor_tensor(x, x, PS[:, 4 + r, :].rearrange("p (t b) -> p b t", t=8)[:, 0:EB, :], ALU.mult)\
                    .then_inc(sem("gates_applied"), 1)

            for r in range(2):
                key_rows(r, 0, 0, 2 * EB, r)
            with dve.Fori(0, 15) as j:
                for r in range(2):
                    key_rows(2 * j + (2 + r), 0, 0, 2 * EB, r)
                    gates_onto_first(2 * j + r, r)
            for r in range(2):
                gates_onto_first(30 + r, r)
            dve.wait_ge(sem("gates_applied"), 34)
            dve.wait_ge(lo_done, 4 * (FIRST_BODY["down0"] + 1))

            for quarter in range(QUARTERS):
                up, down = f"up{quarter}", f"down{quarter}"
                if quarter:
                    link(dve.memset(ada_acc[:, 1, :, :], 0.0))
                    with dve.Fori(0, 16) as j:
                        for u in range(4):
                            b = u // 2
                            if u % 2 == 0 and quarter < QUARTERS - 1:
                                key_rows(2 * j + b, 32 * quarter, (quarter + 1) * EB, EB, b)
                            low(j + (FIRST_BODY[up] + 1), u)
                            if u % 2 == 1:
                                i = 2 * j + b
                                dve.wait_ge(act_free, i + (2 + ACT_BLOCKS[up] + 1))
                                x = one(hid[quarter % 2], i)
                                dve.tensor_tensor(x, x, geluT[:, b, :], ALU.mult).then_inc(sem("gated"), 1)
                            if u:
                                ada_product(2 * quarter - 1, j, u - 1, ada, ada_acc[:, 1, :, :])
                    dve.wait_ge(sem("gated"), EB * quarter + 2)
                link(dve.memset(ada_acc[:, 0, :, :], 0.0))
                source = lambda k: one(hid[quarter % 2], k)
                for s in range(2):
                    stage(source, s, s, down)
                with dve.Fori(0, 15) as j:
                    for u in range(4):
                        low(j + (FIRST_BODY[down] + 1), u)
                        if u % 2 == 1:
                            stage(source, 2 * j + (2 + u // 2), u // 2, down)
                        if u:
                            ada_product(2 * quarter, j, u - 1, ada, ada_acc[:, 0, :, :])
                for u in range(4):
                    low(FIRST_BODY[down] + 16, u)
                    if u:
                        ada_product(2 * quarter, 15, u - 1, ada, ada_acc[:, 0, :, :])
                dve.wait_ge(tile_used, 4 * (FIRST_BODY[down] + 16))
                add_product(sem("x2_done"))
                dve.wait_ge(sem("x2_done"), quarter + 1)
                dve.wait_ge(sem("ada_summed"), quarter + 1)
                for layer in range(2 if quarter else 1):
                    m = 48 * layer + 12 * (quarter - layer)
                    last = dve.tensor_tensor(mod[:, m:m + 12], PS[:, 3, 12 * layer:12 * layer + 12],
                                             pc[:, PC["ada_b"] + m:PC["ada_b"] + m + 12], ALU.add)
                    if layer == 0 and quarter:
                        link.post(last)
                last.then_inc(sem("mod_done"), 1)
            dve.wait_ge(sem("mod_done"), 4)
            dve.tensor_scalar(mod[:, 16:48], mod[:, 16:48], 1.0, None, ALU.add).then_inc(sem("mod_done"), 1)
            dve.wait_ge(sem("rms_root"), 4)
            link(dve.reciprocal(stat[:, 12:14], stat[:, 2:4]))
            dve.wait_ge(sem("row_loaded"), 16)
            for tt in range(TT):
                last = dve.scalar_tensor_tensor(X[:, tt, :], X[:, tt, :], stat[:, 12 + tt:13 + tt], row[:, :],
                                                ALU.mult, ALU.mult)
            last.then_inc(sem("x3_done"), 1)
            dve.wait_ge(sem("mod_done"), 5)
            turned(2, lambda c: mod[:, 16 + c:17 + c], lambda c: mod[:, c:c + 1])

            dve.wait_ge(sem("dt_product"), 1)
            hp = slice(0, SHEADS)
            link(dve.tensor_scalar(dtt[:, 1, :], PS[hp, 2, 0:S], pc[hp, PC["dt_bias"]:PC["dt_bias"] + 1], None, ALU.add))
            dve.scalar_tensor_tensor(dtt[:, 0, :], dtt[:, 1, :], -1.0, dtt[:, 1, :], ALU.mult, ALU.min).then_inc(sem("dt_abs"), 1)
            dve.wait_ge(sem("dt_exp"), 2)
            softplus(dts[:, 0, :], dtt[:, 1, :], dtt[:, 0, :], dtt[:, 2, :], dtt[:, 3, :], dtt[:, 4, :])
            link(dve.tensor_scalar(stat[hp, 13:14], stat[hp, 12:13], -1.0, None, ALU.mult))
            link(dve.tensor_scalar(dtt[:, 2, :], dts[:, 0, :], stat[hp, 13:14], None, ALU.mult))
            link(dve.memset(dtt[:, 3, :], 1.0))
            link(dve.tensor_tensor_scan(dts[:, 2, :], dtt[:, 3, :], dtt[:, 2, :], 0.0, ALU.mult, ALU.add))
            dve.tensor_copy(dts[:, 1, :], dts[:, 2, :]).then_inc(sem("decay_done"), 1)

            with dve.Fori(0, NB["xbc"]) as j:
                link.loop(j, 8)
                for b in range(2):
                    i = 2 * j + b
                    dve.wait_ge(tile_used, 4 * j + (4 * FIRST_BODY["xbc"] + 2 * b + 2))
                    dve.wait_ge(sem("conv_read"), i + 1)
                    convolve(cbuf[:, b, :], PS[:, b, 0:S], lambda t: pc[:, ds(4 * i + (PC["a_conv_w"] + t), 1)], 3)
                    dve.sem_inc(dve_free, 1)
                    dve.sem_inc(sem("conv_done"), 1)
            link.end(NB["xbc"])

            dve.wait_ge(sem("decays_high"), 1)
            high_part = decay_part[:, 0, :].bitcast(F32)
            dve.tensor_tensor(decay_part[:, 1, 0:S], dts[:, 2, :], high_part[:, 0:S], ALU.subtract)\
                .then_inc(sem("decays_low"), 1)
            dve.tensor_tensor(decay_part[:, 1, S:S + P], dts[:, 2, P:S], high_part[:, S:S + P], ALU.subtract)\
                .then_inc(sem("decays_low"), 1)
            dve.wait_ge(sem("ssd_ready"), 1)
            dve.sem_inc(sem("xd_done"), 1)
            dve.sem_inc(sem("mixed"), 2)
            dve.sem_inc(sem("y_added"), 2)
            dve.sem_inc(sem("y_gated"), 2)
            dve.sem_inc(sem("z_taken"), 2)
            dve.wait_ge(lo_done, 4 * (FIRST_BODY["z"] + 1))
            link(dve.memset(ada_acc_z[:, :, :], 0.0))
            with dve.Fori(0, SG) as g:
                dve.wait_ge(sem("xs_turned"), g + 2)
                dve.wait_ge(sem("y_product"), 8 * g + 2)
                for tt in range(TT):
                    dve.tensor_tensor(xd[:, tt, :].rearrange("p (h d) -> p h d", d=64),
                                      PS[:, tt, :].rearrange("p (h d) -> p h d", d=64),
                                      dtn[:, tt, ds(8 * g, 8)].unsqueeze(2).to_broadcast([P, 8, 64]), ALU.mult)\
                        .then_inc(sem("xd_done"), 1)
                dve.wait_ge(sem("cb_done"), g + 2)

                def add(k):
                    c = 4 * g + k // 2
                    dve.wait_ge(sem("y_product"), 8 * g + (k + 4))
                    dve.scalar_tensor_tensor(one(xbc, c), one(xbc, c), pc[:, ds(c + PC["skip"], 1)],
                                             PS[:, 5 + (k // 2) % 2, 0:S], ALU.mult, ALU.add)\
                        .then_inc(sem("y_added"), 1)
                    dve.wait_ge(act_free, c + (2 + ACT_BLOCKS["z"] + 1))
                    z = zt[:, (k // 2) % 2, :]
                    dve.scalar_tensor_tensor(z, z, 1.0, PS[:, z_bank[(k // 2) % 2], 0:S], ALU.add, ALU.mult)\
                        .then_inc(sem("z_taken"), 1)
                    dve.wait_ge(sem("y_added"), c + 3)
                    dve.wait_ge(sem("z_taken"), c + 3)
                    dve.scalar_tensor_tensor(one(xbc, c), one(xbc, c), 0.5, z, ALU.mult, ALU.mult)\
                        .then_inc(sem("y_gated"), 1)

                for k in range(8):
                    dve.wait_ge(sem("decays_read"), 8 * g + (k + 3))
                    dve.wait_ge(sem("y_product"), 8 * g + (k + 1))
                    dve.tensor_tensor(mm_[:, k % 2, :], ex[:, k % 2, :], cbm[:, :], ALU.mult).then_inc(sem("mixed"), 1)
                    low(2 * g + (FIRST_BODY["z"] + k // 4 + 1), k % 4)
                    if k % 4:
                        ada_product(7, 2 * g + k // 4, k % 4 - 1, ada_z, ada_acc_z)
                    if k in (2, 4, 6):
                        add(k - 2)
                add(6)
            dve.wait_ge(sem("y_gated"), XC + 2)
            dve.wait_ge(sem("ada_summed"), QUARTERS + 1)
            b = PC["ada_b"] + 84
            dve.tensor_tensor(mod[:, 84:96], PS[:, 3, 0:12], pc[:, b:b + 12], ALU.add).then_inc(sem("mod_done"), 1)
            dve.wait_ge(sem("mod_done"), 6)
            dve.tensor_scalar(mod[:, 64:96], mod[:, 64:96], 1.0, None, ALU.add).then_inc(sem("mod_done"), 1)
            dve.sem_inc(sem("ssd_normed"), 1)
            dve.wait_ge(sem("gates_high"), 1)
            dve.wait_ge(sem("mod_done"), 7)
            for n in range(2):
                last = dve.tensor_tensor(gate_part[:, n, 1, :], mod[:, 48 * n + 32:48 * n + 48],
                                         gate_part[:, n, 0, :].bitcast(F32), ALU.subtract)
                if n == 0:
                    link.post(last)
            last.then_inc(sem("gates_split"), 1)
            dve.wait_ge(sem("group_root"), 1)

            def norm_group(g):
                root_g = rg[:, ds(S * g, S)]
                dve.reciprocal(root_g, root_g).then_inc(sem("root_inverted"), 1)
                dve.wait_ge(sem("root_inverted"), g + 1)
                for c in range(4):
                    i = 4 * g + c
                    last = dve.scalar_tensor_tensor(one(xbc, i), one(xbc, i), pc[:, ds(i + PC["norm_g"], 1)],
                                                    root_g, ALU.mult, ALU.mult)
                last.then_inc(sem("ssd_normed"), 1)

            norm_group(0)
            dve.wait_ge(sem("ssd_normed"), 2)
            f = FIRST_BODY["a_out"]
            source = lambda k: one(xbc, k)
            for s in range(2):
                stage(source, s, s, "a_out")

            def normed_body(j, group=None):
                for u in range(4):
                    low(j + (f + 1), u)
                    if u % 2 == 1:
                        stage(source, 2 * j + (2 + u // 2), u // 2, "a_out")
                    if group is not None and u == 1:
                        norm_group(group)

            with dve.Fori(0, SG - 1) as g:
                normed_body(2 * g, g + 1)
                dve.wait_ge(sem("ssd_normed"), g + 3)
                normed_body(2 * g + 1)
            normed_body(2 * SG - 2)
            for u in range(4):
                low(f + 2 * SG, u)
            dve.wait_ge(tile_used, 4 * (f + 2 * SG))

            def layer_norm(n, signal):
                dve.tensor_copy(Y[:, 0, :], banks(0, 4)).then_inc(sem("y_copied"), 1)
                dve.wait_ge(sem("y_copied"), n + 1)
                dve.wait_ge(sem("y_half_copied"), n + 1)
                dve.wait_ge(sem("gate_spread"), n + 1)
                for tt in range(TT):
                    link.post(dve.tensor_tensor(Y[:, tt, :], Y[:, tt, :], banks(0, 4), ALU.mult))
                for tt in range(TT):
                    link.wait(1 - tt)
                    dve.scalar_tensor_tensor(X[:, tt, :], X[:, tt, :], ALPHA, Y[:, tt, :], ALU.mult, ALU.add)\
                        .then_inc(sem("ln_in"), 1)
                dve.wait_ge(sem("ln_rows_loaded"), 32 * (n + 1))
                for tt in range(TT):
                    dve.wait_ge(sem("ln_sum"), TT * n + tt + 1)
                    dve.tensor_scalar(stat[:, 2 + tt:3 + tt], stat[:, tt:tt + 1], -1.0 / D, None, ALU.mult)\
                        .then_inc(sem("ln_mean"), 1)
                    dve.wait_ge(sem("ln_mean"), TT * n + tt + 1)
                    dve.wait_ge(sem("ln_in"), TT * n + tt + 1)
                    link.post(dve.scalar_tensor_tensor(Y[:, tt, :], X[:, tt, :], stat[:, 2 + tt:3 + tt], rows[:, 0, :],
                                                       ALU.add, ALU.mult))
                dve.wait_ge(sem("ln_root"), n + 1)
                link(dve.reciprocal(stat[:, 8:10], stat[:, 6:8]))
                for tt in range(TT):
                    last = dve.scalar_tensor_tensor(X[:, tt, :], Y[:, tt, :], stat[:, 8 + tt:9 + tt], rows[:, 1, :],
                                                    ALU.mult, ALU.add)
                    if tt == 0:
                        last.then_inc(sem("half_normed"), 1)
                last.then_inc(signal, 1)

            layer_norm(0, sem("x4_done"))
            turned(3, lambda c: 1.0)
            bodies("k2")
            bodies("v2")
            turned(4, lambda c: mod[:, 64 + c:65 + c], lambda c: mod[:, 48 + c:49 + c])
            bodies("q2")
            bodies("z2")

            dve.wait_ge(sem("distances_loaded"), 16)
            dve.wait_ge(sem("z2_out"), 1)
            dve.sem_inc(sem("dist_added"), 1)
            dve.sem_inc(sem("head_out"), 1)

            def head_maxima(h, r):
                dve.wait_ge(sem("head_scored"), h + 2)
                dve.wait_ge(sem("head_turned"), h + 1)
                for g in range(DG):
                    slope = cd[:, ds(3 * h + (CD["slopes"] + g), 1)]
                    link.post(dve.scalar_tensor_tensor(sc2[:, r, g * P:(g + 1) * P],
                                                       cd[:, CD["d0"] + g * P:CD["d0"] + (g + 1) * P],
                                                       slope, PS[:, 0, g * P:(g + 1) * P], ALU.mult, ALU.add))
                for g in range(DG):
                    slope = cd[:, ds(3 * h + (CD["slopes"] + g), 1)]
                    o = 384 + g * S
                    last = dve.scalar_tensor_tensor(sc2[:, r, o:o + S], cd[:, CD["d1"] + g * S:CD["d1"] + (g + 1) * S],
                                                    slope, PS[:, 1 + g // 2, (g % 2) * S:(g % 2 + 1) * S],
                                                    ALU.mult, ALU.add)
                    if g < DG - 1:
                        link.post(last)
                last.then_inc(sem("dist_added"), 1)
                dve.wait_ge(sem("dist_added"), h + 2)
                link.post(dve.tensor_reduce(sm2[:, r, 0:1], sc2[:, r, 0:384], AX.X, ALU.max))
                link(dve.tensor_reduce(sm2[:, r, 1:2], sc2[:, r, 384:1152], AX.X, ALU.max))
                dve.tensor_scalar(sm2[:, r, 2:4], sm2[:, r, 0:2], -1.0, None, ALU.mult).then_inc(sem("head_max"), 1)

            def head_outputs(h, r):
                dve.wait_ge(sem("head_exp"), h + 1)
                link(dve.reciprocal(sm2[:, r, 6:8], sm2[:, r, 4:6]))
                dve.wait_ge(sem("head_product"), h + 1)
                for tt in range(TT):
                    z = zn[:, tt, ds(h * P, P)]
                    last = dve.scalar_tensor_tensor(z, PS[:, 6 + tt, 0:P], sm2[:, r, 6 + tt:7 + tt], z, ALU.mult, ALU.mult)
                    if tt == 0:
                        link.post(last)
                last.then_inc(sem("head_out"), 1)

            head_maxima(0, 0)
            with dve.Fori(0, DH // 2 - 1) as j:
                link.loop(j, 18)
                for r in range(2):
                    head_maxima(2 * j + (r + 1), 1 - r)
                    head_outputs(2 * j + r, r)
            link.end(DH // 2 - 1)
            head_maxima(DH - 1, 1)
            for r in range(2):
                head_outputs(DH - 2 + r, r)
            dve.wait_ge(sem("oT_done"), 1)
            rows_bodies("b_out", lambda k: one(oT, k))
            layer_norm(1, sem("out_ready"))


def lay_out(i):
    f = np.float32
    c = np.ascontiguousarray

    def columns(v):
        return v.reshape(-1, P).T

    def blocks(w):
        n = w.shape[1] // P
        return c(w.reshape(2, 8, P, n, P).transpose(3, 0, 2, 1, 4)).reshape(2 * n, P, TILE)

    w_in = i["w_in"][0]
    q_end, kv_end = QC, QC + KVC
    a_in = i["a_in_w_2"][0]
    o = {}
    o["x"] = c(i["x"].reshape(TT, P, D).transpose(1, 0, 2))
    o["q"] = c(w_in[:, :q_end]).reshape(KC, P, TILE)
    o["kv"] = c(w_in[:, q_end:kv_end].reshape(8, 2, P, 512).transpose(0, 2, 1, 3)).reshape(8, P, TILE)
    o["gate"] = blocks(w_in[:, kv_end:kv_end + LRU])
    o["rec"] = blocks(w_in[:, kv_end + LRU:])
    o["w_out"] = c(i["w_out"][0]).reshape(KC, P, D)
    o["w_pq"] = blocks(i["w_pq"][0])
    u = i["u_emb"][0].reshape(NK, NK, 2, 8, P)
    o["u_emb"] = c(u.transpose(1, 2, 4, 3, 0)).reshape(2 * NK, P, TILE)
    v = i["v_emb"][0].reshape(NK, NK, 2, TILE)
    o["v_emb"] = c(v.transpose(1, 2, 0, 3)).reshape(2 * NK, P, TILE)
    o["xbc"] = blocks(a_in[:, DI:DI + BC * P])
    o["z"] = blocks(a_in[:, :DI])
    o["w_dt"] = c(a_in[:, DI + BC * P:].reshape(KC, P, SHEADS).transpose(1, 0, 2))
    o["a_out"] = c(i["a_out_w_2"][0]).reshape(XC, P, D)
    kv = i["kv_w_2"]
    W = DG * DH * P
    o["k2"] = blocks(kv[:, :W])
    o["v2"] = c(kv[:, W:].reshape(KC, P, DG, TILE).transpose(2, 0, 1, 3)).reshape(DG * KC, P, TILE)
    b_in = i["b_in_w_2"][0]
    o["q2"] = blocks(b_in[:, :W])
    o["z2"] = c(b_in[:, W:]).reshape(KC, P, TILE)
    o["b_out"] = c(i["b_out_w_2"][0]).reshape(DH, P, D)
    ada = i["ada_w_2"].reshape(2, KC, P, 4, 3, ADA)
    o["ada_w"] = c(ada.transpose(3, 0, 1, 4, 2, 5)).reshape(-1, P, ADA)
    o["gate_w"] = c(np.stack([i[n][0].reshape(LC, 2, 64, 64).transpose(1, 2, 0, 3)
                              for n in ("fwd_wa", "fwd_wx", "bwd_wa", "bwd_wx")]))
    sk = np.stack([i["sub_k1"][0], i["sub_k2"][0]], 1)
    o["skT"] = c(sk.reshape(2 * PH, NK, P).transpose(2, 0, 1))
    o["sink"] = c(i["sink"][0].reshape(NKV, 2, 2).transpose(0, 2, 1)).reshape(NQ)
    o["rows"] = c(np.stack([i["g_final"], i["ln_g_2"][0], i["ln_b_2"][0], i["ln_g_2"][1], i["ln_b_2"][1]]))

    pc = np.zeros((P, PC.n), f)

    def put(name, v):
        pc[:v.shape[0], PC[name]:PC[name] + v.shape[1]] = v

    put("g_mix", columns(i["g_mix"][0]))
    put("g_ffn", columns(i["g_ffn"][0]))
    put("g_attn", columns(i["g_attn_out"][0]))
    put("g_lru", columns(i["g_lru_out"][0]))
    put("conv_w", i["conv_w"][0].reshape(4, LC, P).transpose(2, 1, 0).reshape(P, -1))
    put("conv_b", columns(i["conv_b"][0]))
    put("gate_b", np.concatenate([columns(i[n][0]) for n in ("fwd_ba", "fwd_bx", "bwd_ba", "bwd_bx")], 1))
    put("lam", np.concatenate([columns(i[n][0]) for n in ("fwd_lam", "bwd_lam")], 1))
    put("ada_b", columns(i["ada_b_2"].reshape(-1)))
    put("cond", columns(i["c_2"][0]))
    put("a_conv_w", i["a_conv_w_2"][0].reshape(4, BC, P).transpose(2, 1, 0).reshape(P, -1))
    put("a_conv_b", columns(i["a_conv_b_2"][0]))
    put("norm_g", columns(i["a_norm_g_2"][0]))
    put("skip", columns(np.repeat(i["a_D_2"][0], 64)))
    put("dt_bias", i["a_dt_bias_2"][0][:, None])
    put("a_log", i["a_A_log_2"][0][:, None])
    for name, value in (("eps", EPS), ("ln_eps", LN_EPS), ("tiny", 1e-30)):
        pc[:, PC[name]] = value
    o["pc"] = pc

    cc = np.zeros((P, CC.n), f)
    cc[:, CC["ident"]:CC["ident"] + P] = np.eye(P)
    cc[:, CC["ones"]:CC["ones"] + P] = 1
    cc[:, CC["iota"]:CC["iota"] + P] = np.arange(P)
    cc[:, CC["iota16"]:CC["iota16"] + TOPK] = np.arange(TOPK)
    o["cc"] = cc
    half = HD // 2
    inv = (f(10000.0) ** (-np.arange(half, dtype=f) / f(half))).astype(f)
    ang = (np.arange(S, dtype=f)[:, None] * inv[None]).astype(f)
    pos = np.arange(S)
    cw = np.zeros((P, CW.n), f)
    window = np.where(np.abs(pos[None] - pos[:, None]) <= 128, 0, NEG).astype(f)
    for name, t in (("cos", np.cos(ang)), ("sin", np.sin(ang)), ("window", window)):
        w = t.shape[1] * TT
        cw[:, CW[name]:CW[name] + w] = t.reshape(TT, P, -1).transpose(1, 0, 2).reshape(P, -1)
    o["cw"] = cw
    o["causal"] = np.where(pos[None, :P] >= pos[:P, None], 0, NEG).astype(f)
    far = pos[:, None] - pos[None]
    cd = np.zeros((P, CD.n), f)
    for g, (window, step) in enumerate(((128, 1), (512, 4), (2048, 16))):
        d = np.where((far >= 0) & (far <= window) & (far % step == 0), far, -NEG).astype(f)
        cd[:, CD["d0"] + g * P:CD["d0"] + (g + 1) * P] = d[:P, :P]
        cd[:, CD["d1"] + g * S:CD["d1"] + (g + 1) * S] = d[P:, :]
    n = DG * DH
    slopes = (2.0 ** (-8.0 * np.arange(1, n + 1) / n)).reshape(DG, DH).T.reshape(-1)
    cd[:, CD["slopes"]:CD["slopes"] + n] = -slopes.astype(f)
    o["cd"] = cd
    return o


def kernel(**inputs):
    import concourse.bacc as bacc
    from concourse.bass_utils import run_bass_kernel_spmd

    arrays = lay_out({k: np.asarray(v) for k, v in inputs.items()})
    nc = bacc.Bacc("TRN2", target_bir_lowering=False, num_devices=1)
    aps = {k: nc.dram_tensor(f"in_{k}", v.shape, F32, kind="ExternalInput").ap() for k, v in arrays.items()}
    out = nc.dram_tensor("out", (P, TT, D), F32, kind="ExternalOutput").ap()
    build(nc, aps, out)
    got = run_bass_kernel_spmd(nc, [{f"in_{k}": v for k, v in arrays.items()}], core_ids=[0])
    y = got.results[0]["out"]
    return np.ascontiguousarray(y.transpose(1, 0, 2)).reshape(1, S, D)
```
